# Optimizing a Trainium2 kernel written in Bass

```python
import math
import jax, jax.numpy as jnp
from jax import lax
import numpy as np

D_MODEL = 2048
BATCH = 1
SEQ = 256
DEPTH = 1

BRANCH_W = D_MODEL // 2
N_BRANCHES = 3
CONV_A_WIDTH = 31
ATT_PATTERNS = ((128, 1), (512, 4), (2048, 16))
ATT_GROUPS = len(ATT_PATTERNS)
ATT_HEADS = 8
ATT_HEAD_DIM = BRANCH_W // ATT_HEADS
ATT_W = ATT_GROUPS * ATT_HEADS * ATT_HEAD_DIM
ATT_BLOCK = 128
CONV_C_WIDTH = 3
OFF_Q = 2 * BRANCH_W
OFF_K = OFF_Q + ATT_W
OFF_V = OFF_K + ATT_W
OFF_C = OFF_V + ATT_W
OFF_G = OFF_C + 3 * BRANCH_W
N_IN = OFF_G + N_BRANCHES * D_MODEL
MOE_EXPERTS = 64
MOE_TOPK = 8
MOE_GROUPS = 8
MOE_TOPK_GROUPS = 4
MOE_FFN = D_MODEL // 8
MOE_SHARED_FFN = MOE_FFN
MOE_ROUTED_SCALE = 2.5
MOE_BLOCK = 128
LN_EPS = 1e-5
NEG_INF = -1e30

kernel_name = "hybrid_gated_conformer_dilated_shortconv_moe"

def layer_norm(x, g, b):
    xf = x.astype(jnp.float32)
    mu = jnp.mean(xf, axis=-1, keepdims=True)
    xc = xf - mu
    var = jnp.mean(xc * xc, axis=-1, keepdims=True)
    return (xc * lax.rsqrt(var + LN_EPS) * g + b).astype(x.dtype)

def causal_depthwise_conv(x, w):
    taps = w.shape[0]
    return lax.conv_general_dilated(
        x, w[:, None, :].astype(x.dtype), window_strides=(1,), padding=[(taps - 1, 0)],
        dimension_numbers=("NWC", "WIO", "NWC"), feature_group_count=x.shape[-1])

def dilated_window_attention(q, k, v, dilation, span):
    B, S, H, dh = q.shape
    L = S // dilation
    nb = -(-L // ATT_BLOCK)
    Lp = nb * ATT_BLOCK

    def classes(t):
        t = t.reshape(B, L, dilation, H, dh).transpose(0, 2, 3, 1, 4)
        return jnp.pad(t, ((0, 0), (0, 0), (0, 0), (0, Lp - L), (0, 0)))

    def band(t):
        t = jnp.pad(t, ((0, 0), (0, 0), (0, 0), (ATT_BLOCK, 0), (0, 0)))
        t = t.reshape(B, dilation, H, nb + 1, ATT_BLOCK, dh)
        return jnp.concatenate([t[:, :, :, :-1], t[:, :, :, 1:]], axis=-2)

    qb = classes(q).reshape(B, dilation, H, nb, ATT_BLOCK, dh)
    kb = band(classes(k))
    vb = band(classes(v))
    qi = jnp.arange(ATT_BLOCK)[:, None]
    ki = jnp.arange(2 * ATT_BLOCK)[None, :]
    dist = ATT_BLOCK + qi - ki
    key_pos = (jnp.arange(nb)[:, None, None] - 1) * ATT_BLOCK + ki[None]
    valid = (dist >= 0) & (dist <= span) & (key_pos >= 0)
    s = jnp.einsum("brhnqd,brhnkd->brhnqk", qb, kb,
                   preferred_element_type=jnp.float32) * (dh ** -0.5)
    s = jnp.where(valid, s, NEG_INF)
    lse = jax.nn.logsumexp(s, axis=-1)
    p = jnp.exp(s - lse[..., None]).astype(v.dtype)
    o = jnp.einsum("brhnqk,brhnkd->brhnqd", p, vb)
    o = o.reshape(B, dilation, H, Lp, dh)[:, :, :, :L].transpose(0, 3, 1, 2, 4).reshape(B, S, H, dh)
    lse = lse.reshape(B, dilation, H, Lp)[..., :L].transpose(0, 3, 1, 2).reshape(B, S, H)
    return o, lse

def token_mixer(x, w_in, conv_a_w, conv_a_b, ln_a_g, ln_a_b, conv_c_w, w_branch, w_out):
    B, S, _ = x.shape
    u = x @ w_in
    a_in, q, k, v, c_in, g_in = jnp.split(u, [OFF_Q, OFF_K, OFF_V, OFF_C, OFF_G], axis=-1)

    a_val, a_gate = jnp.split(a_in, 2, axis=-1)
    a = a_val * jax.nn.sigmoid(a_gate)
    a = causal_depthwise_conv(a, conv_a_w) + conv_a_b
    a = jax.nn.silu(layer_norm(a, ln_a_g, ln_a_b))

    shp = (B, S, ATT_GROUPS, ATT_HEADS, ATT_HEAD_DIM)
    q, k, v = q.reshape(shp), k.reshape(shp), v.reshape(shp)
    outs, lses = [], []
    for g, (window, dilation) in enumerate(ATT_PATTERNS):
        o, lse = dilated_window_attention(q[:, :, g], k[:, :, g], v[:, :, g], dilation, window // dilation)
        outs.append(o)
        lses.append(lse)
    wgt = jax.nn.softmax(jnp.stack(lses, axis=0), axis=0).astype(x.dtype)
    att = jnp.einsum("gbsh,gbshd->bshd", wgt, jnp.stack(outs, axis=0)).reshape(B, S, BRANCH_W)

    cb, cc, ch = jnp.split(c_in, 3, axis=-1)
    c = cb * causal_depthwise_conv(cc * ch, conv_c_w)

    proj = jnp.einsum("nbsc,ncd->nbsd", jnp.stack([a, att, c], axis=0), w_branch)
    gates = jax.nn.sigmoid(g_in).reshape(B, S, N_BRANCHES, D_MODEL)
    merged = jnp.einsum("bsnd,nbsd->bsd", gates, proj)
    return merged @ w_out

def route(h, router_w, router_bias):
    T = h.shape[0]
    logits = jnp.dot(h, router_w, preferred_element_type=jnp.float32)
    scores = jax.nn.sigmoid(logits)
    choice = scores + router_bias.astype(jnp.float32)
    grp = choice.reshape(T, MOE_GROUPS, MOE_EXPERTS // MOE_GROUPS)
    grp_score = lax.top_k(grp, 2)[0].sum(-1)
    _, top_grp = lax.top_k(grp_score, MOE_TOPK_GROUPS)
    grp_mask = (top_grp[..., None] == jnp.arange(MOE_GROUPS)).any(axis=-2)
    expert_mask = jnp.repeat(grp_mask, MOE_EXPERTS // MOE_GROUPS, axis=-1)
    _, idx = lax.top_k(jnp.where(expert_mask, choice, NEG_INF), MOE_TOPK)
    w = jnp.take_along_axis(scores, idx, axis=-1)
    w = w / jnp.sum(w, axis=-1, keepdims=True) * MOE_ROUTED_SCALE
    return idx, w

def moe(h, router_w, router_bias, w_gate, w_up, w_down, ws_gate, ws_up, ws_down):
    T, D = h.shape
    idx, wts = route(h, router_w, router_bias)
    TK = T * MOE_TOPK
    flat_e = idx.reshape(-1).astype(jnp.int32)
    flat_t = jnp.broadcast_to(jnp.arange(T, dtype=jnp.int32)[:, None], (T, MOE_TOPK)).reshape(-1)
    flat_w = wts.reshape(-1)
    order = jnp.argsort(flat_e)
    e_s, t_s, w_s = flat_e[order], flat_t[order], flat_w[order]
    counts = jnp.bincount(flat_e, length=MOE_EXPERTS).astype(jnp.int32)
    padded = (counts + MOE_BLOCK - 1) // MOE_BLOCK * MOE_BLOCK
    start = jnp.cumsum(counts) - counts
    pend = jnp.cumsum(padded)
    pstart = pend - padded
    dest = pstart[e_s] + (jnp.arange(TK, dtype=jnp.int32) - start[e_s])
    n_pad = -(-TK // MOE_BLOCK) * MOE_BLOCK + MOE_EXPERTS * MOE_BLOCK
    nb = n_pad // MOE_BLOCK
    row_tok = jnp.full((n_pad,), T, jnp.int32).at[dest].set(t_s)
    row_w = jnp.zeros((n_pad,), h.dtype).at[dest].set(w_s.astype(h.dtype))
    blk_expert = jnp.clip(jnp.searchsorted(pend, jnp.arange(nb, dtype=jnp.int32) * MOE_BLOCK, side="right"),
                          0, MOE_EXPERTS - 1)
    hp = jnp.concatenate([h, jnp.zeros((1, D), h.dtype)], axis=0)

    def step(acc, blk):
        tok, w, e = blk
        xb = hp[tok]
        y = (jax.nn.silu(xb @ w_gate[e]) * (xb @ w_up[e])) @ w_down[e]
        return acc.at[tok].add(y * w[:, None]), None

    acc, _ = lax.scan(step, jnp.zeros((T + 1, D), h.dtype),
                      (row_tok.reshape(nb, MOE_BLOCK), row_w.reshape(nb, MOE_BLOCK), blk_expert))
    shared = (jax.nn.silu(h @ ws_gate) * (h @ ws_up)) @ ws_down
    return acc[:T] + shared

def setup_inputs(seed: int = 0) -> dict:
    key = jax.random.key(seed)
    ks = jax.random.split(key, 21)
    L, D, F = DEPTH, D_MODEL, MOE_FFN
    beta = (8.0 * DEPTH) ** -0.25

    def nrm(k, shape, scale):
        return jax.random.normal(k, shape, jnp.float32) * scale

    return {
        "x": nrm(ks[0], (BATCH, SEQ, D), 1.0),
        "w_in": nrm(ks[1], (L, D, N_IN), D ** -0.5),
        "conv_a_w": nrm(ks[2], (L, CONV_A_WIDTH, BRANCH_W), CONV_A_WIDTH ** -0.5),
        "conv_a_b": nrm(ks[3], (L, BRANCH_W), 0.01),
        "ln_a_g": 1.0 + nrm(ks[4], (L, BRANCH_W), 0.01),
        "ln_a_b": nrm(ks[5], (L, BRANCH_W), 0.01),
        "conv_c_w": nrm(ks[6], (L, CONV_C_WIDTH, BRANCH_W), CONV_C_WIDTH ** -0.5),
        "w_branch": nrm(ks[7], (L, N_BRANCHES, BRANCH_W, D), BRANCH_W ** -0.5),
        "w_out": nrm(ks[8], (L, D, D), D ** -0.5 * beta),
        "ln1_g": 1.0 + nrm(ks[9], (L, D), 0.01),
        "ln1_b": nrm(ks[10], (L, D), 0.01),
        "router_w": nrm(ks[11], (L, D, MOE_EXPERTS), D ** -0.5),
        "router_bias": nrm(ks[12], (L, MOE_EXPERTS), 0.01),
        "w_gate": nrm(ks[13], (L, MOE_EXPERTS, D, F), D ** -0.5),
        "w_up": nrm(ks[14], (L, MOE_EXPERTS, D, F), D ** -0.5),
        "w_down": nrm(ks[15], (L, MOE_EXPERTS, F, D), F ** -0.5 * beta),
        "ws_gate": nrm(ks[16], (L, D, MOE_SHARED_FFN), D ** -0.5),
        "ws_up": nrm(ks[17], (L, D, MOE_SHARED_FFN), D ** -0.5),
        "ws_down": nrm(ks[18], (L, MOE_SHARED_FFN, D), MOE_SHARED_FFN ** -0.5 * beta),
        "ln2_g": 1.0 + nrm(ks[19], (L, D), 0.01),
        "ln2_b": nrm(ks[20], (L, D), 0.01),
    }

def reference(x, w_in, conv_a_w, conv_a_b, ln_a_g, ln_a_b, conv_c_w, w_branch, w_out,
              ln1_g, ln1_b, router_w, router_bias, w_gate, w_up, w_down,
              ws_gate, ws_up, ws_down, ln2_g, ln2_b):
    alpha = (2.0 * DEPTH) ** 0.25
    B, S, D = x.shape
    for l in range(DEPTH):
        mix = token_mixer(x, w_in[l], conv_a_w[l], conv_a_b[l], ln_a_g[l], ln_a_b[l],
                          conv_c_w[l], w_branch[l], w_out[l])
        x = layer_norm(alpha * x + mix, ln1_g[l], ln1_b[l])
        ffn = moe(x.reshape(B * S, D), router_w[l], router_bias[l], w_gate[l], w_up[l], w_down[l],
                  ws_gate[l], ws_up[l], ws_down[l]).reshape(B, S, D)
        x = layer_norm(alpha * x + ffn, ln2_g[l], ln2_b[l])
    return x


_drawn_inputs = setup_inputs


def setup_inputs(seed=0):
    import zlib

    import numpy as np

    out = dict(_drawn_inputs(seed))
    spreads = {}
    factors = {'conv_a_b': 3.419, 'ln_a_g': 4.488, 'ln_a_b': 10.77, 'ln2_g': 33.893, 'ln2_b': 33.377}
    for name, (base, spread) in spreads.items():
        noise = np.random.default_rng([zlib.crc32(name.encode()), seed]).standard_normal(out[name].shape)
        drawn = base * np.exp(spread * noise) if base else spread * noise
        out[name] = __import__('jax').numpy.asarray(drawn.astype(out[name].dtype))
    for name, factor in factors.items():
        out[name] = (out[name] * factor).astype(out[name].dtype)
    return out
```

```python
from contextlib import ExitStack

import concourse.bass as bass
from concourse import mybir

P = 128
F32 = mybir.dt.float32
F32R = mybir.dt.float32r
BF16 = mybir.dt.bfloat16
I32 = mybir.dt.int32
U32 = mybir.dt.uint32
ACT = mybir.ActivationFunctionType
ALU = mybir.AluOpType
AX_X = mybir.AxisListType.X
KB = 1024

N_GROUPS_ATT = 3
DILATIONS = (1, 4, 16)
SPAN = 128
N_ROUTE_GROUPS = 8
TOPK_GROUPS = 4
TOPK = 8
ROUTED_SCALE = 2.5
LN_EPS = 1e-5
NEG = -1e30
FILL = -2e38
CHOSEN = -3e38
NO_SLOT = 1000.0
NO_ROW = 4096.0
SLOTS = 64


class Unit:

    def __init__(self, base, length, i, j):
        self.n = base + length * i + j
        self.ring = j % 4
        self.bank = j % 2
        self.half = j % 2
        self.raw = (j // 2) % 2
        self.raw_count = base // 4 + (length // 4) * i + j // 4 + 1
        self.bank_count = base // 2 + (length // 2) * i + j // 2
        self.first = isinstance(i, int) and base + length * i + j < 4
        self.first_bank = isinstance(i, int) and base + length * i + j < 2


def build(nc, x, w_in, conv_a_w, conv_a_b, ln_a_g, ln_a_b, conv_c_w, w_branch, w_out, ln1_g, ln1_b,
          router_w, router_bias, w_gate, w_up, w_down, ws_gate, ws_up, ws_down, ln2_g, ln2_b, out):
    DEPTH, D, N_IN = w_in.shape
    assert DEPTH == 1
    TOK = x.shape[1]
    TT = TOK // P
    KT = D // P
    C = conv_a_w.shape[2]
    CT = C // P
    TAPS_A = conv_a_w.shape[1]
    TAPS_C = conv_c_w.shape[1]
    HEADS = CT
    ATT_W = N_GROUPS_ATT * C
    OFF_Q = 2 * C
    OFF_C = OFF_Q + 3 * ATT_W
    OFF_G = OFF_C + 3 * C
    E = w_gate.shape[1]
    F = w_gate.shape[3]
    FT = F // P
    PAIRS = E // 2
    ALPHA = float((2.0 * DEPTH) ** 0.25)
    SCALE = float(P) ** -0.5
    MASKED = NEG / SCALE
    BLOCKS = TOK // SLOTS
    N_PAR = TAPS_A + 3 + TAPS_C
    HALF = HEADS // 2
    N_GATHER = 4
    N_PAR = TAPS_A + 3 + TAPS_C
    HALF = HEADS // 2
    N_GATHER = 4
    N_PAR = TAPS_A + 3 + TAPS_C
    HALF = HEADS // 2
    N_GATHER = 4
    N_PAR = TAPS_A + 3 + TAPS_C
    HALF = HEADS // 2
    N_GATHER = 4
    N_PAR = TAPS_A + 3 + TAPS_C
    HALF = HEADS // 2
    N_GATHER = 4
    assert TT == 2 and KT == 16 and CT == 8 and FT == 2

    ctx = ExitStack()
    with ctx:
        base0 = -(-nc.sbuf_base // 32) * 32

        def at(name, shape, dt, kb):
            return nc.alloc_sbuf_tensor_at(name, shape, dt, offset=base0 + int(kb * KB))

        def sem(name):
            return ctx.enter_context(nc.semaphore(name))






        raw = [at(f"raw{r}", [P, 4096], F32, 16 * r) for r in range(2)]
        w_hi = [at(f"w_hi{r}", [P, 2048], F32R, 32 + 8 * r) for r in range(4)]
        w_lo = [at(f"w_lo{r}", [P, 2048], F32R, 64 + 8 * r) for r in range(4)]
        x_hi = at("x_hi", [P, KT, TOK], F32R, 96)
        x_lo = at("x_lo", [P, KT, TOK], F32R, 112)
        x_rows = at("x_rows", [P, TT, D], F32, 128)
        par_rows = at("par_rows", [N_PAR, C], F32, 144)
        dist = at("dist", [P, 2 * P], I32, 148)
        dist_mod = at("dist_mod", [P, 2, 2 * P], I32, 149)
        q_k = at("q_k", [P, 2 * N_GROUPS_ATT, HALF, TOK], F32, 128)
        q_t, k_t = q_k[:, 0:N_GROUPS_ATT, :, :], q_k[:, N_GROUPS_ATT:, :, :]
        v_rows = at("v_rows", [P, N_GROUPS_ATT, HALF, TT, P], F32, 152)
        merged = at("merged", [P, KT, TOK], F32, 128)
        branch_hi = at("branch_hi", [P, CT, TOK], F32R, 144)
        branch_lo = at("branch_lo", [P, CT, TOK], F32R, 152)
        a_mean = at("a_mean", [P, TOK], F32, 160)
        a_rstd = at("a_rstd", [P, TOK], F32, 161)
        branch = at("branch", [P, 3, CT, TOK], F32, 164)
        att_p = [at(f"att_p{r}", [P, N_GROUPS_ATT * 2 * P], F32, 180 + 3 * r) for r in range(2)]
        a_pad = at("a_pad", [P, CT, TAPS_A - 1 + TOK], F32, 188)
        c_pad = at("c_pad", [P, CT, TAPS_C - 1 + TOK], F32, 188)
        gated = [at(f"gated{r}", [P, 2, TOK], F32, 188 + 2 * r) for r in range(2)]
        p_t = at("p_t", [P, 2 * N_GROUPS_ATT, P], F32, 197)
        mask = at("mask", [P, N_GROUPS_ATT, 2, P], F32, 200)
        a_sig = [at(f"a_sig{r}", [P, TOK], F32, 203 + r) for r in range(2)]
        a_sq = at("a_sq", [P, CT, TOK], F32, 197)
        gates = at("gates", [P, CT, TOK], F32, 197)
        par = at("par", [P, CT, N_PAR], F32, 205)
        ident = at("ident", [P, P], F32, 206.25)
        ones = at("ones", [P, P], F32, 206.75)
        tiny = at("tiny", [P, 64], F32, 207.25)
        flag = at("flag", [P, 1], I32, 207.5)
        idx_now = at("idx_now", [P, 1], U32, 207.53125)
        neg_max = [tiny[:, r:r + 1] for r in range(2)]
        row_max = [tiny[:, 2 + r:3 + r] for r in range(2)]
        row_sum = [tiny[:, 4 + r:5 + r] for r in range(2)]
        row_rcp = [tiny[:, 6 + r:7 + r] for r in range(2)]
        mean_var = tiny[:, 8:12].rearrange("p (a b) -> p a b", a=2)
        var_eps = tiny[:, 12:14]
        std = tiny[:, 14:16]
        rstd = tiny[:, 16:18]
        w_sum = tiny[:, 18:20]
        w_rcp = tiny[:, 20:22]
        most = tiny[:, 22:23]
        merged_hi = at("merged_hi", [P, KT, TOK], F32R, 96)
        merged_lo = at("merged_lo", [P, KT, TOK], F32R, 112)
        acc = at("acc", [P, TT, D], F32, 144)
        ln_g = at("ln_g", [P, D], F32, 128)
        ln_b = at("ln_b", [P, D], F32, 136)
        exp_w = [at(f"exp_w{r}", [P, 4096], F32, kb) for r, kb in enumerate((160, 176, 0, 16, 32, 48))]
        h_perm = at("h_perm", [P, TT, D], F32, 48)
        ws = [at(f"ws{r}", [P, 4096], F32, 64 + 16 * r) for r in range(3)]
        y_t = at("y_t", [P, KT, 2 * SLOTS], F32, 64)
        y_rows = at("y_rows", [P, D], F32, 72)
        ln2_gt = at("ln2_gt", [P, D], F32, 80)
        ln2_bt = at("ln2_bt", [P, D], F32, 88)
        match = at("match", [P, TOPK, E], F32, 104)
        h_t = at("h_t", [P, KT, TOK], F32, 112)
        hits = at("hits", [P, E, SLOTS], BF16, 128)
        xg_t = at("xg_t", [P, KT, 2 * SLOTS], F32, 128)
        hg = at("hg", [P, D], F32, 136)
        gather = [at(f"gather{r}", [P, D], F32, 8 * r) for r in range(N_GATHER)]
        choice = at("choice", [P, TT, E], F32, 192)
        scores = at("scores", [P, TT, E], F32, 192.5)
        chosen = at("chosen", [P, TT, E], F32, 193)
        slot_of = at("slot_of", [P, TT, E], F32, 193.5)
        weight = at("weight", [P, TT, E], F32, 194)
        row_of = at("row_of", [P, TT, E], F32, 194.5)
        iota_slot = at("iota_slot", [P, TOK], F32, 195)
        row_base = at("row_base", [P, E], F32, 196)
        bias_b = at("bias_b", [P, E], F32, 196.25)
        top_in_group = at("top_in_group", [P, TT, N_ROUTE_GROUPS, 8], F32, 196.5)
        groups = at("groups", [P, TT, 16], F32, 197)
        groups_left = at("groups_left", [P, TT, 16], F32, 197.125)
        best_groups = at("best_groups", [P, TT, 8], F32, 197.25)
        group_in = at("group_in", [P, TT, 8], F32, 197.3125)
        group_out = at("group_out", [P, TT, 8], F32, 197.375)
        best = at("best", [P, TT, 8], F32, 197.4375)
        masked = at("masked", [P, TT, E], F32, 197.5)
        left = at("left", [P, TT, E], F32, 198)
        expert_sig = [at(f"expert_sig{r}", [P, FT, SLOTS], F32, 198.5 + 0.5 * r) for r in range(2)]
        expert_h = [at(f"expert_h{r}", [P, FT, SLOTS], F32, 199.5 + 0.5 * r) for r in range(2)]
        sh_sig = at("sh_sig", [P, FT, TOK], F32, 200.5)
        sh_h = at("sh_h", [P, FT, TOK], F32, 202.5)
        tok_idx = at("tok_idx", [P, PAIRS], U32, 204.5)
        stats = at("stats", [P, TT, 4, 6], F32, 204.625)
        tok_val = at("tok_val", [P, TT, 2], BF16, 204.8125)
        before = at("before", [P, P], F32, 205)
        hit_sum = [at(f"hit_sum{r}", [P, PAIRS, 2], F32, 205.5 + 0.25 * r) for r in range(2)]
        my_row = at("my_row", [P, TT, TOPK], F32, 206)
        my_idx = at("my_idx", [P, TT, TOPK], U32, 206.0625)
        my_w = at("my_w", [P, TT, TOPK], F32, 206.125)
        rw = at("rw", [P, KT, E], F32, 100)

        ps_proj = [nc.alloc_psum_tensor(f"ps_proj{r}", [P, 512], F32) for r in range(2)]
        ps_s = [nc.alloc_psum_tensor(f"ps_s{r}", [P, 1024], F32) for r in range(2)]
        ps_t = nc.alloc_psum_tensor("ps_t", [P, 1024], F32)
        turn_ring = [ps_s[0][:, 0:512], ps_s[0][:, 512:1024]]
        down_out = [ps_s[1], ps_t]

        h_dram = nc.dram_tensor("h_perm_dram", (TOK, D), F32, kind="Internal").ap()
        y_dram = nc.dram_tensor("y_dram", (BLOCKS * E * SLOTS, D), F32, kind="Internal").ap()
        x2 = x[0]
        out2 = out[0]
        w_in_v = w_in[0].rearrange("(t p) c -> p t c", p=P)
        w_branch_v = w_branch[0].rearrange("n (t p) c -> p (n t) c", p=P)
        w_out_v = w_out[0].rearrange("(t p) c -> p t c", p=P)
        gate_v = w_gate[0].rearrange("e (p t) f -> e p (t f)", p=P)
        up_v = w_up[0].rearrange("e (p t) f -> e p (t f)", p=P)
        down_v = w_down[0].rearrange("e (t p) c -> e p t c", p=P)

        s_x, s_par, s_const, s_residue, s_turned, s_xhi, s_xlo = map(sem, (
            "s_x", "s_par", "s_const", "s_residue", "s_turned", "s_xhi", "s_xlo"))
        s_raw = [sem(f"s_raw{r}") for r in range(2)]
        s_hi, s_lo, s_mm = map(sem, ("s_hi", "s_lo", "s_mm"))
        s_ev = [sem(f"s_ev{r}") for r in range(2)]
        s_scored, s_masked, s_exp, s_norm, s_pturn, s_pt, s_av, s_att = map(sem, (
            "s_scored", "s_masked", "s_exp", "s_norm", "s_pturn", "s_pt", "s_av", "s_att"))
        s_asig, s_glu, s_conv, s_asum, s_acent, s_asq, s_avar, s_astd, s_anorm, s_aout = map(sem, (
            "s_asig", "s_glu", "s_conv", "s_asum", "s_acent", "s_asq", "s_avar", "s_astd", "s_anorm", "s_aout"))
        s_ctap, s_gated, s_added, s_brhi, s_brlo, s_mhi, s_mlo = map(sem, (
            "s_ctap", "s_gated", "s_added", "s_brhi", "s_brlo", "s_mhi", "s_mlo"))
        s_xr, s_lnp, s_var, s_std, s_scaled, s_ln = map(sem, (
            "s_xr", "s_lnp", "s_var", "s_std", "s_scaled", "s_ln"))
        s_perm, s_hdram, s_ht, s_rw, s_ws, s_logit, s_score, s_chosen, s_count, s_flag = map(sem, (
            "s_perm", "s_hdram", "s_ht", "s_rw", "s_ws", "s_logit", "s_score", "s_chosen", "s_count", "s_flag"))
        s_shgu, s_shsig, s_shh, s_shd, s_shacc, s_tab, s_bias = map(sem, (
            "s_shgu", "s_shsig", "s_shh", "s_shd", "s_shacc", "s_tab", "s_bias"))
        s_hit, s_hitsum, s_idx, s_idxnow, s_hg, s_turn, s_turnout = map(sem, (
            "s_hit", "s_hitsum", "s_idx", "s_idxnow", "s_hg", "s_turn", "s_turnout"))
        s_w = [sem(f"s_w{r}") for r in range(6)]
        s_gu, s_sig, s_eh, s_dn, s_yt, s_yw, s_mine, s_ln2p, s_done = map(sem, (
            "s_gu", "s_sig", "s_eh", "s_dn", "s_yt", "s_yw", "s_mine", "s_ln2p", "s_done"))
        s_got = [sem(f"s_got{r}") for r in range(N_GATHER)]
        s_fetch, s_used, s_hgzero, s_turned_par, s_par_t, s_wsd = map(sem, (
            "s_fetch", "s_used", "s_hgzero", "s_turned_par", "s_par_t", "s_wsd"))
        s_pool, s_dve = map(sem, ("s_pool", "s_dve"))

        def seg(name, n, length, base):
            return {"name": name, "n": n, "len": length, "base": base}

        segs, units = [], 0
        for name, n, length in (("qk0", 6, 4), ("v0", 3, 4), ("aval", CT // 4, 4), ("agate", CT // 4, 4),
                                ("qk1", 6, 4), ("v1", 3, 4), ("cc", CT // 4, 4), ("ch", CT // 4, 4),
                                ("cb", CT // 4, 4), ("gb", 6, 12), ("out", KT // 4, 4)):
            segs.append(seg(name, n, length, units))
            units += n * length
        at_seg = {s["name"]: s for s in segs}
        BASE_OUT = at_seg["out"]["base"]

        def chunk(name, i, c):
            if name in ("qk0", "v0", "qk1", "v1"):
                first = {"qk": 0, "v0": 6, "v1": 6}[name if name in ("v0", "v1") else "qk"]
                col = OFF_Q + first * C + i * C + int(name[-1]) * (C // 2) + c * 256
            elif name == "aval":
                col = i * 512 + c * 256
            elif name == "agate":
                col = C + i * 512 + c * 256
            elif name in ("cb", "cc", "ch"):
                col = OFF_C + ("cb", "cc", "ch").index(name) * C + i * 512 + c * 256
            elif name == "gb" and c < 4:
                col = OFF_G + i * (D // 2) + c * 256
            elif name == "gb":
                return w_branch_v[:, bass.ds((i // 2) * CT, CT), bass.ds((i % 2) * (D // 2) + (c - 4) * 512, 512)]
            else:
                return w_out_v[:, :, bass.ds(i * 512 + c * 256, 256)]
            return w_in_v[:, :, bass.ds(col, 256)]

        def wide(name, j):
            return name == "gb" and j >= 8

        def raw_half(u, w):
            if w:
                return raw[u.raw][:, :].rearrange("p (t c) -> p t c", t=CT)[:, :, u.half * 256:u.half * 256 + 256]
            return raw[u.raw][:, :].rearrange("p (t c) -> p t c", t=KT)[:, :, u.half * P:u.half * P + P]

        def tiles(ring, u, w):
            return ring[u.ring][:, :].rearrange("p (t c) -> p t c", t=CT if w else KT)

        def stream(eng, per_unit, evacuate, after=lambda name, i, j: None):
            prev = None
            for s in segs:
                def body(i, s=s, prev=prev):
                    for j in range(s["len"]):
                        u = Unit(s["base"], s["len"], i, j)
                        per_unit(s["name"], i, j, u)
                        if j >= 3:
                            evacuate(s["name"], i, j - 3, Unit(s["base"], s["len"], i, j - 3))
                        elif not (isinstance(i, int) and i == 0):
                            jj = s["len"] + j - 3
                            evacuate(s["name"], i - 1, jj, Unit(s["base"], s["len"], i - 1, jj))
                        elif prev is not None:
                            jj = prev["len"] + j - 3
                            evacuate(prev["name"], prev["n"] - 1, jj, Unit(prev["base"], prev["len"], prev["n"] - 1, jj))
                        after(s["name"], i, j)
                body(0)
                with eng.Fori(1, s["n"]) as i:
                    body(i)
                prev = s
            for j in range(prev["len"] - 3, prev["len"]):
                evacuate(prev["name"], prev["n"] - 1, j, Unit(prev["base"], prev["len"], prev["n"] - 1, j))

        JOBS = 2 * HALF

        def evacuated(eng, name):
            for r in range(2):
                eng.wait_ge(s_ev[r], at_seg[name]["base"] // 2)

        def layer_norm_rows(eng, g, b, n):
            for tt in range(TT):
                for c in range(4):
                    nc.vector.bn_stats(stats[:, tt, c, :], acc[:, tt, c * 512:(c + 1) * 512]).then_inc(s_dve, 1)
            eng.wait_ge(s_dve, dve_done(8))
            for tt in range(TT):
                nc.vector.bn_aggr(mean_var[:, tt, :], stats[:, tt, :, :]).then_inc(s_dve, 1)
            eng.wait_ge(s_dve, dve_done(2))
            nc.vector.tensor_scalar(var_eps, mean_var[:, :, 1], LN_EPS, None, ALU.add).then_inc(s_var, 1)
            eng.wait_ge(s_std, n + 1)
            nc.vector.reciprocal(rstd, std).then_inc(s_dve, 1)
            eng.wait_ge(s_dve, dve_done(1))
            for tt in range(TT):
                nc.vector.tensor_scalar(acc[:, tt, :], acc[:, tt, :], mean_var[:, tt, 0:1], rstd[:, tt:tt + 1],
                                        ALU.subtract, ALU.mult).then_inc(s_dve, 1)
                eng.wait_ge(s_dve, dve_done(1))
                if tt == 0:
                    eng.wait_ge(s_ln2p if n else s_lnp, 32)
                nc.vector.tensor_tensor(acc[:, tt, :], acc[:, tt, :], g[:, :], ALU.mult).then_inc(s_scaled, 1)

        counted = {"dve": 0, "pool": 0}

        def dve_done(k):
            counted["dve"] += k
            return counted["dve"]

        def pool_done(k):
            counted["pool"] += k
            return counted["pool"]

        block = ctx.enter_context(nc.Block())

        @block.sync
        def _(sp):
            for s in segs:
                def body(i, s=s):
                    for c in range(s["len"] // 2):
                        u = Unit(s["base"], s["len"], i, 2 * c)
                        if not u.first:
                            sp.wait_ge(s_lo, u.n - 2)
                        if s["name"] == "gb" and c >= 4:
                            dst = raw[u.raw][:, :].rearrange("p (t c) -> p t c", t=CT)
                        else:
                            dst = raw[u.raw][:, :].rearrange("p (t c) -> p t c", t=KT)
                        sp.dma_start(dst, chunk(s["name"], i, c)).then_inc(s_raw[u.raw], 16)
                body(0)
                with sp.Fori(1, s["n"]) as i:
                    body(i)

            sp.wait_ge(s_added, 24)
            sp.dma_start(exp_w[0][:, :], gate_v[0]).then_inc(s_w[0], 16)
            sp.dma_start(exp_w[1][:, :], up_v[0]).then_inc(s_w[1], 16)
            sp.wait_ge(s_mm, units)
            for r, v in enumerate((ws_gate, ws_up)):
                sp.dma_start(ws[r][:, :], v[0].rearrange("(p t) f -> p (t f)", p=P)).then_inc(s_ws, 16)
            sp.dma_start(exp_w[3][:, :], gate_v[1]).then_inc(s_w[3], 16)
            sp.dma_start(exp_w[4][:, :], up_v[1]).then_inc(s_w[4], 16)
            sp.dma_start(exp_w[2][:, :].rearrange("p (t c) -> p t c", t=FT), down_v[0]).then_inc(s_w[2], 16)
            sp.wait_ge(s_logit, 1)
            sp.dma_start(ws[2][:, :].rearrange("p (t c) -> p t c", t=FT),
                         ws_down[0].rearrange("(t p) c -> p t c", p=P)).then_inc(s_wsd, 16)

            def load_down(slot, e):
                return sp.dma_start(exp_w[slot][:, :].rearrange("p (t c) -> p t c", t=FT),
                                    down_v[bass.ds(e, 1)].rearrange("e p t c -> p (e t) c")).then_inc(s_w[slot], 16)

            def load_gate_up(slot, e):
                sp.dma_start(exp_w[slot][:, :], gate_v[bass.ds(e, 1)].rearrange("e p m -> (e p) m")).then_inc(s_w[slot], 16)
                sp.dma_start(exp_w[slot + 1][:, :], up_v[bass.ds(e, 1)].rearrange("e p m -> (e p) m")).then_inc(s_w[slot + 1], 16)

            def experts(i, n):
                sp.wait_ge(s_gu, 2 * n - 1)
                load_gate_up(0, 2 * i)
                if isinstance(n, int) and n == 1:
                    sp.wait_ge(s_hdram, 32)
                    sp.wait_ge(s_ht, 8)
                else:
                    sp.wait_ge(s_dn, 2 * n - 2)
                load_down(5, 2 * i - 1)
                sp.wait_ge(s_gu, 2 * n)
                load_gate_up(3, 2 * i + 1)
                sp.wait_ge(s_dn, 2 * n - 1)
                load_down(2, 2 * i)

            experts(1, 1)
            with sp.Fori(2, PAIRS) as i:
                experts(i, i)
            sp.wait_ge(s_dn, 2 * PAIRS - 2)
            load_down(5, E - 1)
            sp.wait_ge(s_flag, 1)
            too_many = sp.value_load(flag[0:1, 0:1], min_val=0, max_val=TOK)
            with sp.If(too_many > SLOTS):
                with sp.Fori(1, BLOCKS) as b:
                    n = b * PAIRS
                    sp.wait_ge(s_gu, 2 * n - 1)
                    load_gate_up(0, 0)
                    sp.wait_ge(s_gu, 2 * n)
                    load_gate_up(3, 1)
                    sp.wait_ge(s_dn, 2 * n - 1)
                    load_down(2, 0)
                    with sp.Fori(1, PAIRS) as i:
                        experts(i, b * PAIRS + i)
                    sp.wait_ge(s_dn, 2 * n + 2 * PAIRS - 2)
                    load_down(5, E - 1)
            sp.wait_ge(s_ln, 4)
            for tt in range(TT):
                sp.dma_start(out2[tt * P:(tt + 1) * P, :], acc[:, tt, :]).then_inc(s_done, 16)
            sp.wait_ge(s_done, 32)

        @block.gpsimd
        def _(pool):
            pool.memset(ident[:, :], 0.0).then_inc(s_pool, 1)
            pool.memset(ones[:, :], 1.0).then_inc(s_const, 1)
            pool.wait_ge(s_pool, pool_done(1))
            pool.affine_select(out=ident[:, :], in_=ident[:, :], compare_op=ALU.not_equal, fill=1.0, base=0,
                               pattern=[[-1, P]], channel_multiplier=1).then_inc(s_const, 1)
            pool.iota(dist[:, :], pattern=[[-1, 2 * P]], base=P, channel_multiplier=1).then_inc(s_const, 1)
            pool.memset(a_pad[:, :, 0:TAPS_A - 1], 0.0).then_inc(s_const, 1)
            pool.wait_ge(s_residue, 3)
            for g in range(N_GROUPS_ATT):
                m = mask[:, g, :, :].rearrange("p a b -> p (a b)")
                pool.affine_select(out=m, in_=m, compare_op=ALU.is_ge, fill=MASKED, base=P,
                                   pattern=[[-1, 2 * P]], channel_multiplier=1).then_inc(s_pool, 1)
            pool.wait_ge(s_pool, pool_done(3))
            m = mask[:, 0, :, :].rearrange("p a b -> p (a b)")
            pool.affine_select(out=m, in_=m, compare_op=ALU.is_ge, fill=MASKED, base=0,
                               pattern=[[1, 2 * P]], channel_multiplier=-1).then_inc(s_const, 1)

            for j in range(CT):
                pool.wait_ge(s_asig, j + 1)
                row = a_pad[:, j, TAPS_A - 1:]
                pool.tensor_tensor(row, row, a_sig[j % 2][:, :], ALU.mult).then_inc(s_glu, 1)

            pool.wait_ge(s_conv, CT * TAPS_A)
            pool.memset(c_pad[:, :, 0:TAPS_C - 1], 0.0).then_inc(s_const, 1)
            pool.wait_ge(s_att, 2 * JOBS)
            pool.memset(merged[:, :, :], 0.0).then_inc(s_pool, 1)
            pool.wait_ge(s_pool, pool_done(1))

            def add_branch(i, k):
                w = 4 * i + k
                pool.wait_ge(s_gated, w + 1)
                if not (isinstance(w, int) and w == 0):
                    pool.wait_ge(s_added, w)
                m = merged[:, bass.ds((i % 2) * CT + 2 * k, 2), :]
                pool.tensor_tensor(m, m, gated[k % 2][:, :, :], ALU.add).then_inc(s_added, 1)

            for k in range(4):
                add_branch(0, k)
            with pool.Fori(1, 6) as i:
                for k in range(4):
                    add_branch(i, k)

            pool.wait_ge(s_mm, BASE_OUT)
            pool.dma_start(acc[:, :, :], x2.rearrange("(a p) c -> p a c", p=P)).then_inc(s_xr, 16)
            pool.wait_ge(s_mlo, 4)
            pool.dma_start(ln_g[:, :], ln1_g.to_broadcast([P, D])).then_inc(s_lnp, 16)
            pool.dma_start(ln_b[:, :], ln1_b.to_broadcast([P, D])).then_inc(s_lnp, 16)
            pool.dma_start(bias_b[:, :], router_bias.to_broadcast([P, E])).then_inc(s_bias, 16)
            pool.iota(iota_slot[:, :], pattern=[[1, TOK]], base=0, channel_multiplier=0,
                      allow_small_or_imprecise_dtypes=True).then_inc(s_tab, 1)
            pool.iota(row_base[:, :], pattern=[[SLOTS, E]], base=1, channel_multiplier=0,
                      allow_small_or_imprecise_dtypes=True).then_inc(s_tab, 1)
            pool.iota(tok_val[:, :, 0], pattern=[[P, TT]], base=0, channel_multiplier=1,
                      allow_small_or_imprecise_dtypes=True).then_inc(s_tab, 1)
            pool.memset(tok_val[:, :, 1], 1.0).then_inc(s_tab, 1)
            pool.memset(before[:, :], 1.0).then_inc(s_pool, 1)
            pool.wait_ge(s_pool, pool_done(1))
            pool.affine_select(out=before[:, :], in_=before[:, :], compare_op=ALU.is_ge, fill=0.0, base=-1,
                               pattern=[[1, P]], channel_multiplier=-1).then_inc(s_tab, 1)

            def add_shift(b, n):
                for tt in range(TT):
                    pool.wait_ge(s_scaled, 2 * n + tt + 1)
                    pool.tensor_tensor(acc[:, tt, :], acc[:, tt, :], b[:, :], ALU.add).then_inc(s_ln, 1)

            add_shift(ln_b, 0)
            pool.wait_ge(s_ln, 2)
            pool.memset(hg[:, :], 0.0).then_inc(s_hgzero, 1)
            for tt in range(TT):
                pool.wait_ge(s_perm, tt + 1)
                pool.dma_start(h_dram[tt * P:(tt + 1) * P, :], h_perm[:, tt, :]).then_inc(s_hdram, 16)
            pool.wait_ge(s_hdram, 32)
            pool.wait_ge(s_hgzero, 1)

            def fetch(i, n):
                pool.sem_inc(s_fetch, 1)
                pool.tensor_copy(idx_now[:, :], tok_idx[:, bass.ds(i, 1)]).then_inc(s_idxnow, 1)
                pool.wait_ge(s_idxnow, n + 1)
                pool.sem_inc(s_fetch, 1)
                pool.indirect_dma_start(out=hg[:, :], out_offset=None, in_=h_dram[:, :],
                                        in_offset=bass.IndirectOffsetOnAxis(ap=idx_now[:, 0:1], axis=0),
                                        bounds_check=TOK - 1, oob_is_err=False).then_inc(s_hg, 16)

            def keep(n):
                pool.dma_start(y_dram[bass.ds(n * P, P), :], y_rows[:, :]).then_inc(s_yw, 16)

            def experts(i, n):
                pool.wait_ge(s_turnout, 8 * n + 4)
                keep(n - 1)
                pool.wait_ge(s_turn, 8 * n + 8)
                fetch(i + 2, n + 2)

            def last_two(n):
                pool.wait_ge(s_turnout, 8 * n + 4)
                keep(n - 1)
                pool.wait_ge(s_turnout, 8 * n + 12)
                keep(n)
                pool.wait_ge(s_turnout, 8 * n + 16)
                keep(n + 1)

            pool.wait_ge(s_idx, 4)
            fetch(0, 0)
            pool.wait_ge(s_turn, 4)
            fetch(1, 1)
            pool.wait_ge(s_turn, 8)
            fetch(2, 2)
            pool.wait_ge(s_shgu, 1)
            pool.dma_start(ln2_gt[:, :], ln2_g.to_broadcast([P, D])).then_inc(s_ln2p, 16)
            pool.dma_start(ln2_bt[:, :], ln2_b.to_broadcast([P, D])).then_inc(s_ln2p, 16)
            with pool.Fori(1, PAIRS - 2) as i:
                experts(i, i)
            last_two(PAIRS - 2)
            pool.wait_ge(s_flag, 1)
            too_many = pool.value_load(flag[0:1, 0:1], min_val=0, max_val=TOK)
            with pool.If(too_many > SLOTS):
                with pool.Fori(1, BLOCKS) as b:
                    n = b * PAIRS
                    pool.wait_ge(s_idx, 4 * b + 4)
                    fetch(0, n)
                    pool.wait_ge(s_turn, 8 * n + 4)
                    fetch(1, n + 1)
                    pool.wait_ge(s_turn, 8 * n + 8)
                    fetch(2, n + 2)
                    with pool.Fori(1, PAIRS - 2) as i:
                        experts(i, b * PAIRS + i)
                    last_two(n + PAIRS - 2)
                    pool.wait_ge(s_yw, 16 * (n + PAIRS))
            pool.wait_ge(s_yw, 16 * PAIRS)
            pool.wait_ge(s_mine, 1)
            for k in range(TOPK):
                for tt in range(TT):
                    n = TT * k + tt
                    if n >= N_GATHER:
                        pool.wait_ge(s_used, n - N_GATHER + 1)
                    pool.indirect_dma_start(out=gather[n % N_GATHER][:, :], out_offset=None, in_=y_dram[:, :],
                                            in_offset=bass.IndirectOffsetOnAxis(ap=my_idx[:, tt, k:k + 1], axis=0),
                                            bounds_check=BLOCKS * E * SLOTS - 1,
                                            oob_is_err=False).then_inc(s_got[n % N_GATHER], 16)
            add_shift(ln2_bt, 1)

        @block.scalar
        def _(act):
            act.dma_start(x_rows[:, :, :], x2.rearrange("(a p) c -> p a c", p=P)).then_inc(s_x, 16)
            row = 0
            for v, k in ((conv_a_w[0], TAPS_A), (conv_a_b, 1), (ln_a_g, 1), (ln_a_b, 1), (conv_c_w[0], TAPS_C)):
                act.dma_start(par_rows[row:row + k, :], v).then_inc(s_par, 16)
                row += k
            for n in range(8):
                act.wait_ge(s_turned, n + 1)
                tt, t = n // 4, n % 4 * 4
                nc.scalar.activation(x_hi[:, t:t + 4, tt * P:(tt + 1) * P],
                                     turn_ring[n % 2].rearrange("p (t c) -> p t c", t=4), ACT.Copy).then_inc(s_xhi, 1)

            def split(name, i, j, u):
                if u.half == 0:
                    act.wait_ge(s_raw[u.raw], 16 * u.raw_count)
                if not u.first:
                    act.wait_ge(s_mm, u.n - 3)
                w = wide(name, j)
                nc.scalar.activation(tiles(w_hi, u, w), raw_half(u, w), ACT.Copy).then_inc(s_hi, 1)

            def evacuate(name, i, j, u):
                if name in ("ch", "cb", "out") or wide(name, j):
                    return
                act.wait_ge(s_mm, u.n + 1)
                ps = ps_proj[u.bank][:, 0:TOK]
                if name in ("qk0", "qk1"):
                    both = q_k[:, bass.ds(i, 1), j, :]
                    ins = nc.scalar.activation(both.rearrange("p a c -> p (a c)"), ps, ACT.Copy)
                elif name in ("v0", "v1"):
                    dst = v_rows[:, bass.ds(i, 1), j, :, :].rearrange("p a t c -> p (a t c)")
                    ins = nc.scalar.activation(dst, ps, ACT.Copy)
                elif name == "aval":
                    dst = a_pad[:, bass.ds(4 * i + j, 1), TAPS_A - 1:].rearrange("p a c -> p (a c)")
                    if j == 0 and isinstance(i, int):
                        act.wait_ge(s_const, 4)
                    ins = nc.scalar.activation(dst, ps, ACT.Copy)
                elif name == "agate":
                    n = 4 * i + j
                    if not (isinstance(n, int) and n < 2):
                        act.wait_ge(s_glu, n - 1)
                    ins = nc.scalar.activation(a_sig[j % 2][:, :], ps, ACT.Sigmoid)
                    ins.then_inc(s_asig, 1)
                    act.wait_ge(s_asig, n + 1)
                    act.sem_inc(s_ev[u.bank], 1)
                    return
                elif name == "cc":
                    if j == 0 and isinstance(i, int):
                        act.wait_ge(s_const, 6)
                    dst = c_pad[:, bass.ds(4 * i + j, 1), TAPS_C - 1:].rearrange("p a c -> p (a c)")
                    ins = nc.scalar.activation(dst, ps, ACT.Copy)
                else:
                    if j == 0 and not (isinstance(i, int) and i == 0):
                        act.wait_ge(s_gated, 4 * i)
                    elif j == 0:
                        act.wait_ge(s_aout, CT)
                    ins = nc.scalar.activation(gates[:, j, :], ps, ACT.Sigmoid)
                ins.then_inc(s_ev[u.bank], 1)

            def attention(half):
                def exps(job):
                    r, w = job % 2, N_GROUPS_ATT * P * (job % 2 + 1)
                    n = JOBS * half + job
                    act.wait_ge(s_masked, n + 1)
                    nc.scalar.activation(att_p[r][:, 0:w], att_p[r][:, 0:w], ACT.Exp, bias=neg_max[r],
                                         accum_out=row_sum[r]).then_inc(s_exp, 1)

                exps(0)
                for job in range(JOBS):
                    n = JOBS * half + job
                    kt = job % 2 + 1
                    if job + 1 < JOBS:
                        exps(job + 1)
                    act.wait_ge(s_pturn, n + 1)
                    if n >= 1:
                        act.wait_ge(s_av, n)
                    nc.scalar.activation(p_t[:, 0:3 * kt, :],
                                         ps_t[:, 0:3 * kt * P].rearrange("p (a b) -> p a b", b=P),
                                         ACT.Copy).then_inc(s_pt, 1)
                    act.wait_ge(s_av, n + 1)
                    nc.scalar.activation(branch[:, 1, HALF * half + job // 2, (job % 2) * P:(job % 2 + 1) * P],
                                         ps_t[:, 768:768 + P], ACT.Copy).then_inc(s_att, 1)

            def after(name, i, j):
                first = isinstance(i, int) and i == 0
                last = j == 3
                if first and last and name == "aval":
                    attention(0)
                if first and last and name == "cc":
                    attention(1)
                if first and last and name == "ch":
                    act.wait_ge(s_acent, 1)
                    nc.scalar.activation(a_sq[:, :, :], branch[:, 0, :, :], ACT.Square).then_inc(s_asq, 1)
                if first and last and name == "cb":
                    act.wait_ge(s_avar, 1)
                    nc.scalar.activation(a_rstd[:, :], a_mean[:, :], ACT.Sqrt).then_inc(s_astd, 1)
                    act.wait_ge(s_anorm, 1)
                    for c in range(CT):
                        nc.scalar.activation(branch[:, 0, c, :], branch[:, 0, c, :], ACT.Silu,
                                             scale=par[:, c, TAPS_A + 1:TAPS_A + 2],
                                             bias=par[:, c, TAPS_A + 2:TAPS_A + 3]).then_inc(s_aout, 1)
                if name == "gb" and j == 6:
                    if first:
                        act.wait_ge(s_aout, CT)
                        evacuated(act, "gb")
                    nc.scalar.activation(branch_hi[:, :, :],
                                         branch[:, bass.ds(i // 2, 1), :, :].rearrange("p n t c -> p (n t) c"),
                                         ACT.Copy).then_inc(s_brhi, 1)
                if name == "out" and first and j == 2:
                    act.wait_ge(s_added, 24)
                    for c in range(4):
                        nc.scalar.activation(merged_hi[:, 4 * c:4 * c + 4, :], merged[:, 4 * c:4 * c + 4, :],
                                             ACT.Copy).then_inc(s_mhi, 1)

            stream(act, split, evacuate, after)

            act.wait_ge(s_var, 1)
            nc.scalar.activation(std, var_eps, ACT.Sqrt).then_inc(s_std, 1)
            act.wait_ge(s_mm, units)
            act.dma_start(rw[:, :, :], router_w[0].rearrange("(p t) e -> p t e", p=P)).then_inc(s_rw, 16)
            for tt in range(TT):
                act.wait_ge(s_ln, tt + 1)
                nc.scalar.activation(h_perm[:, tt, :].rearrange("p (t q) -> p t q", t=KT),
                                     acc[:, tt, :].rearrange("p (q t) -> p t q", t=KT), ACT.Copy).then_inc(s_perm, 1)
            for n in range(8):
                act.wait_ge(s_turned, 8 + n + 1)
                tt, t = n // 4, n % 4 * 4
                nc.scalar.activation(h_t[:, t:t + 4, tt * P:(tt + 1) * P],
                                     turn_ring[n % 2].rearrange("p (t c) -> p t c", t=4), ACT.Copy).then_inc(s_ht, 1)
            act.wait_ge(s_logit, 1)
            nc.scalar.activation(scores[:, :, :], ps_s[1][:, 0:TT * E].rearrange("p (a e) -> p a e", a=TT),
                                 ACT.Sigmoid).then_inc(s_score, 1)
            act.wait_ge(s_shgu, 1)
            nc.scalar.activation(sh_sig[:, :, :], ps_proj[0][:, :].rearrange("p (a c) -> p a c", a=FT),
                                 ACT.Silu).then_inc(s_shsig, 1)

            def silu(k, n):
                act.wait_ge(s_gu, 2 * n + k + 1)
                if not (isinstance(n, int) and n == 0):
                    act.wait_ge(s_eh, 2 * n + k - 1)
                nc.scalar.activation(expert_sig[k][:, :, :],
                                     ps_proj[k][:, 0:FT * SLOTS].rearrange("p (a c) -> p a c", a=FT),
                                     ACT.Silu).then_inc(s_sig, 1)

            def take_down(k, n):
                act.wait_ge(s_dn, 2 * n + k + 1)
                nc.scalar.activation(y_t[:, :, k * SLOTS:(k + 1) * SLOTS],
                                     down_out[k][:, :].rearrange("p (t c) -> p t c", t=KT), ACT.Copy).then_inc(s_yt, 1)

            def experts(n):
                silu(0, n)
                take_down(1, n - 1)
                silu(1, n)
                take_down(0, n)

            def whole_pass(n):
                silu(0, n)
                silu(1, n)
                take_down(0, n)
                with act.Fori(1, PAIRS) as i:
                    experts(n + i)
                take_down(1, n + PAIRS - 1)

            whole_pass(0)
            act.wait_ge(s_flag, 1)
            too_many = act.value_load(flag[0:1, 0:1], min_val=0, max_val=TOK)
            with act.If(too_many > SLOTS):
                with act.Fori(1, BLOCKS) as b:
                    whole_pass(b * PAIRS)
            act.wait_ge(s_var, 2)
            nc.scalar.activation(std, var_eps, ACT.Sqrt).then_inc(s_std, 1)

        @block.vector
        def _(dve):
            dve.wait_ge(s_const, 4)
            nc.vector.memset(mask[:, 0, :, :], 0.0).then_inc(s_residue, 1)
            for g in (1, 2):
                nc.vector.tensor_scalar(dist_mod[:, g - 1, :], dist[:, :], DILATIONS[g] - 1, None,
                                        ALU.bitwise_and).then_inc(s_dve, 1)
            dve.wait_ge(s_dve, dve_done(2))
            for g in (1, 2):
                nc.vector.tensor_scalar(mask[:, g, :, :].rearrange("p a b -> p (a b)"), dist_mod[:, g - 1, :], 1.0,
                                        MASKED, ALU.min, ALU.mult).then_inc(s_residue, 1)
            for r in range(2):
                dve.wait_ge(s_turned_par, r + 1)
                nc.vector.tensor_copy(par[:, 4 * r:4 * r + 4, :],
                                      ps_s[1][:, r * 512:r * 512 + 4 * N_PAR].rearrange("p (a b) -> p a b", b=N_PAR)
                                      ).then_inc(s_par_t, 1)
            for n in range(8):
                dve.wait_ge(s_xhi, n + 1)
                tt, t = n // 4, n % 4 * 4
                nc.vector.tensor_tensor(x_lo[:, t:t + 4, tt * P:(tt + 1) * P],
                                        turn_ring[n % 2].rearrange("p (t c) -> p t c", t=4),
                                        x_hi[:, t:t + 4, tt * P:(tt + 1) * P].bitcast(F32),
                                        ALU.subtract).then_inc(s_xlo, 1)

            def split(name, i, j, u):
                dve.wait_ge(s_hi, u.n + 1)
                w = wide(name, j)
                nc.vector.tensor_tensor(tiles(w_lo, u, w), raw_half(u, w), tiles(w_hi, u, w).bitcast(F32),
                                        ALU.subtract).then_inc(s_lo, 1)

            def evacuate(name, i, j, u):
                if not (name in ("ch", "cb", "out") or wide(name, j)):
                    return
                dve.wait_ge(s_mm, u.n + 1)
                if name == "ch":
                    n = 4 * i + j
                    if j == 0 and isinstance(i, int):
                        evacuated(dve, "ch")
                        dve.wait_ge(s_const, 6)
                    dst = c_pad[:, bass.ds(n, 1), TAPS_C - 1:].rearrange("p a c -> p (a c)")
                    nc.vector.tensor_tensor(dst, ps_proj[u.bank][:, 0:TOK], dst, ALU.mult).then_inc(s_ev[u.bank], 1)
                    dve.wait_ge(s_ev[u.bank], u.bank_count + 1)
                    y = branch[:, 2, bass.ds(n, 1), :].rearrange("p a c -> p (a c)")
                    for k in range(TAPS_C):
                        v = c_pad[:, bass.ds(n, 1), k:k + TOK].rearrange("p a c -> p (a c)")
                        w = par[:, bass.ds(n, 1), TAPS_A + 3 + k:TAPS_A + 4 + k].rearrange("p a c -> p (a c)")
                        if k == 0:
                            ins = nc.vector.tensor_scalar(y, v, w, None, ALU.mult)
                        else:
                            ins = nc.vector.scalar_tensor_tensor(out=y, in0=v, scalar=w, in1=y, op0=ALU.mult, op1=ALU.add)
                        ins.then_inc(s_ctap, 1)
                        dve.wait_ge(s_ctap, n * TAPS_C + k + 1)
                elif name == "cb":
                    y = branch[:, 2, bass.ds(4 * i + j, 1), :].rearrange("p a c -> p (a c)")
                    nc.vector.tensor_tensor(y, ps_proj[u.bank][:, 0:TOK], y, ALU.mult).then_inc(s_ev[u.bank], 1)
                elif name == "out":
                    if j == 0 and isinstance(i, int):
                        dve.wait_ge(s_xr, 16)
                    cols = acc[:, :, bass.ds(512 * i + P * j, P)]
                    nc.vector.scalar_tensor_tensor(out=cols, in0=cols, scalar=ALPHA,
                                                   in1=ps_proj[u.bank][:, 0:TOK].rearrange("p (a c) -> p a c", a=TT),
                                                   op0=ALU.mult, op1=ALU.add).then_inc(s_ev[u.bank], 1)
                else:
                    k = j - 8
                    w = 4 * i + k
                    if not (isinstance(w, int) and w < 2):
                        dve.wait_ge(s_added, w - 1)
                    if k == 0:
                        dve.wait_ge(s_ev[0], u.bank_count)
                        dve.wait_ge(s_ev[1], u.bank_count)
                    nc.vector.tensor_tensor(gated[k % 2][:, :, :].rearrange("p a c -> p (a c)"), ps_proj[u.bank][:, :],
                                            gates[:, 2 * k:2 * k + 2, :].rearrange("p a c -> p (a c)"),
                                            ALU.mult).then_inc(s_gated, 1)
                    dve.wait_ge(s_gated, w + 1)
                    dve.sem_inc(s_ev[u.bank], 1)

            def attention(half):
                def masked(job):
                    n, r, kt = JOBS * half + job, job % 2, job % 2 + 1
                    dve.wait_ge(s_scored, n + 1)
                    if n >= 2:
                        dve.wait_ge(s_pturn, n - 1)
                    p = att_p[r][:, 0:3 * kt * P].rearrange("p (g k) -> p g k", g=N_GROUPS_ATT)
                    m = mask[:, :, 2 - kt:2, :].rearrange("p g a b -> p g (a b)")
                    nc.vector.tensor_tensor_reduce(p, ps_s[r][:, 0:3 * kt * P].rearrange("p (g k) -> p g k", g=N_GROUPS_ATT),
                                                   m, SCALE, NEG, ALU.add, ALU.max, row_max[r]).then_inc(s_dve, 1)
                    dve.wait_ge(s_dve, dve_done(1))
                    nc.vector.tensor_scalar(neg_max[r], row_max[r], -1.0, None, ALU.mult).then_inc(s_masked, 1)

                if half == 0:
                    dve.wait_ge(s_const, 5)
                masked(0)
                for job in range(JOBS):
                    n, r, kt = JOBS * half + job, job % 2, job % 2 + 1
                    if job + 1 < JOBS:
                        masked(job + 1)
                    dve.wait_ge(s_exp, n + 1)
                    nc.vector.reciprocal(row_rcp[r], row_sum[r]).then_inc(s_dve, 1)
                    dve.wait_ge(s_dve, dve_done(1))
                    nc.vector.tensor_scalar(att_p[r][:, 0:3 * kt * P], att_p[r][:, 0:3 * kt * P], row_rcp[r], None,
                                            ALU.mult).then_inc(s_norm, 1)

            def conv_tap(tap, const):
                if const and tap == 0:
                    dve.wait_ge(s_glu, CT)
                    dve.wait_ge(s_par_t, 2)
                else:
                    dve.wait_ge(s_conv, CT * tap)
                for c in range(CT):
                    v = a_pad[:, c, bass.ds(tap, TOK)]
                    w = par[:, c, bass.ds(tap, 1)]
                    y = branch[:, 0, c, :]
                    if const and tap == 0:
                        ins = nc.vector.tensor_scalar(y, v, w, par[:, c, TAPS_A:TAPS_A + 1], ALU.mult, ALU.add)
                    else:
                        ins = nc.vector.scalar_tensor_tensor(out=y, in0=v, scalar=w, in1=y, op0=ALU.mult, op1=ALU.add)
                    ins.then_inc(s_conv, 1)

            def after(name, i, j):
                first = isinstance(i, int) and i == 0
                if first and j == 3 and name == "aval":
                    attention(0)
                if name == "qk1" and (j == 3 or not first):
                    conv_tap(4 * i + j - 3, first)
                if name == "v1" and first:
                    conv_tap(21 + j, False)
                if name == "v1" and not first and j < 3:
                    conv_tap(25 + 3 * (i - 1) + j, False)
                if first and j == 3 and name == "cc":
                    attention(1)
                if first and j == 3 and name == "ch":
                    dve.wait_ge(s_asum, 1)
                    nc.vector.tensor_scalar(a_mean[:, :], ps_s[0][:, 0:TOK], 1.0 / C, None, ALU.mult).then_inc(s_dve, 1)
                    dve.wait_ge(s_dve, dve_done(1))
                    nc.vector.tensor_tensor(branch[:, 0, :, :], branch[:, 0, :, :],
                                            a_mean[:, :].unsqueeze(1).to_broadcast([P, CT, TOK]),
                                            ALU.subtract).then_inc(s_acent, 1)
                if first and j == 3 and name == "cb":
                    dve.wait_ge(s_asum, 2)
                    nc.vector.tensor_scalar(a_mean[:, :], ps_s[0][:, 512:512 + TOK], 1.0 / C, LN_EPS, ALU.mult,
                                            ALU.add).then_inc(s_avar, 1)
                    dve.wait_ge(s_astd, 1)
                    nc.vector.reciprocal(a_mean[:, :], a_rstd[:, :]).then_inc(s_dve, 1)
                    dve.wait_ge(s_dve, dve_done(1))
                    nc.vector.tensor_tensor(branch[:, 0, :, :], branch[:, 0, :, :],
                                            a_mean[:, :].unsqueeze(1).to_broadcast([P, CT, TOK]),
                                            ALU.mult).then_inc(s_anorm, 1)
                if name == "gb" and j == 6:
                    dve.wait_ge(s_brhi, i + 1)
                    nc.vector.tensor_tensor(branch_lo[:, :, :],
                                            branch[:, bass.ds(i // 2, 1), :, :].rearrange("p n t c -> p (n t) c"),
                                            branch_hi[:, :, :].bitcast(F32), ALU.subtract).then_inc(s_brlo, 1)
                if name == "out" and first and j == 2:
                    for c in range(4):
                        dve.wait_ge(s_mhi, c + 1)
                        nc.vector.tensor_tensor(merged_lo[:, 4 * c:4 * c + 4, :], merged[:, 4 * c:4 * c + 4, :],
                                                merged_hi[:, 4 * c:4 * c + 4, :].bitcast(F32),
                                                ALU.subtract).then_inc(s_mlo, 1)

            stream(dve, split, evacuate, after)

            evacuated_all = units // 2
            for r in range(2):
                dve.wait_ge(s_ev[r], evacuated_all)
            layer_norm_rows(dve, ln_g, ln_b, 0)

            def step(ins, k=1):
                ins.then_inc(s_dve, 1)
                dve.wait_ge(s_dve, dve_done(1))

            def batch(instructions):
                k = 0
                for ins in instructions:
                    ins.then_inc(s_dve, 1)
                    k += 1
                dve.wait_ge(s_dve, dve_done(k))

            nc.vector.memset(groups[:, :, 8:16], FILL).then_inc(s_dve, 1)
            dve.wait_ge(s_dve, dve_done(1))
            dve.wait_ge(s_score, 1)
            dve.wait_ge(s_bias, 16)
            step(nc.vector.tensor_tensor(choice[:, :, :], scores[:, :, :],
                                         bias_b[:, :].unsqueeze(1).to_broadcast([P, TT, E]), ALU.add))
            G8 = E // N_ROUTE_GROUPS
            batch(nc.vector.max(top_in_group[:, tt, g, :], choice[:, tt, g * G8:(g + 1) * G8])
                  for tt in range(TT) for g in range(N_ROUTE_GROUPS))
            step(nc.vector.tensor_tensor(groups[:, :, 0:8], top_in_group[:, :, :, 0], top_in_group[:, :, :, 1], ALU.add))
            batch(nc.vector.max(best_groups[:, tt, :], groups[:, tt, :]) for tt in range(TT))
            step(nc.vector.memset(best_groups[:, :, TOPK_GROUPS:8], FILL))
            batch(nc.vector.match_replace(groups_left[:, tt, :], best_groups[:, tt, :], groups[:, tt, :], CHOSEN)
                  for tt in range(TT))
            step(nc.vector.tensor_scalar(group_in[:, :, :], groups_left[:, :, 0:8], CHOSEN, None, ALU.is_equal))
            step(nc.vector.tensor_scalar(group_out[:, :, :], group_in[:, :, :], -NEG, NEG, ALU.mult, ALU.add))
            by_group = lambda a: a[:, :, :].rearrange("p a (g e) -> p (a g) e", e=G8)
            spread = lambda a: a[:, :, :].rearrange("p a g -> p (a g)").unsqueeze(2).to_broadcast(
                [P, TT * N_ROUTE_GROUPS, G8])
            step(nc.vector.tensor_tensor(by_group(masked), by_group(choice), spread(group_in), ALU.mult))
            step(nc.vector.tensor_tensor(by_group(masked), by_group(masked), spread(group_out), ALU.add))
            batch(nc.vector.max(best[:, tt, :], masked[:, tt, :]) for tt in range(TT))
            batch(nc.vector.match_replace(left[:, tt, :], best[:, tt, :], masked[:, tt, :], CHOSEN) for tt in range(TT))
            nc.vector.tensor_scalar(chosen[:, :, :], left[:, :, :], CHOSEN, None, ALU.is_equal).then_inc(s_chosen, 1)
            dve.wait_ge(s_chosen, 1)
            step(nc.vector.tensor_scalar(slot_of[:, :, :], chosen[:, :, :], -NO_SLOT, NO_SLOT, ALU.mult, ALU.add))
            dve.wait_ge(s_count, 1)
            step(nc.vector.tensor_tensor(slot_of[:, :, :], slot_of[:, :, :],
                                         ps_s[1][:, 512:512 + TT * E].rearrange("p (a e) -> p a e", a=TT), ALU.add))
            step(nc.vector.tensor_reduce(most, ps_s[1][:, 512 + TT * E:512 + (TT + 1) * E], AX_X, ALU.max))
            nc.vector.tensor_copy(flag[:, :], most).then_inc(s_flag, 1)

            def index(b):
                for tt in range(TT):
                    if not (isinstance(b, int) and b == 0 and tt == 0):
                        dve.wait_ge(s_hitsum, 2 * b + tt)
                    nc.vector.tensor_tensor(hits[:, :, :],
                                            slot_of[:, tt, :].unsqueeze(2).to_broadcast([P, E, SLOTS]),
                                            iota_slot[:, bass.ds(b * SLOTS, SLOTS)].unsqueeze(1).to_broadcast(
                                                [P, E, SLOTS]), ALU.is_equal).then_inc(s_hit, 1)
                dve.wait_ge(s_hitsum, 2 * b + 2)
                sums = lambda tt: ps_s[0][:, 512 * tt:512 * tt + 2 * PAIRS].rearrange("p (n k) -> p n k", k=2)
                nc.vector.tensor_copy(hit_sum[0][:, :, :], sums(0)).then_inc(s_idx, 1)
                dve.wait_ge(s_idx, 4 * b + 1)
                nc.vector.tensor_tensor(hit_sum[1][:, :, :], sums(1), hit_sum[0][:, :, :], ALU.add).then_inc(s_idx, 1)
                dve.wait_ge(s_idx, 4 * b + 2)
                nc.vector.tensor_scalar(hit_sum[0][:, :, 0], hit_sum[1][:, :, 1], -NO_ROW, NO_ROW, ALU.mult,
                                        ALU.add).then_inc(s_idx, 1)
                dve.wait_ge(s_idx, 4 * b + 3)
                nc.vector.tensor_tensor(tok_idx[:, :], hit_sum[0][:, :, 0], hit_sum[1][:, :, 0], ALU.add).then_inc(s_idx, 1)

            dve.wait_ge(s_tab, 5)
            index(0)

            dve.wait_ge(s_shsig, 1)
            nc.vector.tensor_tensor(sh_h[:, :, :], ps_proj[1][:, :].rearrange("p (a c) -> p a c", a=FT),
                                    sh_sig[:, :, :], ALU.mult).then_inc(s_shh, 1)
            dve.wait_ge(s_perm, 2)
            for n in range(8):
                dve.wait_ge(s_shd, n + 1)
                cols = acc[:, n // 4, n % 4 * 512:n % 4 * 512 + 512]
                nc.vector.scalar_tensor_tensor(out=cols, in0=cols, scalar=ALPHA, in1=down_out[n % 2][:, 0:512],
                                               op0=ALU.mult, op1=ALU.add).then_inc(s_shacc, 1)

            step(nc.vector.tensor_tensor(weight[:, :, :], scores[:, :, :], chosen[:, :, :], ALU.mult))
            step(nc.vector.tensor_reduce(w_sum, weight[:, :, :], AX_X, ALU.add))
            step(nc.vector.reciprocal(w_rcp, w_sum))
            batch(nc.vector.tensor_scalar(weight[:, tt, :], weight[:, tt, :], w_rcp[:, tt:tt + 1], ROUTED_SCALE,
                                          ALU.mult, ALU.mult) for tt in range(TT))
            step(nc.vector.tensor_tensor(row_of[:, :, :], slot_of[:, :, :],
                                         row_base[:, :].unsqueeze(1).to_broadcast([P, TT, E]), ALU.add))
            for b in range(1, BLOCKS):
                step(nc.vector.tensor_scalar(masked[:, :, :], slot_of[:, :, :], float(b * SLOTS),
                                             float(E * SLOTS - SLOTS), ALU.is_ge, ALU.mult))
                step(nc.vector.tensor_tensor(row_of[:, :, :], row_of[:, :, :], masked[:, :, :], ALU.add))
            step(nc.vector.tensor_tensor(row_of[:, :, :], row_of[:, :, :], chosen[:, :, :], ALU.mult))
            batch(nc.vector.max(my_row[:, tt, :], row_of[:, tt, :]) for tt in range(TT))
            for tt in range(TT):
                batch(nc.vector.scalar_tensor_tensor(out=match[:, k, :], in0=row_of[:, tt, :],
                                                     scalar=my_row[:, tt, k:k + 1], in1=weight[:, tt, :],
                                                     op0=ALU.is_equal, op1=ALU.mult) for k in range(TOPK))
                step(nc.vector.tensor_reduce(my_w[:, tt, :], match[:, :, :], AX_X, ALU.add))
            nc.vector.tensor_scalar(my_idx[:, :, :], my_row[:, :, :], -1.0, None, ALU.add).then_inc(s_mine, 1)

            def product(k, n):
                dve.wait_ge(s_sig, 2 * n + k + 1)
                if not (isinstance(n, int) and n == 0):
                    dve.wait_ge(s_dn, 2 * n + k - 1)
                nc.vector.tensor_tensor(expert_h[k][:, :, :],
                                        ps_proj[k][:, FT * SLOTS:2 * FT * SLOTS].rearrange("p (a c) -> p a c", a=FT),
                                        expert_sig[k][:, :, :], ALU.mult).then_inc(s_eh, 1)

            def rows_out(t0, n):
                for g in range(4):
                    dve.wait_ge(s_turn, t0 + g + 1)
                    if g == 0 and not (isinstance(n, int) and n == 0):
                        dve.wait_ge(s_yw, 16 * n)
                    nc.vector.tensor_copy(y_rows[:, g * 512:(g + 1) * 512], turn_ring[g % 2]).then_inc(s_turnout, 1)

            def rows_in(t0):
                for g in range(4):
                    dve.wait_ge(s_turn, t0 + g + 1)
                    nc.vector.tensor_copy(xg_t[:, 4 * g:4 * g + 4, :],
                                          turn_ring[g % 2].rearrange("p (t c) -> p t c", t=4)).then_inc(s_turnout, 1)

            def whole_pass(n):
                rows_in(8 * n)
                product(0, n)
                product(1, n)
                rows_in(8 * n + 4)
                with dve.Fori(1, PAIRS - 1) as i:
                    m = n + i
                    product(0, m)
                    product(1, m)
                    rows_out(8 * m, m - 1)
                    rows_in(8 * m + 4)
                m = n + PAIRS - 1
                product(0, m)
                product(1, m)
                rows_out(8 * m, m - 1)
                rows_out(8 * m + 4, m)

            whole_pass(0)
            too_many = dve.value_load(flag[0:1, 0:1], min_val=0, max_val=TOK)
            with dve.If(too_many > SLOTS):
                with dve.Fori(1, BLOCKS) as b:
                    index(b)
                    whole_pass(b * PAIRS)
            for k in range(TOPK):
                for tt in range(TT):
                    n = TT * k + tt
                    dve.wait_ge(s_got[n % N_GATHER], 16 * (n // N_GATHER + 1))
                    if k:
                        dve.wait_ge(s_used, n - TT + 1)
                    nc.vector.scalar_tensor_tensor(out=acc[:, tt, :], in0=gather[n % N_GATHER][:, :],
                                                   scalar=my_w[:, tt, k:k + 1], in1=acc[:, tt, :],
                                                   op0=ALU.mult, op1=ALU.add).then_inc(s_used, 1)
            dve.wait_ge(s_used, TT * TOPK)
            layer_norm_rows(dve, ln2_gt, ln2_bt, 1)

        @block.tensor
        def _(pe):
            pe.wait_ge(s_const, 2)
            pe.wait_ge(s_par, 16 * 5)
            for r in range(2):
                for c in range(4):
                    ins = pe.transpose(ps_s[1][:, r * 512 + c * N_PAR:r * 512 + (c + 1) * N_PAR],
                                       par_rows[:, (4 * r + c) * P:(4 * r + c + 1) * P], ident[0:N_PAR, 0:N_PAR])
                ins.then_inc(s_turned_par, 1)

            def turn_tokens(rows, first, seen, seen_base):
                for n in range(8):
                    if n >= 2:
                        pe.wait_ge(seen, seen_base + n - 1)
                    tt, t = n // 4, n % 4 * 4
                    for k in range(4):
                        ins = pe.transpose(turn_ring[n % 2][:, k * P:(k + 1) * P],
                                           rows[:, tt, (t + k) * P:(t + k + 1) * P], ident[:, :])
                    ins.then_inc(s_turned, 1)

            pe.wait_ge(s_x, 16)
            turn_tokens(x_rows, 0, s_xlo, 0)
            pe.wait_ge(s_xlo, 8)

            def multiply(name, i, j, u):
                pe.wait_ge(s_lo, u.n + 1)
                if not u.first_bank:
                    pe.wait_ge(s_ev[u.bank], u.bank_count)
                w = wide(name, j)
                hi, lo = tiles(w_hi, u, w), tiles(w_lo, u, w)
                ps = ps_proj[u.bank]
                if w:
                    if j == 8:
                        pe.wait_ge(s_brlo, i + 1)
                    for half in range(2):
                        n = 0
                        for t in range(CT):
                            for a, b in ((hi, branch_hi), (hi, branch_lo), (lo, branch_hi)):
                                ins = pe.matmul(ps[:, half * TOK:(half + 1) * TOK], a[:, t, half * P:(half + 1) * P],
                                                b[:, t, :], start=(n == 0), stop=(n == 3 * CT - 1))
                                n += 1
                elif name in ("v0", "v1", "out"):
                    m_hi, m_lo = (merged_hi, merged_lo) if name == "out" else (x_hi, x_lo)
                    if name == "out" and j == 0 and isinstance(i, int):
                        pe.wait_ge(s_mlo, 4)
                    for tt in range(TT):
                        n = 0
                        for t in range(KT):
                            for a, b in ((m_hi, hi), (m_hi, lo), (m_lo, hi)):
                                ins = pe.matmul(ps[:, tt * P:(tt + 1) * P], a[:, t, tt * P:(tt + 1) * P], b[:, t, :],
                                                start=(n == 0), stop=(n == 3 * KT - 1))
                                n += 1
                else:
                    n = 0
                    for t in range(KT):
                        for a, b in ((hi, x_hi), (hi, x_lo), (lo, x_hi)):
                            ins = pe.matmul(ps[:, 0:TOK], a[:, t, :], b[:, t, :], start=(n == 0), stop=(n == 3 * KT - 1))
                            n += 1
                ins.then_inc(s_mm, 1)

            def attention(half):
                def score(job):
                    n, r, kt, head = JOBS * half + job, job % 2, job % 2 + 1, job // 2
                    if n >= 2:
                        pe.wait_ge(s_masked, n - 1)
                    for g in range(N_GROUPS_ATT):
                        ins = pe.matmul(ps_s[r][:, g * kt * P:(g + 1) * kt * P],
                                        q_t[:, g, head, (kt - 1) * P:kt * P], k_t[:, g, head, 0:kt * P],
                                        start=True, stop=True)
                    ins.then_inc(s_scored, 1)

                evacuated(pe, "aval" if half == 0 else "cc")
                score(0)
                for job in range(JOBS):
                    n, r, kt, head = JOBS * half + job, job % 2, job % 2 + 1, job // 2
                    if job + 1 < JOBS:
                        score(job + 1)
                    pe.wait_ge(s_norm, n + 1)
                    if n >= 1:
                        pe.wait_ge(s_pt, n)
                        pe.wait_ge(s_att, n)
                    for m in range(3 * kt):
                        ins = pe.transpose(ps_t[:, m * P:(m + 1) * P], att_p[r][:, m * P:(m + 1) * P], ident[:, :])
                    ins.then_inc(s_pturn, 1)
                    pe.wait_ge(s_pt, n + 1)
                    for m in range(3 * kt):
                        ins = pe.matmul(ps_t[:, 768:768 + P], v_rows[:, m // kt, head, m % kt, :], p_t[:, m, :],
                                        start=(m == 0), stop=(m == 3 * kt - 1))
                    ins.then_inc(s_av, 1)

            def channel_sum(src, col):
                for c in range(CT):
                    ins = pe.matmul(ps_s[0][:, col:col + TOK], ones[:, :], src[:, c, :], start=(c == 0), stop=(c == CT - 1))
                ins.then_inc(s_asum, 1)

            def between(name):
                if name == "aval":
                    attention(0)
                if name == "cc":
                    attention(1)
                if name == "ch":
                    pe.wait_ge(s_conv, CT * TAPS_A)
                    channel_sum(branch[:, 0, :, :], 0)
                if name == "cb":
                    pe.wait_ge(s_asq, 1)
                    channel_sum(a_sq, 512)

            for s in segs:
                for j in range(s["len"]):
                    if j == 3:
                        between(s["name"])
                    multiply(s["name"], 0, j, Unit(s["base"], s["len"], 0, j))
                with pe.Fori(1, s["n"]) as i:
                    for j in range(s["len"]):
                        multiply(s["name"], i, j, Unit(s["base"], s["len"], i, j))

            pe.wait_ge(s_perm, 2)
            turn_tokens(h_perm, 8, s_ht, 0)
            pe.wait_ge(s_ht, 8)
            pe.wait_ge(s_rw, 16)
            for tt in range(TT):
                for t in range(KT):
                    ins = pe.matmul(ps_s[1][:, tt * E:(tt + 1) * E], h_t[:, t, tt * P:(tt + 1) * P], rw[:, t, :],
                                    start=(t == 0), stop=(t == KT - 1))
            ins.then_inc(s_logit, 1)
            pe.wait_ge(s_ws, 32)
            for r in range(2):
                w = ws[r][:, :].rearrange("p (t f) -> p t f", t=KT)
                for f in range(FT):
                    for t in range(KT):
                        ins = pe.matmul(ps_proj[r][:, f * TOK:(f + 1) * TOK], w[:, t, f * P:(f + 1) * P], h_t[:, t, :],
                                        start=(t == 0), stop=(t == KT - 1))
            ins.then_inc(s_shgu, 1)
            pe.wait_ge(s_chosen, 1)
            pe.wait_ge(s_tab, 5)
            count = lambda k: ps_s[1][:, 512 + k * E:512 + (k + 1) * E]
            pe.matmul(count(0), before[:, :], chosen[:, 0, :], start=True, stop=True)
            pe.matmul(count(1), ones[:, :], chosen[:, 0, :], start=True, stop=False)
            pe.matmul(count(1), before[:, :], chosen[:, 1, :], start=False, stop=True)
            pe.matmul(count(2), ones[:, :], chosen[:, 0, :], start=True, stop=False)
            pe.matmul(count(2), ones[:, :], chosen[:, 1, :], start=False, stop=True).then_inc(s_count, 1)

            def index(b):
                for tt in range(TT):
                    pe.wait_ge(s_hit, 2 * b + tt + 1)
                    for n in range(PAIRS):
                        ins = pe.matmul(ps_s[0][:, 512 * tt + 2 * n:512 * tt + 2 * n + 2],
                                        hits[:, 2 * n:2 * n + 2, :].rearrange("p a s -> p (a s)"), tok_val[:, tt, :],
                                        start=True, stop=True)
                    ins.then_inc(s_hitsum, 1)

            index(0)
            pe.wait_ge(s_shh, 1)
            pe.wait_ge(s_wsd, 16)
            pe.wait_ge(s_flag, 1)
            wd = ws[2][:, :].rearrange("p (t c) -> p t c", t=FT)
            for n in range(8):
                if n >= 2:
                    pe.wait_ge(s_shacc, n - 1)
                tt, c = n // 4, n % 4
                for f in range(FT):
                    ins = pe.matmul(down_out[n % 2][:, 0:512], sh_h[:, f, tt * P:(tt + 1) * P],
                                    wd[:, f, c * 512:(c + 1) * 512], start=(f == 0), stop=(f == FT - 1))
                ins.then_inc(s_shd, 1)
            pe.wait_ge(s_shacc, 8)

            def gate_up(k, n, turned=0):
                for r in range(2):
                    pe.wait_ge(s_w[3 * k + r], 16 * (n + 1))
                if k == 0:
                    pe.wait_ge(s_turnout, turned)
                if not (isinstance(n, int) and n == 0):
                    pe.wait_ge(s_eh, 2 * n + k - 1)
                for r in range(2):
                    w = exp_w[3 * k + r][:, :].rearrange("p (t f) -> p t f", t=KT)
                    for f in range(FT):
                        o = (r * FT + f) * SLOTS
                        for t in range(KT):
                            ins = pe.matmul(ps_proj[k][:, o:o + SLOTS], w[:, t, f * P:(f + 1) * P],
                                            xg_t[:, t, k * SLOTS:(k + 1) * SLOTS], start=(t == 0), stop=(t == KT - 1))
                ins.then_inc(s_gu, 1)

            def down(k, n):
                pe.wait_ge(s_w[3 * k + 2], 16 * (n + 1))
                pe.wait_ge(s_eh, 2 * n + k + 1)
                if not (isinstance(n, int) and n == 0):
                    pe.wait_ge(s_yt, 2 * n + k - 1)
                w = exp_w[3 * k + 2][:, :].rearrange("p (t c) -> p t c", t=FT)
                for c in range(KT):
                    for f in range(FT):
                        ins = pe.matmul(down_out[k][:, c * SLOTS:(c + 1) * SLOTS], w[:, f, c * P:(c + 1) * P],
                                        expert_h[k][:, f, :], start=(f == 0), stop=(f == FT - 1))
                ins.then_inc(s_dn, 1)

            def turn(src, t0, g):
                if not (isinstance(t0, int) and t0 + g < 2):
                    pe.wait_ge(s_turnout, t0 + g - 1)
                for k in range(4):
                    c = 4 * g + k
                    ins = pe.transpose(turn_ring[g % 2][:, k * P:(k + 1) * P], src(c), ident[:, :])
                ins.then_inc(s_turn, 1)

            def turn_out(t0, n):
                pe.wait_ge(s_yt, 2 * n + 2)
                for g in range(4):
                    turn(lambda c: y_t[:, c, :], t0, g)

            def turn_in(t0, n):
                pe.wait_ge(s_hg, 16 * (n + 1))
                for g in range(4):
                    turn(lambda c: hg[:, c * P:(c + 1) * P], t0, g)

            def whole_pass(n):
                turn_in(8 * n, n)
                gate_up(0, n, 8 * n + 4)
                gate_up(1, n)
                turn_in(8 * n + 4, n + 1)
                down(0, n)
                with pe.Fori(1, PAIRS - 1) as i:
                    m = n + i
                    gate_up(0, m, 8 * m)
                    down(1, m - 1)
                    gate_up(1, m)
                    turn_out(8 * m, m - 1)
                    turn_in(8 * m + 4, m + 1)
                    down(0, m)
                m = n + PAIRS - 1
                gate_up(0, m, 8 * m)
                down(1, m - 1)
                gate_up(1, m)
                turn_out(8 * m, m - 1)
                down(0, m)
                down(1, m)
                turn_out(8 * m + 4, m)

            whole_pass(0)
            too_many = pe.value_load(flag[0:1, 0:1], min_val=0, max_val=TOK)
            with pe.If(too_many > SLOTS):
                with pe.Fori(1, BLOCKS) as b:
                    index(b)
                    whole_pass(b * PAIRS)


_INS = ['x', 'w_in', 'conv_a_w', 'conv_a_b', 'ln_a_g', 'ln_a_b', 'conv_c_w', 'w_branch', 'w_out', 'ln1_g', 'ln1_b',
        'router_w', 'router_bias', 'w_gate', 'w_up', 'w_down', 'ws_gate', 'ws_up', 'ws_down', 'ln2_g', 'ln2_b']
_OUTS = [((1, 256, 2048), 'float32')]


def kernel(**inputs):
    import numpy as _np
    import concourse.bacc as _bacc
    from concourse import mybir as _mybir
    from concourse.bass_utils import run_bass_kernel_spmd as _run

    nc = _bacc.Bacc("TRN2", target_bir_lowering=False, num_devices=1)
    arrays, args = {}, []
    for name in _INS:
        a = _np.ascontiguousarray(inputs[name])
        arrays[f"in_{name}_dram"] = a
        args.append(nc.dram_tensor(f"in_{name}_dram", a.shape, _mybir.dt.from_np(a.dtype), kind="ExternalInput").ap())
    for i, (shape, dtype) in enumerate(_OUTS):
        dt = _mybir.dt.from_np(_np.dtype(dtype))
        args.append(nc.dram_tensor(f"out_{i}_dram", shape, dt, kind="ExternalOutput").ap())
    build(nc, *args)
    r = _run(nc, [arrays], core_ids=[0])
    got = tuple(r.results[0][f"out_{i}_dram"] for i in range(len(_OUTS)))
    return got[0]
```

```python
from contextlib import ExitStack

import concourse.bass as bass
from concourse import mybir

P = 128
F32 = mybir.dt.float32
F32R = mybir.dt.float32r
BF16 = mybir.dt.bfloat16
I32 = mybir.dt.int32
U32 = mybir.dt.uint32
ACT = mybir.ActivationFunctionType
ALU = mybir.AluOpType
AX_X = mybir.AxisListType.X
KB = 1024

N_GROUPS_ATT = 3
DILATIONS = (1, 4, 16)
SPAN = 128
N_ROUTE_GROUPS = 8
TOPK_GROUPS = 4
TOPK = 8
ROUTED_SCALE = 2.5
LN_EPS = 1e-5
NEG = -1e30
FILL = -2e38
CHOSEN = -3e38
NO_SLOT = 1000.0
NO_ROW = 4096.0
SLOTS = 64


class Unit:

    def __init__(self, base, length, i, j):
        self.n = base + length * i + j
        self.ring = j % 4
        self.bank = j % 2
        self.half = j % 2
        self.raw = (j // 2) % 2
        self.raw_count = base // 4 + (length // 4) * i + j // 4 + 1
        self.bank_count = base // 2 + (length // 2) * i + j // 2
        self.first = isinstance(i, int) and base + length * i + j < 4
        self.first_bank = isinstance(i, int) and base + length * i + j < 2


def build(nc, x, w_in, conv_a_w, conv_a_b, ln_a_g, ln_a_b, conv_c_w, w_branch, w_out, ln1_g, ln1_b,
          router_w, router_bias, w_gate, w_up, w_down, ws_gate, ws_up, ws_down, ln2_g, ln2_b, out):
    DEPTH, D, N_IN = w_in.shape
    assert DEPTH == 1
    TOK = x.shape[1]
    TT = TOK // P
    KT = D // P
    C = conv_a_w.shape[2]
    CT = C // P
    TAPS_A = conv_a_w.shape[1]
    TAPS_C = conv_c_w.shape[1]
    HEADS = CT
    ATT_W = N_GROUPS_ATT * C
    OFF_Q = 2 * C
    OFF_C = OFF_Q + 3 * ATT_W
    OFF_G = OFF_C + 3 * C
    E = w_gate.shape[1]
    F = w_gate.shape[3]
    FT = F // P
    PAIRS = E // 2
    ALPHA = float((2.0 * DEPTH) ** 0.25)
    SCALE = float(P) ** -0.5
    MASKED = NEG / SCALE
    BLOCKS = TOK // SLOTS
    MAX_JOBS = TOK * TOPK // SLOTS
    N_PAR = TAPS_A + 3 + TAPS_C
    HALF = HEADS // 2
    N_GATHER = 4
    assert TT == 2 and KT == 16 and CT == 8 and FT == 2

    ctx = ExitStack()
    with ctx:
        base0 = -(-nc.sbuf_base // 32) * 32

        def at(name, shape, dt, kb):
            return nc.alloc_sbuf_tensor_at(name, shape, dt, offset=base0 + int(kb * KB))

        def sem(name):
            return ctx.enter_context(nc.semaphore(name))

        raw = [at(f"raw{r}", [P, 4096], F32, 16 * r) for r in range(2)]
        w_hi = at("w_hi", [P, 4, 2048], F32R, 32)
        w_lo = at("w_lo", [P, 4, 2048], F32R, 64)
        x_hi = at("x_hi", [P, KT, TOK], F32R, 96)
        x_lo = at("x_lo", [P, KT, TOK], F32R, 112)
        x_rows = at("x_rows", [P, TT, D], F32, 128)
        par_rows = at("par_rows", [N_PAR, C], F32, 144)
        dist = at("dist", [P, 2 * P], I32, 148)
        dist_mod = at("dist_mod", [P, 2, 2 * P], I32, 149)
        q_k = at("q_k", [P, 2 * N_GROUPS_ATT, HALF, TOK], F32, 128)
        q_t, k_t = q_k[:, 0:N_GROUPS_ATT, :, :], q_k[:, N_GROUPS_ATT:, :, :]
        v_rows = at("v_rows", [P, N_GROUPS_ATT, HALF, TT, P], F32, 152)
        merged = at("merged", [P, KT, TOK], F32, 128)
        branch_hi = at("branch_hi", [P, CT, TOK], F32R, 144)
        branch_lo = at("branch_lo", [P, CT, TOK], F32R, 152)
        a_mean = at("a_mean", [P, TOK], F32, 160)
        a_rstd = at("a_rstd", [P, TOK], F32, 161)
        branch = at("branch", [P, 3, CT, TOK], F32, 164)
        att_p = [at(f"att_p{r}", [P, N_GROUPS_ATT * 2 * P], F32, 180 + 3 * r) for r in range(2)]
        a_pad = at("a_pad", [P, CT, TAPS_A - 1 + TOK], F32, 188)
        c_pad = at("c_pad", [P, CT, TAPS_C - 1 + TOK], F32, 188)
        gated = [at(f"gated{r}", [P, 2, TOK], F32, 188 + 2 * r) for r in range(2)]
        p_t = at("p_t", [P, 2 * N_GROUPS_ATT, P], F32, 197)
        mask = at("mask", [P, N_GROUPS_ATT, 2, P], F32, 200)
        a_sig = [at(f"a_sig{r}", [P, TOK], F32, 203 + r) for r in range(2)]
        a_sq = at("a_sq", [P, CT, TOK], F32, 197)
        gates = at("gates", [P, CT, TOK], F32, 197)
        zeros = at("zeros", [P, 512], F32, 186)
        par = at("par", [P, CT, N_PAR], F32, 205)
        ident = at("ident", [P, P], F32, 206.25)
        ones = at("ones", [P, P], F32, 206.75)
        tiny = at("tiny", [P, 64], F32, 207.25)
        idx_now = at("idx_now", [P, 1], U32, 207.53125)
        job_idx = at("job_idx", [P, 1], U32, 207.5625)
        jobs = at("jobs", [P, 1], I32, 207.59375)
        neg_max = [tiny[:, r:r + 1] for r in range(2)]
        row_max = [tiny[:, 2 + r:3 + r] for r in range(2)]
        row_sum = [tiny[:, 4 + r:5 + r] for r in range(2)]
        row_rcp = [tiny[:, 6 + r:7 + r] for r in range(2)]
        mean_var = tiny[:, 8:12].rearrange("p (a b) -> p a b", a=2)
        var_eps = tiny[:, 12:14]
        std = tiny[:, 14:16]
        rstd = tiny[:, 16:18]
        w_sum = tiny[:, 18:20]
        w_rcp = tiny[:, 20:22]
        job_free = tiny[:, 22:23]
        merged_hi = at("merged_hi", [P, KT, TOK], F32R, 96)
        merged_lo = at("merged_lo", [P, KT, TOK], F32R, 112)
        acc = at("acc", [P, TT, D], F32, 144)
        ln_g = at("ln_g", [P, D], F32, 128)
        ln_b = at("ln_b", [P, D], F32, 136)
        exp_w = [at(f"exp_w{r}", [P, 4096], F32, kb) for r, kb in enumerate((160, 176, 0, 16, 32, 48))]
        h_perm = at("h_perm", [P, TT, D], F32, 48)
        ws = [at(f"ws{r}", [P, 4096], F32, 64 + 16 * r) for r in range(3)]
        y_t = at("y_t", [P, KT, 2 * SLOTS], F32, 64)
        y_rows = at("y_rows", [P, D], F32, 72)
        ln2_gt = at("ln2_gt", [P, D], F32, 80)
        ln2_bt = at("ln2_bt", [P, D], F32, 88)
        match = at("match", [P, TOPK, E], F32, 104)
        job_table = at("job_table", [P, MAX_JOBS, E], F32, 96)
        extra = at("extra", [P, E], F32, 106)
        job_ends = at("job_ends", [P, E], F32, 106.25)
        over_row = at("over_row", [P, E], F32, 106.5)
        job_n = at("job_n", [P, 2, MAX_JOBS], F32, 106.75)
        job_hits = at("job_hits", [P, TT, 2, SLOTS], BF16, 107)
        h_t = at("h_t", [P, KT, TOK], F32, 112)
        hits = at("hits", [P, E, SLOTS], BF16, 128)
        xg_t = at("xg_t", [P, KT, 2 * SLOTS], F32, 128)
        hg = at("hg", [P, D], F32, 136)
        gather = [at(f"gather{r}", [P, D], F32, 8 * r) for r in range(N_GATHER)]
        choice = at("choice", [P, TT, E], F32, 192)
        scores = at("scores", [P, TT, E], F32, 192.5)
        chosen = at("chosen", [P, TT, E], F32, 193)
        slot_of = at("slot_of", [P, TT, E], F32, 193.5)
        weight = at("weight", [P, TT, E], F32, 194)
        row_of = at("row_of", [P, TT, E], F32, 194.5)
        iota_slot = at("iota_slot", [P, TOK], F32, 195)
        row_base = at("row_base", [P, E], F32, 196)
        bias_b = at("bias_b", [P, E], F32, 196.25)
        top_in_group = at("top_in_group", [P, TT, N_ROUTE_GROUPS, 8], F32, 196.5)
        groups = at("groups", [P, TT, 16], F32, 197)
        groups_left = at("groups_left", [P, TT, 16], F32, 197.125)
        best_groups = at("best_groups", [P, TT, 8], F32, 197.25)
        group_in = at("group_in", [P, TT, 8], F32, 197.3125)
        group_out = at("group_out", [P, TT, 8], F32, 197.375)
        best = at("best", [P, TT, 8], F32, 197.4375)
        masked = at("masked", [P, TT, E], F32, 197.5)
        left = at("left", [P, TT, E], F32, 194.5)
        expert_sig = [at(f"expert_sig{r}", [P, FT, SLOTS], F32, 198.5 + 0.5 * r) for r in range(2)]
        expert_h = [at(f"expert_h{r}", [P, FT, SLOTS], F32, 199.5 + 0.5 * r) for r in range(2)]
        sh_sig = at("sh_sig", [P, FT, TOK], F32, 200.5)
        sh_h = at("sh_h", [P, FT, TOK], F32, 202.5)
        job_expert = at("job_expert", [P, MAX_JOBS], I32, 198.25)
        job_first = at("job_first", [P, MAX_JOBS], I32, 198.375)
        count_of = at("count_of", [P, E], F32, 196.5)
        tok_idx = at("tok_idx", [P, PAIRS], U32, 204.5)
        stats = at("stats", [P, TT, 4, 6], F32, 204.625)
        tok_val = at("tok_val", [P, TT, 2], BF16, 204.8125)
        before = at("before", [P, P], F32, 205)
        hit_sum = [at(f"hit_sum{r}", [P, PAIRS, 2], F32, 205.5 + 0.25 * r) for r in range(2)]
        my_row = at("my_row", [P, TT, TOPK], F32, 206)
        my_idx = at("my_idx", [P, TT, TOPK], U32, 206.0625)
        my_w = at("my_w", [P, TT, TOPK], F32, 206.125)
        rw = at("rw", [P, KT, E], F32, 100)

        ps_proj = [nc.alloc_psum_tensor(f"ps_proj{r}", [P, 512], F32) for r in range(2)]
        ps_s = [nc.alloc_psum_tensor(f"ps_s{r}", [P, 1024], F32) for r in range(2)]
        ps_t = nc.alloc_psum_tensor("ps_t", [P, 1024], F32)
        turn_ring = [ps_s[0][:, 0:512], ps_s[0][:, 512:1024]]
        down_out = [ps_s[1], ps_t]

        h_dram = nc.dram_tensor("h_perm_dram", (TOK, D), F32, kind="Internal").ap()
        y_dram = nc.dram_tensor("y_dram", ((E + MAX_JOBS) * SLOTS, D), F32, kind="Internal").ap()
        x2 = x[0]
        out2 = out[0]
        w_in_v = w_in[0].rearrange("(t p) c -> p t c", p=P)
        w_branch_v = w_branch[0].rearrange("n (t p) c -> p (n t) c", p=P)
        w_out_v = w_out[0].rearrange("(t p) c -> p t c", p=P)
        gate_v = w_gate[0].rearrange("e (p t) f -> e p (t f)", p=P)
        up_v = w_up[0].rearrange("e (p t) f -> e p (t f)", p=P)
        down_v = w_down[0].rearrange("e (t p) c -> e p t c", p=P)

        s_x, s_par, s_const, s_residue, s_turned, s_xhi, s_xlo = map(sem, (
            "s_x", "s_par", "s_const", "s_residue", "s_turned", "s_xhi", "s_xlo"))
        s_raw = [sem(f"s_raw{r}") for r in range(2)]
        s_hi, s_lo, s_mm = map(sem, ("s_hi", "s_lo", "s_mm"))
        s_ev = [sem(f"s_ev{r}") for r in range(2)]
        s_scored, s_masked, s_exp, s_norm, s_pturn, s_pt, s_av, s_att = map(sem, (
            "s_scored", "s_masked", "s_exp", "s_norm", "s_pturn", "s_pt", "s_av", "s_att"))
        s_asig, s_glu, s_conv, s_asum, s_acent, s_asq, s_avar, s_astd, s_anorm, s_aout = map(sem, (
            "s_asig", "s_glu", "s_conv", "s_asum", "s_acent", "s_asq", "s_avar", "s_astd", "s_anorm", "s_aout"))
        s_ctap, s_gated, s_added, s_brhi, s_brlo, s_mhi, s_mlo = map(sem, (
            "s_ctap", "s_gated", "s_added", "s_brhi", "s_brlo", "s_mhi", "s_mlo"))
        s_xr, s_lnp, s_var, s_std, s_scaled, s_ln = map(sem, (
            "s_xr", "s_lnp", "s_var", "s_std", "s_scaled", "s_ln"))
        s_perm, s_hdram, s_ht, s_rw, s_ws, s_logit, s_score, s_chosen, s_count, s_counted = map(sem, (
            "s_perm", "s_hdram", "s_ht", "s_rw", "s_ws", "s_logit", "s_score", "s_chosen", "s_count", "s_counted"))
        s_shgu, s_shsig, s_shh, s_shd, s_shacc, s_tab, s_bias = map(sem, (
            "s_shgu", "s_shsig", "s_shh", "s_shd", "s_shacc", "s_tab", "s_bias"))
        s_hit, s_hitsum, s_idx, s_idxnow, s_hg, s_turn, s_turnout = map(sem, (
            "s_hit", "s_hitsum", "s_idx", "s_idxnow", "s_hg", "s_turn", "s_turnout"))
        s_w = [sem(f"s_w{r}") for r in range(6)]
        s_gu, s_sig, s_eh, s_dn, s_yt, s_yw, s_mine, s_ln2p, s_done = map(sem, (
            "s_gu", "s_sig", "s_eh", "s_dn", "s_yt", "s_yw", "s_mine", "s_ln2p", "s_done"))
        s_got = [sem(f"s_got{r}") for r in range(N_GATHER)]
        s_fetch, s_used, s_hgzero, s_turned_par, s_par_t, s_wsd = map(sem, (
            "s_fetch", "s_used", "s_hgzero", "s_turned_par", "s_par_t", "s_wsd"))
        s_jobs, s_jobhit, s_jobsum, s_jobidx = map(sem, ("s_jobs", "s_jobhit", "s_jobsum", "s_jobidx"))
        s_pool, s_dve, s_zeros, s_cleared = map(sem, ("s_pool", "s_dve", "s_zeros", "s_cleared"))

        def seg(name, n, length, base):
            return {"name": name, "n": n, "len": length, "base": base}

        segs, units = [], 0
        for name, n, length in (("qk0", 6, 4), ("v0", 3, 4), ("aval", CT // 4, 4), ("agate", CT // 4, 4),
                                ("qk1", 6, 4), ("v1", 3, 4), ("cc", CT // 4, 4), ("ch", CT // 4, 4),
                                ("cb", CT // 4, 4), ("gb", 6, 12), ("out", KT // 4, 4)):
            segs.append(seg(name, n, length, units))
            units += n * length
        at_seg = {s["name"]: s for s in segs}
        BASE_OUT = at_seg["out"]["base"]

        def chunk(name, i, c):
            if name in ("qk0", "v0", "qk1", "v1"):
                first = {"qk": 0, "v0": 6, "v1": 6}[name if name in ("v0", "v1") else "qk"]
                col = OFF_Q + first * C + i * C + int(name[-1]) * (C // 2) + c * 256
            elif name == "aval":
                col = i * 512 + c * 256
            elif name == "agate":
                col = C + i * 512 + c * 256
            elif name in ("cb", "cc", "ch"):
                col = OFF_C + ("cb", "cc", "ch").index(name) * C + i * 512 + c * 256
            elif name == "gb" and c < 4:
                col = OFF_G + i * (D // 2) + c * 256
            elif name == "gb":
                return w_branch_v[:, bass.ds((i // 2) * CT, CT), bass.ds((i % 2) * (D // 2) + (c - 4) * 512, 512)]
            else:
                return w_out_v[:, :, bass.ds(i * 512 + c * 256, 256)]
            return w_in_v[:, :, bass.ds(col, 256)]

        def wide(name, j):
            return name == "gb" and j >= 8

        def raw_half(u, w):
            if w:
                return raw[u.raw][:, :].rearrange("p (t c) -> p t c", t=CT)[:, :, u.half * 256:u.half * 256 + 256]
            return raw[u.raw][:, :].rearrange("p (t c) -> p t c", t=KT)[:, :, u.half * P:u.half * P + P]

        def tiles(ring, u, w):
            return ring[:, u.ring, :].rearrange("p (t c) -> p t c", t=CT if w else KT)

        def by_pair(name):
            return name in ("v0", "v1", "out")

        def pair_out(j):
            if j // 2 == 0:
                return ps_s[0][:, 512 * (j % 2):512 * (j % 2) + 2 * P]
            return ps_proj[j % 2][:, 0:2 * P]

        def stream(eng, per_unit, evacuate, after=lambda name, i, j: None):
            prev = None
            for s in segs:
                def body(i, s=s, prev=prev):
                    for j in range(s["len"]):
                        u = Unit(s["base"], s["len"], i, j)
                        per_unit(s["name"], i, j, u)
                        if j >= 3:
                            evacuate(s["name"], i, j - 3, Unit(s["base"], s["len"], i, j - 3))
                        elif not (isinstance(i, int) and i == 0):
                            jj = s["len"] + j - 3
                            evacuate(s["name"], i - 1, jj, Unit(s["base"], s["len"], i - 1, jj))
                        elif prev is not None:
                            jj = prev["len"] + j - 3
                            evacuate(prev["name"], prev["n"] - 1, jj, Unit(prev["base"], prev["len"], prev["n"] - 1, jj))
                        after(s["name"], i, j)
                body(0)
                with eng.Fori(1, s["n"]) as i:
                    body(i)
                prev = s
            for j in range(prev["len"] - 3, prev["len"]):
                evacuate(prev["name"], prev["n"] - 1, j, Unit(prev["base"], prev["len"], prev["n"] - 1, j))

        JOBS = 2 * HALF

        def evacuated(eng, name):
            for r in range(2):
                eng.wait_ge(s_ev[r], at_seg[name]["base"] // 2)

        def layer_norm_rows(eng, g, b, n):
            for tt in range(TT):
                for c in range(4):
                    nc.vector.bn_stats(stats[:, tt, c, :], acc[:, tt, c * 512:(c + 1) * 512]).then_inc(s_dve, 1)
            eng.wait_ge(s_dve, dve_done(8))
            for tt in range(TT):
                nc.vector.bn_aggr(mean_var[:, tt, :], stats[:, tt, :, :]).then_inc(s_dve, 1)
            eng.wait_ge(s_dve, dve_done(2))
            nc.vector.tensor_scalar(var_eps, mean_var[:, :, 1], LN_EPS, None, ALU.add).then_inc(s_var, 1)
            eng.wait_ge(s_std, n + 1)
            nc.vector.reciprocal(rstd, std).then_inc(s_dve, 1)
            eng.wait_ge(s_dve, dve_done(1))
            for tt in range(TT):
                nc.vector.tensor_scalar(acc[:, tt, :], acc[:, tt, :], mean_var[:, tt, 0:1], rstd[:, tt:tt + 1],
                                        ALU.subtract, ALU.mult).then_inc(s_dve, 1)
                eng.wait_ge(s_dve, dve_done(1))
                if tt == 0:
                    eng.wait_ge(s_ln2p if n else s_lnp, 32)
                nc.vector.tensor_tensor(acc[:, tt, :], acc[:, tt, :], g[:, :], ALU.mult).then_inc(s_scaled, 1)

        counted = {"dve": 0, "pool": 0}

        def dve_done(k):
            counted["dve"] += k
            return counted["dve"]

        def pool_done(k):
            counted["pool"] += k
            return counted["pool"]

        block = ctx.enter_context(nc.Block())

        @block.sync
        def _(sp):
            for s in segs:
                def body(i, s=s):
                    for c in range(s["len"] // 2):
                        u = Unit(s["base"], s["len"], i, 2 * c)
                        if not u.first:
                            sp.wait_ge(s_lo, u.n - 2)
                        if s["name"] == "gb" and c >= 4:
                            dst = raw[u.raw][:, :].rearrange("p (t c) -> p t c", t=CT)
                        else:
                            dst = raw[u.raw][:, :].rearrange("p (t c) -> p t c", t=KT)
                        sp.dma_start(dst, chunk(s["name"], i, c)).then_inc(s_raw[u.raw], 16)
                body(0)
                with sp.Fori(1, s["n"]) as i:
                    body(i)

            sp.wait_ge(s_added, 24)
            sp.dma_start(exp_w[0][:, :], gate_v[0]).then_inc(s_w[0], 16)
            sp.dma_start(exp_w[1][:, :], up_v[0]).then_inc(s_w[1], 16)
            sp.wait_ge(s_mm, units)
            for r, v in enumerate((ws_gate, ws_up)):
                sp.dma_start(ws[r][:, :], v[0].rearrange("(p t) f -> p (t f)", p=P)).then_inc(s_ws, 16)
            sp.dma_start(exp_w[3][:, :], gate_v[1]).then_inc(s_w[3], 16)
            sp.dma_start(exp_w[4][:, :], up_v[1]).then_inc(s_w[4], 16)
            sp.dma_start(exp_w[2][:, :].rearrange("p (t c) -> p t c", t=FT), down_v[0]).then_inc(s_w[2], 16)
            sp.wait_ge(s_logit, 1)
            sp.dma_start(ws[2][:, :].rearrange("p (t c) -> p t c", t=FT),
                         ws_down[0].rearrange("(t p) c -> p t c", p=P)).then_inc(s_wsd, 16)

            def load_down(slot, e):
                return sp.dma_start(exp_w[slot][:, :].rearrange("p (t c) -> p t c", t=FT),
                                    down_v[bass.ds(e, 1)].rearrange("e p t c -> p (e t) c")).then_inc(s_w[slot], 16)

            def load_gate_up(slot, e):
                sp.dma_start(exp_w[slot][:, :], gate_v[bass.ds(e, 1)].rearrange("e p m -> (e p) m")).then_inc(s_w[slot], 16)
                sp.dma_start(exp_w[slot + 1][:, :], up_v[bass.ds(e, 1)].rearrange("e p m -> (e p) m")).then_inc(s_w[slot + 1], 16)

            def experts(i, n):
                sp.wait_ge(s_gu, 2 * n - 1)
                load_gate_up(0, 2 * i)
                if isinstance(n, int) and n == 1:
                    sp.wait_ge(s_hdram, 32)
                    sp.wait_ge(s_ht, 8)
                else:
                    sp.wait_ge(s_dn, 2 * n - 2)
                load_down(5, 2 * i - 1)
                sp.wait_ge(s_gu, 2 * n)
                load_gate_up(3, 2 * i + 1)
                sp.wait_ge(s_dn, 2 * n - 1)
                load_down(2, 2 * i)

            experts(1, 1)
            with sp.Fori(2, PAIRS) as i:
                experts(i, i)
            sp.wait_ge(s_dn, 2 * PAIRS - 2)
            load_down(5, E - 1)
            sp.wait_ge(s_jobs, 1)
            n_jobs = sp.value_load(jobs[0:1, 0:1], min_val=0, max_val=MAX_JOBS)
            with sp.Fori(0, MAX_JOBS // 2) as i:
                with sp.If(n_jobs > 2 * i):
                    n = PAIRS + i
                    first = sp.value_load(job_expert[0:1, bass.ds(2 * i, 1)], min_val=0, max_val=E - 1)
                    second = sp.value_load(job_expert[0:1, bass.ds(2 * i + 1, 1)], min_val=0, max_val=E - 1)
                    sp.wait_ge(s_gu, 2 * n - 1)
                    load_gate_up(0, first)
                    sp.wait_ge(s_gu, 2 * n)
                    load_gate_up(3, second)
                    sp.wait_ge(s_dn, 2 * n - 1)
                    load_down(2, first)
                    sp.wait_ge(s_dn, 2 * n)
                    load_down(5, second)
            sp.wait_ge(s_ln, 4)
            for tt in range(TT):
                sp.dma_start(out2[tt * P:(tt + 1) * P, :], acc[:, tt, :]).then_inc(s_done, 16)
            sp.wait_ge(s_done, 32)

        @block.gpsimd
        def _(pool):
            pool.memset(ident[:, :], 0.0).then_inc(s_pool, 1)
            pool.memset(ones[:, :], 1.0).then_inc(s_const, 1)
            pool.wait_ge(s_pool, pool_done(1))
            pool.affine_select(out=ident[:, :], in_=ident[:, :], compare_op=ALU.not_equal, fill=1.0, base=0,
                               pattern=[[-1, P]], channel_multiplier=1).then_inc(s_const, 1)
            pool.iota(dist[:, :], pattern=[[-1, 2 * P]], base=P, channel_multiplier=1).then_inc(s_const, 1)
            pool.memset(a_pad[:, :, 0:TAPS_A - 1], 0.0).then_inc(s_const, 1)
            pool.wait_ge(s_residue, 3)
            for g in range(N_GROUPS_ATT):
                m = mask[:, g, :, :].rearrange("p a b -> p (a b)")
                pool.affine_select(out=m, in_=m, compare_op=ALU.is_ge, fill=MASKED, base=P,
                                   pattern=[[-1, 2 * P]], channel_multiplier=1).then_inc(s_pool, 1)
            pool.wait_ge(s_pool, pool_done(3))
            m = mask[:, 0, :, :].rearrange("p a b -> p (a b)")
            pool.affine_select(out=m, in_=m, compare_op=ALU.is_ge, fill=MASKED, base=0,
                               pattern=[[1, 2 * P]], channel_multiplier=-1).then_inc(s_const, 1)

            pool.memset(zeros[:, :], 0.0).then_inc(s_zeros, 1)
            pool.wait_ge(s_zeros, 1)
            for n in range(MAX_JOBS // 2):
                pool.wait_ge(s_mm, 2 * n + 1)
                row = E * SLOTS + n * P
                pool.dma_start(y_dram[row:row + P, :].rearrange("p (b c) -> p b c", c=512),
                               zeros[:, :].unsqueeze(1).to_broadcast([P, D // 512, 512])).then_inc(s_cleared, 16)

            for j in range(CT):
                pool.wait_ge(s_asig, j + 1)
                row = a_pad[:, j, TAPS_A - 1:]
                pool.tensor_tensor(row, row, a_sig[j % 2][:, :], ALU.mult).then_inc(s_glu, 1)

            pool.wait_ge(s_conv, CT * TAPS_A)
            pool.memset(c_pad[:, :, 0:TAPS_C - 1], 0.0).then_inc(s_const, 1)
            pool.wait_ge(s_att, 2 * JOBS)
            pool.memset(merged[:, :, :], 0.0).then_inc(s_pool, 1)
            pool.wait_ge(s_pool, pool_done(1))

            def add_branch(i, k):
                w = 4 * i + k
                pool.wait_ge(s_gated, w + 1)
                if not (isinstance(w, int) and w == 0):
                    pool.wait_ge(s_added, w)
                m = merged[:, bass.ds((i % 2) * CT + 2 * k, 2), :]
                pool.tensor_tensor(m, m, gated[k % 2][:, :, :], ALU.add).then_inc(s_added, 1)

            for k in range(4):
                add_branch(0, k)
            with pool.Fori(1, 6) as i:
                for k in range(4):
                    add_branch(i, k)

            pool.wait_ge(s_mm, BASE_OUT)
            pool.dma_start(acc[:, :, :], x2.rearrange("(a p) c -> p a c", p=P)).then_inc(s_xr, 16)
            pool.wait_ge(s_mlo, 4)
            pool.dma_start(ln_g[:, :], ln1_g.to_broadcast([P, D])).then_inc(s_lnp, 16)
            pool.dma_start(ln_b[:, :], ln1_b.to_broadcast([P, D])).then_inc(s_lnp, 16)
            pool.dma_start(bias_b[:, :], router_bias.to_broadcast([P, E])).then_inc(s_bias, 16)
            pool.iota(iota_slot[:, :], pattern=[[1, TOK]], base=0, channel_multiplier=0,
                      allow_small_or_imprecise_dtypes=True).then_inc(s_tab, 1)
            pool.iota(row_base[:, :], pattern=[[SLOTS, E]], base=1, channel_multiplier=0,
                      allow_small_or_imprecise_dtypes=True).then_inc(s_tab, 1)
            pool.iota(tok_val[:, :, 0], pattern=[[P, TT]], base=0, channel_multiplier=1,
                      allow_small_or_imprecise_dtypes=True).then_inc(s_tab, 1)
            pool.memset(tok_val[:, :, 1], 1.0).then_inc(s_tab, 1)
            pool.memset(before[:, :], 1.0).then_inc(s_pool, 1)
            pool.wait_ge(s_pool, pool_done(1))
            pool.affine_select(out=before[:, :], in_=before[:, :], compare_op=ALU.is_ge, fill=0.0, base=-1,
                               pattern=[[1, P]], channel_multiplier=-1).then_inc(s_tab, 1)

            def add_shift(b, n):
                for tt in range(TT):
                    pool.wait_ge(s_scaled, 2 * n + tt + 1)
                    pool.tensor_tensor(acc[:, tt, :], acc[:, tt, :], b[:, :], ALU.add).then_inc(s_ln, 1)

            add_shift(ln_b, 0)
            pool.wait_ge(s_ln, 2)
            pool.memset(hg[:, :], 0.0).then_inc(s_hgzero, 1)
            for tt in range(TT):
                pool.wait_ge(s_perm, tt + 1)
                pool.dma_start(h_dram[tt * P:(tt + 1) * P, :], h_perm[:, tt, :]).then_inc(s_hdram, 16)
            pool.wait_ge(s_hdram, 32)
            pool.wait_ge(s_hgzero, 1)

            def fetch(i, n):
                pool.sem_inc(s_fetch, 1)
                pool.tensor_copy(idx_now[:, :], tok_idx[:, bass.ds(i, 1)]).then_inc(s_idxnow, 1)
                pool.wait_ge(s_idxnow, n + 1)
                pool.sem_inc(s_fetch, 1)
                pool.indirect_dma_start(out=hg[:, :], out_offset=None, in_=h_dram[:, :],
                                        in_offset=bass.IndirectOffsetOnAxis(ap=idx_now[:, 0:1], axis=0),
                                        bounds_check=TOK - 1, oob_is_err=False).then_inc(s_hg, 16)

            def keep(n):
                pool.dma_start(y_dram[bass.ds(n * P, P), :], y_rows[:, :]).then_inc(s_yw, 16)

            def experts(i, n):
                pool.wait_ge(s_turnout, 8 * n + 4)
                keep(n - 1)
                pool.wait_ge(s_turn, 8 * n + 8)
                fetch(i + 2, n + 2)

            def last_two(n):
                pool.wait_ge(s_turnout, 8 * n + 4)
                keep(n - 1)
                pool.wait_ge(s_turnout, 8 * n + 12)
                keep(n)
                pool.wait_ge(s_turnout, 8 * n + 16)
                keep(n + 1)

            pool.wait_ge(s_idx, 4)
            fetch(0, 0)
            pool.wait_ge(s_turn, 4)
            fetch(1, 1)
            pool.wait_ge(s_turn, 8)
            fetch(2, 2)
            pool.wait_ge(s_shgu, 1)
            pool.dma_start(ln2_gt[:, :], ln2_g.to_broadcast([P, D])).then_inc(s_ln2p, 16)
            pool.dma_start(ln2_bt[:, :], ln2_b.to_broadcast([P, D])).then_inc(s_ln2p, 16)
            with pool.Fori(1, PAIRS - 2) as i:
                experts(i, i)
            last_two(PAIRS - 2)
            pool.wait_ge(s_jobs, 1)
            n_jobs = pool.value_load(jobs[0:1, 0:1], min_val=0, max_val=MAX_JOBS)
            pool.wait_ge(s_cleared, 16 * (MAX_JOBS // 2))
            with pool.Fori(0, MAX_JOBS // 2) as i:
                with pool.If(n_jobs > 2 * i):
                    n = PAIRS + i
                    pool.wait_ge(s_jobidx, 2 * i + 2)
                    pool.sem_inc(s_fetch, 1)
                    pool.indirect_dma_start(out=hg[:, :], out_offset=None, in_=h_dram[:, :],
                                            in_offset=bass.IndirectOffsetOnAxis(ap=job_idx[:, 0:1], axis=0),
                                            bounds_check=TOK - 1, oob_is_err=False).then_inc(s_hg, 16)
                    pool.wait_ge(s_turnout, 8 * n + 8)
                    keep(n)
                    pool.wait_ge(s_yw, 16 * (n + 1))
            pool.wait_ge(s_yw, 16 * PAIRS)
            pool.wait_ge(s_mine, 1)
            for k in range(TOPK):
                for tt in range(TT):
                    n = TT * k + tt
                    if n >= N_GATHER:
                        pool.wait_ge(s_used, n - N_GATHER + 1)
                    pool.indirect_dma_start(out=gather[n % N_GATHER][:, :], out_offset=None, in_=y_dram[:, :],
                                            in_offset=bass.IndirectOffsetOnAxis(ap=my_idx[:, tt, k:k + 1], axis=0),
                                            bounds_check=(E + MAX_JOBS) * SLOTS - 1,
                                            oob_is_err=False).then_inc(s_got[n % N_GATHER], 16)
            add_shift(ln2_bt, 1)

        @block.scalar
        def _(act):
            act.dma_start(x_rows[:, :, :], x2.rearrange("(a p) c -> p a c", p=P)).then_inc(s_x, 16)
            row = 0
            for v, k in ((conv_a_w[0], TAPS_A), (conv_a_b, 1), (ln_a_g, 1), (ln_a_b, 1), (conv_c_w[0], TAPS_C)):
                act.dma_start(par_rows[row:row + k, :], v).then_inc(s_par, 16)
                row += k
            for n in range(8):
                act.wait_ge(s_turned, n + 1)
                tt, t = n // 4, n % 4 * 4
                nc.scalar.activation(x_hi[:, t:t + 4, tt * P:(tt + 1) * P],
                                     turn_ring[n % 2].rearrange("p (t c) -> p t c", t=4), ACT.Copy).then_inc(s_xhi, 1)

            def split(name, i, j, u):
                if u.half == 0:
                    act.wait_ge(s_raw[u.raw], 16 * u.raw_count)
                if not u.first:
                    act.wait_ge(s_mm, u.n - 3)
                w = wide(name, j)
                nc.scalar.activation(tiles(w_hi, u, w), raw_half(u, w), ACT.Copy).then_inc(s_hi, 1)

            def evacuate(name, i, j, u):
                if name in ("ch", "cb", "out") or wide(name, j):
                    return
                act.wait_ge(s_mm, u.n + 1)
                ps = ps_proj[u.bank][:, 0:TOK]
                if name in ("qk0", "qk1"):
                    both = q_k[:, bass.ds(i, 1), j, :]
                    ins = nc.scalar.activation(both.rearrange("p a c -> p (a c)"), ps, ACT.Copy)
                elif name in ("v0", "v1"):
                    m = j // 2 * 2
                    dst = v_rows[:, bass.ds(i, 1), m:m + 2, j % 2, :].rearrange("p a h c -> p (a h) c")
                    ins = nc.scalar.activation(dst, pair_out(j).rearrange("p (h c) -> p h c", h=2), ACT.Copy)
                elif name == "aval":
                    dst = a_pad[:, bass.ds(4 * i + j, 1), TAPS_A - 1:].rearrange("p a c -> p (a c)")
                    if j == 0 and isinstance(i, int):
                        act.wait_ge(s_const, 4)
                    ins = nc.scalar.activation(dst, ps, ACT.Copy)
                elif name == "agate":
                    n = 4 * i + j
                    if not (isinstance(n, int) and n < 2):
                        act.wait_ge(s_glu, n - 1)
                    ins = nc.scalar.activation(a_sig[j % 2][:, :], ps, ACT.Sigmoid)
                    ins.then_inc(s_asig, 1)
                    act.wait_ge(s_asig, n + 1)
                    act.sem_inc(s_ev[u.bank], 1)
                    return
                elif name == "cc":
                    if j == 0 and isinstance(i, int):
                        act.wait_ge(s_const, 6)
                    dst = c_pad[:, bass.ds(4 * i + j, 1), TAPS_C - 1:].rearrange("p a c -> p (a c)")
                    ins = nc.scalar.activation(dst, ps, ACT.Copy)
                else:
                    if j == 0 and not (isinstance(i, int) and i == 0):
                        act.wait_ge(s_gated, 4 * i)
                    elif j == 0:
                        act.wait_ge(s_aout, CT)
                    ins = nc.scalar.activation(gates[:, j, :], ps, ACT.Sigmoid)
                ins.then_inc(s_ev[u.bank], 1)

            def attention(half):
                def exps(job):
                    r, w = job % 2, N_GROUPS_ATT * P * (job % 2 + 1)
                    n = JOBS * half + job
                    act.wait_ge(s_masked, n + 1)
                    nc.scalar.activation(att_p[r][:, 0:w], att_p[r][:, 0:w], ACT.Exp, bias=neg_max[r],
                                         accum_out=row_sum[r]).then_inc(s_exp, 1)

                exps(0)
                for job in range(JOBS):
                    n = JOBS * half + job
                    kt = job % 2 + 1
                    if job + 1 < JOBS:
                        exps(job + 1)
                    act.wait_ge(s_pturn, n + 1)
                    if n >= 1:
                        act.wait_ge(s_av, n)
                    nc.scalar.activation(p_t[:, 0:3 * kt, :],
                                         ps_t[:, 0:3 * kt * P].rearrange("p (a b) -> p a b", b=P),
                                         ACT.Copy).then_inc(s_pt, 1)
                    act.wait_ge(s_av, n + 1)
                    nc.scalar.activation(branch[:, 1, HALF * half + job // 2, (job % 2) * P:(job % 2 + 1) * P],
                                         ps_t[:, 768:768 + P], ACT.Copy).then_inc(s_att, 1)

            def after(name, i, j):
                first = isinstance(i, int) and i == 0
                last = j == 3
                if first and last and name == "aval":
                    attention(0)
                if first and last and name == "cc":
                    attention(1)
                if first and last and name == "ch":
                    act.wait_ge(s_acent, 1)
                    nc.scalar.activation(a_sq[:, :, :], branch[:, 0, :, :], ACT.Square).then_inc(s_asq, 1)
                if first and last and name == "cb":
                    act.wait_ge(s_avar, 1)
                    nc.scalar.activation(a_rstd[:, :], a_mean[:, :], ACT.Sqrt).then_inc(s_astd, 1)
                    act.wait_ge(s_anorm, 1)
                    for c in range(CT):
                        nc.scalar.activation(branch[:, 0, c, :], branch[:, 0, c, :], ACT.Silu,
                                             scale=par[:, c, TAPS_A + 1:TAPS_A + 2],
                                             bias=par[:, c, TAPS_A + 2:TAPS_A + 3]).then_inc(s_aout, 1)
                if name == "gb" and j == 6:
                    if first:
                        act.wait_ge(s_aout, CT)
                        evacuated(act, "gb")
                    nc.scalar.activation(branch_hi[:, :, :],
                                         branch[:, bass.ds(i // 2, 1), :, :].rearrange("p n t c -> p (n t) c"),
                                         ACT.Copy).then_inc(s_brhi, 1)
                if name == "out" and first and j == 2:
                    act.wait_ge(s_added, 24)
                    for c in range(4):
                        nc.scalar.activation(merged_hi[:, 4 * c:4 * c + 4, :], merged[:, 4 * c:4 * c + 4, :],
                                             ACT.Copy).then_inc(s_mhi, 1)

            stream(act, split, evacuate, after)

            act.wait_ge(s_var, 1)
            nc.scalar.activation(std, var_eps, ACT.Sqrt).then_inc(s_std, 1)
            act.wait_ge(s_mm, units)
            act.dma_start(rw[:, :, :], router_w[0].rearrange("(p t) e -> p t e", p=P)).then_inc(s_rw, 16)
            for tt in range(TT):
                act.wait_ge(s_ln, tt + 1)
                nc.scalar.activation(h_perm[:, tt, :].rearrange("p (t q) -> p t q", t=KT),
                                     acc[:, tt, :].rearrange("p (q t) -> p t q", t=KT), ACT.Copy).then_inc(s_perm, 1)
            for n in range(8):
                act.wait_ge(s_turned, 8 + n + 1)
                tt, t = n // 4, n % 4 * 4
                nc.scalar.activation(h_t[:, t:t + 4, tt * P:(tt + 1) * P],
                                     turn_ring[n % 2].rearrange("p (t c) -> p t c", t=4), ACT.Copy).then_inc(s_ht, 1)
            act.wait_ge(s_logit, 1)
            nc.scalar.activation(scores[:, :, :], ps_s[1][:, 0:TT * E].rearrange("p (a e) -> p a e", a=TT),
                                 ACT.Sigmoid).then_inc(s_score, 1)
            act.wait_ge(s_shgu, 1)
            nc.scalar.activation(sh_sig[:, :, :], ps_proj[0][:, :].rearrange("p (a c) -> p a c", a=FT),
                                 ACT.Silu).then_inc(s_shsig, 1)

            def silu(k, n):
                act.wait_ge(s_gu, 2 * n + k + 1)
                if not (isinstance(n, int) and n == 0):
                    act.wait_ge(s_eh, 2 * n + k - 1)
                nc.scalar.activation(expert_sig[k][:, :, :],
                                     ps_proj[k][:, 0:FT * SLOTS].rearrange("p (a c) -> p a c", a=FT),
                                     ACT.Silu).then_inc(s_sig, 1)

            def take_down(k, n):
                act.wait_ge(s_dn, 2 * n + k + 1)
                nc.scalar.activation(y_t[:, :, k * SLOTS:(k + 1) * SLOTS],
                                     down_out[k][:, :].rearrange("p (t c) -> p t c", t=KT), ACT.Copy).then_inc(s_yt, 1)

            def experts(n):
                silu(0, n)
                take_down(1, n - 1)
                silu(1, n)
                take_down(0, n)

            def whole_pass(n):
                silu(0, n)
                silu(1, n)
                take_down(0, n)
                with act.Fori(1, PAIRS) as i:
                    experts(n + i)
                take_down(1, n + PAIRS - 1)

            whole_pass(0)
            act.wait_ge(s_jobs, 1)
            n_jobs = act.value_load(jobs[0:1, 0:1], min_val=0, max_val=MAX_JOBS)
            with act.Fori(0, MAX_JOBS // 2) as i:
                with act.If(n_jobs > 2 * i):
                    silu(0, PAIRS + i)
                    silu(1, PAIRS + i)
                    take_down(0, PAIRS + i)
                    take_down(1, PAIRS + i)
            act.wait_ge(s_var, 2)
            nc.scalar.activation(std, var_eps, ACT.Sqrt).then_inc(s_std, 1)

        @block.vector
        def _(dve):
            dve.wait_ge(s_const, 4)
            nc.vector.memset(mask[:, 0, :, :], 0.0).then_inc(s_residue, 1)
            for g in (1, 2):
                nc.vector.tensor_scalar(dist_mod[:, g - 1, :], dist[:, :], DILATIONS[g] - 1, None,
                                        ALU.bitwise_and).then_inc(s_dve, 1)
            dve.wait_ge(s_dve, dve_done(2))
            for g in (1, 2):
                nc.vector.tensor_scalar(mask[:, g, :, :].rearrange("p a b -> p (a b)"), dist_mod[:, g - 1, :], 1.0,
                                        MASKED, ALU.min, ALU.mult).then_inc(s_residue, 1)
            for r in range(2):
                dve.wait_ge(s_turned_par, r + 1)
                nc.vector.tensor_copy(par[:, 4 * r:4 * r + 4, :],
                                      ps_s[1][:, r * 512:r * 512 + 4 * N_PAR].rearrange("p (a b) -> p a b", b=N_PAR)
                                      ).then_inc(s_par_t, 1)
            for n in range(8):
                dve.wait_ge(s_xhi, n + 1)
                tt, t = n // 4, n % 4 * 4
                nc.vector.tensor_tensor(x_lo[:, t:t + 4, tt * P:(tt + 1) * P],
                                        turn_ring[n % 2].rearrange("p (t c) -> p t c", t=4),
                                        x_hi[:, t:t + 4, tt * P:(tt + 1) * P].bitcast(F32),
                                        ALU.subtract).then_inc(s_xlo, 1)

            def split(name, i, j, u):
                dve.wait_ge(s_hi, u.n + 1)
                w = wide(name, j)
                nc.vector.tensor_tensor(tiles(w_lo, u, w), raw_half(u, w), tiles(w_hi, u, w).bitcast(F32),
                                        ALU.subtract).then_inc(s_lo, 1)

            def evacuate(name, i, j, u):
                if not (name in ("ch", "cb", "out") or wide(name, j)):
                    return
                dve.wait_ge(s_mm, u.n + 1)
                if name == "ch":
                    n = 4 * i + j
                    if j == 0 and isinstance(i, int):
                        evacuated(dve, "ch")
                        dve.wait_ge(s_const, 6)
                        dve.wait_ge(s_cleared, 16 * (MAX_JOBS // 2))
                    dst = c_pad[:, bass.ds(n, 1), TAPS_C - 1:].rearrange("p a c -> p (a c)")
                    nc.vector.tensor_tensor(dst, ps_proj[u.bank][:, 0:TOK], dst, ALU.mult).then_inc(s_ev[u.bank], 1)
                    dve.wait_ge(s_ev[u.bank], u.bank_count + 1)
                    y = branch[:, 2, bass.ds(n, 1), :].rearrange("p a c -> p (a c)")
                    for k in range(TAPS_C):
                        v = c_pad[:, bass.ds(n, 1), k:k + TOK].rearrange("p a c -> p (a c)")
                        w = par[:, bass.ds(n, 1), TAPS_A + 3 + k:TAPS_A + 4 + k].rearrange("p a c -> p (a c)")
                        if k == 0:
                            ins = nc.vector.tensor_scalar(y, v, w, None, ALU.mult)
                        else:
                            ins = nc.vector.scalar_tensor_tensor(out=y, in0=v, scalar=w, in1=y, op0=ALU.mult, op1=ALU.add)
                        ins.then_inc(s_ctap, 1)
                        dve.wait_ge(s_ctap, n * TAPS_C + k + 1)
                elif name == "cb":
                    y = branch[:, 2, bass.ds(4 * i + j, 1), :].rearrange("p a c -> p (a c)")
                    nc.vector.tensor_tensor(y, ps_proj[u.bank][:, 0:TOK], y, ALU.mult).then_inc(s_ev[u.bank], 1)
                elif name == "out":
                    if j == 0 and isinstance(i, int):
                        dve.wait_ge(s_xr, 16)
                    cols = acc[:, j % 2, bass.ds(512 * i + 2 * P * (j // 2), 2 * P)]
                    nc.vector.scalar_tensor_tensor(out=cols, in0=cols, scalar=ALPHA, in1=pair_out(j),
                                                   op0=ALU.mult, op1=ALU.add).then_inc(s_ev[u.bank], 1)
                else:
                    k = j - 8
                    w = 4 * i + k
                    if not (isinstance(w, int) and w < 2):
                        dve.wait_ge(s_added, w - 1)
                    if k == 0:
                        dve.wait_ge(s_ev[0], u.bank_count)
                        dve.wait_ge(s_ev[1], u.bank_count)
                    nc.vector.tensor_tensor(gated[k % 2][:, :, :].rearrange("p a c -> p (a c)"), ps_proj[u.bank][:, :],
                                            gates[:, 2 * k:2 * k + 2, :].rearrange("p a c -> p (a c)"),
                                            ALU.mult).then_inc(s_gated, 1)
                    dve.wait_ge(s_gated, w + 1)
                    dve.sem_inc(s_ev[u.bank], 1)

            def attention(half):
                def masked(job):
                    n, r, kt = JOBS * half + job, job % 2, job % 2 + 1
                    dve.wait_ge(s_scored, n + 1)
                    if n >= 2:
                        dve.wait_ge(s_pturn, n - 1)
                    p = att_p[r][:, 0:3 * kt * P].rearrange("p (g k) -> p g k", g=N_GROUPS_ATT)
                    m = mask[:, :, 2 - kt:2, :].rearrange("p g a b -> p g (a b)")
                    nc.vector.tensor_tensor_reduce(p, ps_s[r][:, 0:3 * kt * P].rearrange("p (g k) -> p g k", g=N_GROUPS_ATT),
                                                   m, SCALE, NEG, ALU.add, ALU.max, row_max[r]).then_inc(s_dve, 1)
                    dve.wait_ge(s_dve, dve_done(1))
                    nc.vector.tensor_scalar(neg_max[r], row_max[r], -1.0, None, ALU.mult).then_inc(s_masked, 1)

                if half == 0:
                    dve.wait_ge(s_const, 5)
                masked(0)
                for job in range(JOBS):
                    n, r, kt = JOBS * half + job, job % 2, job % 2 + 1
                    if job + 1 < JOBS:
                        masked(job + 1)
                    dve.wait_ge(s_exp, n + 1)
                    nc.vector.reciprocal(row_rcp[r], row_sum[r]).then_inc(s_dve, 1)
                    dve.wait_ge(s_dve, dve_done(1))
                    nc.vector.tensor_scalar(att_p[r][:, 0:3 * kt * P], att_p[r][:, 0:3 * kt * P], row_rcp[r], None,
                                            ALU.mult).then_inc(s_norm, 1)

            def conv_tap(tap, const):
                if const and tap == 0:
                    dve.wait_ge(s_glu, CT)
                    dve.wait_ge(s_par_t, 2)
                else:
                    dve.wait_ge(s_conv, CT * tap)
                for c in range(CT):
                    v = a_pad[:, c, bass.ds(tap, TOK)]
                    w = par[:, c, bass.ds(tap, 1)]
                    y = branch[:, 0, c, :]
                    if const and tap == 0:
                        ins = nc.vector.tensor_scalar(y, v, w, par[:, c, TAPS_A:TAPS_A + 1], ALU.mult, ALU.add)
                    else:
                        ins = nc.vector.scalar_tensor_tensor(out=y, in0=v, scalar=w, in1=y, op0=ALU.mult, op1=ALU.add)
                    ins.then_inc(s_conv, 1)

            def after(name, i, j):
                first = isinstance(i, int) and i == 0
                if first and j == 3 and name == "aval":
                    attention(0)
                if name == "qk1" and (j == 3 or not first):
                    conv_tap(4 * i + j - 3, first)
                if name == "v1" and first:
                    conv_tap(21 + j, False)
                if name == "v1" and not first and j < 3:
                    conv_tap(25 + 3 * (i - 1) + j, False)
                if first and j == 3 and name == "cc":
                    attention(1)
                if first and j == 3 and name == "ch":
                    dve.wait_ge(s_asum, 1)
                    nc.vector.tensor_scalar(a_mean[:, :], ps_s[0][:, 0:TOK], 1.0 / C, None, ALU.mult).then_inc(s_dve, 1)
                    dve.wait_ge(s_dve, dve_done(1))
                    nc.vector.tensor_tensor(branch[:, 0, :, :], branch[:, 0, :, :],
                                            a_mean[:, :].unsqueeze(1).to_broadcast([P, CT, TOK]),
                                            ALU.subtract).then_inc(s_acent, 1)
                if first and j == 3 and name == "cb":
                    dve.wait_ge(s_asum, 2)
                    nc.vector.tensor_scalar(a_mean[:, :], ps_s[0][:, 512:512 + TOK], 1.0 / C, LN_EPS, ALU.mult,
                                            ALU.add).then_inc(s_avar, 1)
                    dve.wait_ge(s_astd, 1)
                    nc.vector.reciprocal(a_mean[:, :], a_rstd[:, :]).then_inc(s_dve, 1)
                    dve.wait_ge(s_dve, dve_done(1))
                    nc.vector.tensor_tensor(branch[:, 0, :, :], branch[:, 0, :, :],
                                            a_mean[:, :].unsqueeze(1).to_broadcast([P, CT, TOK]),
                                            ALU.mult).then_inc(s_anorm, 1)
                if name == "gb" and j == 6:
                    dve.wait_ge(s_brhi, i + 1)
                    nc.vector.tensor_tensor(branch_lo[:, :, :],
                                            branch[:, bass.ds(i // 2, 1), :, :].rearrange("p n t c -> p (n t) c"),
                                            branch_hi[:, :, :].bitcast(F32), ALU.subtract).then_inc(s_brlo, 1)
                if name == "out" and first and j == 2:
                    for c in range(4):
                        dve.wait_ge(s_mhi, c + 1)
                        nc.vector.tensor_tensor(merged_lo[:, 4 * c:4 * c + 4, :], merged[:, 4 * c:4 * c + 4, :],
                                                merged_hi[:, 4 * c:4 * c + 4, :].bitcast(F32),
                                                ALU.subtract).then_inc(s_mlo, 1)

            stream(dve, split, evacuate, after)

            evacuated_all = units // 2
            for r in range(2):
                dve.wait_ge(s_ev[r], evacuated_all)
            layer_norm_rows(dve, ln_g, ln_b, 0)

            def step(ins, k=1):
                ins.then_inc(s_dve, 1)
                dve.wait_ge(s_dve, dve_done(1))

            def batch(instructions):
                k = 0
                for ins in instructions:
                    ins.then_inc(s_dve, 1)
                    k += 1
                dve.wait_ge(s_dve, dve_done(k))

            nc.vector.memset(groups[:, :, 8:16], FILL).then_inc(s_dve, 1)
            dve.wait_ge(s_dve, dve_done(1))
            dve.wait_ge(s_score, 1)
            dve.wait_ge(s_bias, 16)
            step(nc.vector.tensor_tensor(choice[:, :, :], scores[:, :, :],
                                         bias_b[:, :].unsqueeze(1).to_broadcast([P, TT, E]), ALU.add))
            G8 = E // N_ROUTE_GROUPS
            batch(nc.vector.max(top_in_group[:, tt, g, :], choice[:, tt, g * G8:(g + 1) * G8])
                  for tt in range(TT) for g in range(N_ROUTE_GROUPS))
            step(nc.vector.tensor_tensor(groups[:, :, 0:8], top_in_group[:, :, :, 0], top_in_group[:, :, :, 1], ALU.add))
            batch(nc.vector.max(best_groups[:, tt, :], groups[:, tt, :]) for tt in range(TT))
            step(nc.vector.memset(best_groups[:, :, TOPK_GROUPS:8], FILL))
            batch(nc.vector.match_replace(groups_left[:, tt, :], best_groups[:, tt, :], groups[:, tt, :], CHOSEN)
                  for tt in range(TT))
            step(nc.vector.tensor_scalar(group_in[:, :, :], groups_left[:, :, 0:8], CHOSEN, None, ALU.is_equal))
            step(nc.vector.tensor_scalar(group_out[:, :, :], group_in[:, :, :], -NEG, NEG, ALU.mult, ALU.add))
            by_group = lambda a: a[:, :, :].rearrange("p a (g e) -> p (a g) e", e=G8)
            spread = lambda a: a[:, :, :].rearrange("p a g -> p (a g)").unsqueeze(2).to_broadcast(
                [P, TT * N_ROUTE_GROUPS, G8])
            step(nc.vector.tensor_tensor(by_group(masked), by_group(choice), spread(group_in), ALU.mult))
            step(nc.vector.tensor_tensor(by_group(masked), by_group(masked), spread(group_out), ALU.add))
            batch(nc.vector.max(best[:, tt, :], masked[:, tt, :]) for tt in range(TT))
            batch(nc.vector.match_replace(left[:, tt, :], best[:, tt, :], masked[:, tt, :], CHOSEN) for tt in range(TT))
            nc.vector.tensor_scalar(chosen[:, :, :], left[:, :, :], CHOSEN, None, ALU.is_equal).then_inc(s_chosen, 1)
            dve.wait_ge(s_chosen, 1)
            step(nc.vector.tensor_scalar(slot_of[:, :, :], chosen[:, :, :], -NO_SLOT, NO_SLOT, ALU.mult, ALU.add))
            dve.wait_ge(s_count, 1)
            step(nc.vector.tensor_tensor(slot_of[:, :, :], slot_of[:, :, :],
                                         ps_s[1][:, 512:512 + TT * E].rearrange("p (a e) -> p a e", a=TT), ALU.add))
            nc.vector.tensor_copy(count_of[:, :], ps_s[1][:, 512 + TT * E:512 + (TT + 1) * E]).then_inc(s_counted, 1)

            def index():
                for tt in range(TT):
                    if tt:
                        dve.wait_ge(s_hitsum, tt)
                    nc.vector.tensor_tensor(hits[:, :, :],
                                            slot_of[:, tt, :].unsqueeze(2).to_broadcast([P, E, SLOTS]),
                                            iota_slot[:, 0:SLOTS].unsqueeze(1).to_broadcast(
                                                [P, E, SLOTS]), ALU.is_equal).then_inc(s_hit, 1)
                dve.wait_ge(s_hitsum, 2)
                sums = lambda tt: ps_s[0][:, 512 * tt:512 * tt + 2 * PAIRS].rearrange("p (n k) -> p n k", k=2)
                nc.vector.tensor_copy(hit_sum[0][:, :, :], sums(0)).then_inc(s_idx, 1)
                dve.wait_ge(s_idx, 1)
                nc.vector.tensor_tensor(hit_sum[1][:, :, :], sums(1), hit_sum[0][:, :, :], ALU.add).then_inc(s_idx, 1)
                dve.wait_ge(s_idx, 2)
                nc.vector.tensor_scalar(hit_sum[0][:, :, 0], hit_sum[1][:, :, 1], -NO_ROW, NO_ROW, ALU.mult,
                                        ALU.add).then_inc(s_idx, 1)
                dve.wait_ge(s_idx, 3)
                nc.vector.tensor_tensor(tok_idx[:, :], hit_sum[0][:, :, 0], hit_sum[1][:, :, 0], ALU.add).then_inc(s_idx, 1)

            dve.wait_ge(s_tab, 5)
            index()

            dve.wait_ge(s_shsig, 1)
            nc.vector.tensor_tensor(sh_h[:, :, :], ps_proj[1][:, :].rearrange("p (a c) -> p a c", a=FT),
                                    sh_sig[:, :, :], ALU.mult).then_inc(s_shh, 1)
            dve.wait_ge(s_perm, 2)
            for n in range(8):
                dve.wait_ge(s_shd, n + 1)
                cols = acc[:, n // 4, n % 4 * 512:n % 4 * 512 + 512]
                nc.vector.scalar_tensor_tensor(out=cols, in0=cols, scalar=ALPHA, in1=down_out[n % 2][:, 0:512],
                                               op0=ALU.mult, op1=ALU.add).then_inc(s_shacc, 1)

            step(nc.vector.tensor_tensor(weight[:, :, :], scores[:, :, :], chosen[:, :, :], ALU.mult))
            step(nc.vector.tensor_reduce(w_sum, weight[:, :, :], AX_X, ALU.add))
            step(nc.vector.reciprocal(w_rcp, w_sum))
            batch(nc.vector.tensor_scalar(weight[:, tt, :], weight[:, tt, :], w_rcp[:, tt:tt + 1], ROUTED_SCALE,
                                          ALU.mult, ALU.mult) for tt in range(TT))
            dve.wait_ge(s_counted, 1)
            step(nc.vector.tensor_scalar(extra[:, :], count_of[:, :], float(SLOTS), None, ALU.is_gt))
            for b in range(2, BLOCKS):
                step(nc.vector.tensor_scalar(over_row[:, :], count_of[:, :], float(b * SLOTS), None, ALU.is_gt))
                step(nc.vector.tensor_tensor(extra[:, :], extra[:, :], over_row[:, :], ALU.add))
            step(nc.vector.tensor_tensor_scan(job_ends[:, :], ones[:, 0:E], extra[:, :], 0.0, ALU.mult, ALU.add))
            numbers = iota_slot[:, 0:MAX_JOBS]
            step(nc.vector.tensor_tensor(job_table[:, :, :], job_ends[:, :].unsqueeze(1).to_broadcast([P, MAX_JOBS, E]),
                                         numbers.unsqueeze(2).to_broadcast([P, MAX_JOBS, E]), ALU.is_le))
            step(nc.vector.tensor_reduce(job_n[:, 0, :], job_table[:, :, :], AX_X, ALU.add))
            step(nc.vector.tensor_tensor(job_table[:, :, :], job_table[:, :, :],
                                         extra[:, :].unsqueeze(1).to_broadcast([P, MAX_JOBS, E]), ALU.mult))
            step(nc.vector.tensor_reduce(job_n[:, 1, :], job_table[:, :, :], AX_X, ALU.add))
            step(nc.vector.tensor_scalar(job_expert[:, :], job_n[:, 0, :], float(E - 1), None, ALU.min))
            step(nc.vector.tensor_tensor(job_n[:, 1, :], numbers, job_n[:, 1, :], ALU.subtract))
            step(nc.vector.tensor_scalar(job_n[:, 1, :], job_n[:, 1, :], 1.0, float(SLOTS), ALU.add, ALU.mult))
            step(nc.vector.tensor_scalar(job_first[:, :], job_n[:, 1, :], float((BLOCKS - 1) * SLOTS), None, ALU.min))
            nc.vector.tensor_copy(jobs[:, :], job_ends[:, E - 1:E]).then_inc(s_jobs, 1)
            step(nc.vector.tensor_tensor(over_row[:, :], job_ends[:, :], extra[:, :], ALU.subtract))
            step(nc.vector.tensor_scalar(over_row[:, :], over_row[:, :], float(SLOTS), float(E * SLOTS - SLOTS + 1),
                                         ALU.mult, ALU.add))
            step(nc.vector.tensor_tensor(over_row[:, :], over_row[:, :], row_base[:, :], ALU.subtract))
            step(nc.vector.tensor_scalar(masked[:, :, :], slot_of[:, :, :], float(SLOTS), None, ALU.is_ge))
            step(nc.vector.tensor_tensor(masked[:, :, :], masked[:, :, :],
                                         over_row[:, :].unsqueeze(1).to_broadcast([P, TT, E]), ALU.mult))
            step(nc.vector.tensor_tensor(row_of[:, :, :], slot_of[:, :, :],
                                         row_base[:, :].unsqueeze(1).to_broadcast([P, TT, E]), ALU.add))
            step(nc.vector.tensor_tensor(row_of[:, :, :], row_of[:, :, :], masked[:, :, :], ALU.add))
            step(nc.vector.tensor_tensor(row_of[:, :, :], row_of[:, :, :], chosen[:, :, :], ALU.mult))
            batch(nc.vector.max(my_row[:, tt, :], row_of[:, tt, :]) for tt in range(TT))
            for tt in range(TT):
                batch(nc.vector.scalar_tensor_tensor(out=match[:, k, :], in0=row_of[:, tt, :],
                                                     scalar=my_row[:, tt, k:k + 1], in1=weight[:, tt, :],
                                                     op0=ALU.is_equal, op1=ALU.mult) for k in range(TOPK))
                step(nc.vector.tensor_reduce(my_w[:, tt, :], match[:, :, :], AX_X, ALU.add))
            nc.vector.tensor_scalar(my_idx[:, :, :], my_row[:, :, :], -1.0, None, ALU.add).then_inc(s_mine, 1)

            def product(k, n):
                dve.wait_ge(s_sig, 2 * n + k + 1)
                if not (isinstance(n, int) and n == 0):
                    dve.wait_ge(s_dn, 2 * n + k - 1)
                nc.vector.tensor_tensor(expert_h[k][:, :, :],
                                        ps_proj[k][:, FT * SLOTS:2 * FT * SLOTS].rearrange("p (a c) -> p a c", a=FT),
                                        expert_sig[k][:, :, :], ALU.mult).then_inc(s_eh, 1)

            def rows_out(t0, n):
                for g in range(4):
                    dve.wait_ge(s_turn, t0 + g + 1)
                    if g == 0 and not (isinstance(n, int) and n == 0):
                        dve.wait_ge(s_yw, 16 * n)
                    nc.vector.tensor_copy(y_rows[:, g * 512:(g + 1) * 512], turn_ring[g % 2]).then_inc(s_turnout, 1)

            def rows_in(t0):
                for g in range(4):
                    dve.wait_ge(s_turn, t0 + g + 1)
                    nc.vector.tensor_copy(xg_t[:, 4 * g:4 * g + 4, :],
                                          turn_ring[g % 2].rearrange("p (t c) -> p t c", t=4)).then_inc(s_turnout, 1)

            def whole_pass(n):
                rows_in(8 * n)
                product(0, n)
                product(1, n)
                rows_in(8 * n + 4)
                with dve.Fori(1, PAIRS - 1) as i:
                    m = n + i
                    product(0, m)
                    product(1, m)
                    rows_out(8 * m, m - 1)
                    rows_in(8 * m + 4)
                m = n + PAIRS - 1
                product(0, m)
                product(1, m)
                rows_out(8 * m, m - 1)
                rows_out(8 * m + 4, m)

            whole_pass(0)
            n_jobs = dve.value_load(jobs[0:1, 0:1], min_val=0, max_val=MAX_JOBS)
            with dve.Fori(0, MAX_JOBS // 2) as i:
                with dve.If(n_jobs > 2 * i):
                    n = PAIRS + i
                    for k in range(2):
                        e = dve.value_load(job_expert[0:1, bass.ds(2 * i + k, 1)], min_val=0, max_val=E - 1)
                        first = dve.value_load(job_first[0:1, bass.ds(2 * i + k, 1)], min_val=0,
                                               max_val=(BLOCKS - 1) * SLOTS)
                        for tt in range(TT):
                            nc.vector.tensor_scalar(job_hits[:, tt, k, :], iota_slot[:, bass.ds(first, SLOTS)],
                                                    slot_of[:, tt, bass.ds(e, 1)], None, ALU.is_equal).then_inc(s_jobhit, 1)
                    dve.wait_ge(s_jobsum, i + 1)
                    nc.vector.tensor_scalar(job_free, ps_s[0][:, 1:2], -NO_ROW, NO_ROW, ALU.mult,
                                            ALU.add).then_inc(s_jobidx, 1)
                    dve.wait_ge(s_jobidx, 2 * i + 1)
                    nc.vector.tensor_tensor(job_idx[:, :], ps_s[0][:, 0:1], job_free, ALU.add).then_inc(s_jobidx, 1)
                    rows_in(8 * n)
                    product(0, n)
                    product(1, n)
                    rows_out(8 * n + 4, n)
            for k in range(TOPK):
                for tt in range(TT):
                    n = TT * k + tt
                    dve.wait_ge(s_got[n % N_GATHER], 16 * (n // N_GATHER + 1))
                    if k:
                        dve.wait_ge(s_used, n - TT + 1)
                    nc.vector.scalar_tensor_tensor(out=acc[:, tt, :], in0=gather[n % N_GATHER][:, :],
                                                   scalar=my_w[:, tt, k:k + 1], in1=acc[:, tt, :],
                                                   op0=ALU.mult, op1=ALU.add).then_inc(s_used, 1)
            dve.wait_ge(s_used, TT * TOPK)
            layer_norm_rows(dve, ln2_gt, ln2_bt, 1)

        @block.tensor
        def _(pe):
            pe.wait_ge(s_const, 2)
            pe.wait_ge(s_par, 16 * 5)
            for r in range(2):
                for c in range(4):
                    ins = pe.transpose(ps_s[1][:, r * 512 + c * N_PAR:r * 512 + (c + 1) * N_PAR],
                                       par_rows[:, (4 * r + c) * P:(4 * r + c + 1) * P], ident[0:N_PAR, 0:N_PAR])
                ins.then_inc(s_turned_par, 1)

            def turn_tokens(rows, first, seen, seen_base):
                for n in range(8):
                    if n >= 2:
                        pe.wait_ge(seen, seen_base + n - 1)
                    tt, t = n // 4, n % 4 * 4
                    for k in range(4):
                        ins = pe.transpose(turn_ring[n % 2][:, k * P:(k + 1) * P],
                                           rows[:, tt, (t + k) * P:(t + k + 1) * P], ident[:, :])
                    ins.then_inc(s_turned, 1)

            pe.wait_ge(s_x, 16)
            turn_tokens(x_rows, 0, s_xlo, 0)
            pe.wait_ge(s_xlo, 8)

            def multiply(name, i, j, u):
                if by_pair(name) and j % 2 == 0:
                    return
                pe.wait_ge(s_lo, u.n + 1)
                if by_pair(name):
                    for r in range(2):
                        pe.wait_ge(s_ev[r], u.bank_count - 1)
                elif not u.first_bank:
                    pe.wait_ge(s_ev[u.bank], u.bank_count)
                w = wide(name, j)
                hi, lo = tiles(w_hi, u, w), tiles(w_lo, u, w)
                ps = ps_proj[u.bank]
                if w:
                    if j == 8:
                        pe.wait_ge(s_brlo, i + 1)
                    for half in range(2):
                        n = 0
                        for t in range(CT):
                            for a, b in ((hi, branch_hi), (hi, branch_lo), (lo, branch_hi)):
                                ins = pe.matmul(ps[:, half * TOK:(half + 1) * TOK], a[:, t, half * P:(half + 1) * P],
                                                b[:, t, :], start=(n == 0), stop=(n == 3 * CT - 1))
                                n += 1
                elif by_pair(name):
                    hi, lo = (a[:, u.ring - 1:u.ring + 1, :].rearrange("p r (t c) -> p r t c", t=KT) for a in (w_hi, w_lo))
                    m_hi, m_lo = (merged_hi, merged_lo) if name == "out" else (x_hi, x_lo)
                    if name == "out" and j == 1 and isinstance(i, int):
                        pe.wait_ge(s_mlo, 4)
                    for tt in range(TT):
                        n = 0
                        for t in range(KT):
                            for a, b in ((m_hi, hi), (m_hi, lo), (m_lo, hi)):
                                ins = pe.matmul(pair_out(j - 1 + tt), a[:, t, tt * P:(tt + 1) * P], b[:, :, t, :],
                                                start=(n == 0), stop=(n == 3 * KT - 1))
                                n += 1
                    ins.then_inc(s_mm, 2)
                    return
                else:
                    n = 0
                    for t in range(KT):
                        for a, b in ((hi, x_hi), (hi, x_lo), (lo, x_hi)):
                            ins = pe.matmul(ps[:, 0:TOK], a[:, t, :], b[:, t, :], start=(n == 0), stop=(n == 3 * KT - 1))
                            n += 1
                ins.then_inc(s_mm, 1)

            def attention(half):
                def score(job):
                    n, r, kt, head = JOBS * half + job, job % 2, job % 2 + 1, job // 2
                    if n >= 2:
                        pe.wait_ge(s_masked, n - 1)
                    for g in range(N_GROUPS_ATT):
                        ins = pe.matmul(ps_s[r][:, g * kt * P:(g + 1) * kt * P],
                                        q_t[:, g, head, (kt - 1) * P:kt * P], k_t[:, g, head, 0:kt * P],
                                        start=True, stop=True)
                    ins.then_inc(s_scored, 1)

                evacuated(pe, "aval" if half == 0 else "cc")
                score(0)
                for job in range(JOBS):
                    n, r, kt, head = JOBS * half + job, job % 2, job % 2 + 1, job // 2
                    if job + 1 < JOBS:
                        score(job + 1)
                    pe.wait_ge(s_norm, n + 1)
                    if n >= 1:
                        pe.wait_ge(s_pt, n)
                        pe.wait_ge(s_att, n)
                    for m in range(3 * kt):
                        ins = pe.transpose(ps_t[:, m * P:(m + 1) * P], att_p[r][:, m * P:(m + 1) * P], ident[:, :])
                    ins.then_inc(s_pturn, 1)
                    pe.wait_ge(s_pt, n + 1)
                    for m in range(3 * kt):
                        ins = pe.matmul(ps_t[:, 768:768 + P], v_rows[:, m // kt, head, m % kt, :], p_t[:, m, :],
                                        start=(m == 0), stop=(m == 3 * kt - 1))
                    ins.then_inc(s_av, 1)

            def channel_sum(src, col):
                for c in range(CT):
                    ins = pe.matmul(ps_s[0][:, col:col + TOK], ones[:, :], src[:, c, :], start=(c == 0), stop=(c == CT - 1))
                ins.then_inc(s_asum, 1)

            def between(name):
                if name == "aval":
                    attention(0)
                if name == "cc":
                    attention(1)
                if name == "ch":
                    pe.wait_ge(s_conv, CT * TAPS_A)
                    channel_sum(branch[:, 0, :, :], 0)
                if name == "cb":
                    pe.wait_ge(s_asq, 1)
                    channel_sum(a_sq, 512)

            for s in segs:
                for j in range(s["len"]):
                    if j == 3:
                        between(s["name"])
                    multiply(s["name"], 0, j, Unit(s["base"], s["len"], 0, j))
                with pe.Fori(1, s["n"]) as i:
                    for j in range(s["len"]):
                        multiply(s["name"], i, j, Unit(s["base"], s["len"], i, j))

            pe.wait_ge(s_perm, 2)
            turn_tokens(h_perm, 8, s_ht, 0)
            pe.wait_ge(s_ht, 8)
            pe.wait_ge(s_rw, 16)
            for tt in range(TT):
                for t in range(KT):
                    ins = pe.matmul(ps_s[1][:, tt * E:(tt + 1) * E], h_t[:, t, tt * P:(tt + 1) * P], rw[:, t, :],
                                    start=(t == 0), stop=(t == KT - 1))
            ins.then_inc(s_logit, 1)
            pe.wait_ge(s_ws, 32)
            for r in range(2):
                w = ws[r][:, :].rearrange("p (t f) -> p t f", t=KT)
                for f in range(FT):
                    for t in range(KT):
                        ins = pe.matmul(ps_proj[r][:, f * TOK:(f + 1) * TOK], w[:, t, f * P:(f + 1) * P], h_t[:, t, :],
                                        start=(t == 0), stop=(t == KT - 1))
            ins.then_inc(s_shgu, 1)
            pe.wait_ge(s_chosen, 1)
            pe.wait_ge(s_tab, 5)
            count = lambda k: ps_s[1][:, 512 + k * E:512 + (k + 1) * E]
            pe.matmul(count(0), before[:, :], chosen[:, 0, :], start=True, stop=True)
            pe.matmul(count(1), ones[:, :], chosen[:, 0, :], start=True, stop=False)
            pe.matmul(count(1), before[:, :], chosen[:, 1, :], start=False, stop=True)
            pe.matmul(count(2), ones[:, :], chosen[:, 0, :], start=True, stop=False)
            pe.matmul(count(2), ones[:, :], chosen[:, 1, :], start=False, stop=True).then_inc(s_count, 1)

            def index():
                for tt in range(TT):
                    pe.wait_ge(s_hit, tt + 1)
                    for n in range(PAIRS):
                        ins = pe.matmul(ps_s[0][:, 512 * tt + 2 * n:512 * tt + 2 * n + 2],
                                        hits[:, 2 * n:2 * n + 2, :].rearrange("p a s -> p (a s)"), tok_val[:, tt, :],
                                        start=True, stop=True)
                    ins.then_inc(s_hitsum, 1)

            index()
            pe.wait_ge(s_shh, 1)
            pe.wait_ge(s_wsd, 16)
            pe.wait_ge(s_counted, 1)
            wd = ws[2][:, :].rearrange("p (t c) -> p t c", t=FT)
            for n in range(8):
                if n >= 2:
                    pe.wait_ge(s_shacc, n - 1)
                tt, c = n // 4, n % 4
                for f in range(FT):
                    ins = pe.matmul(down_out[n % 2][:, 0:512], sh_h[:, f, tt * P:(tt + 1) * P],
                                    wd[:, f, c * 512:(c + 1) * 512], start=(f == 0), stop=(f == FT - 1))
                ins.then_inc(s_shd, 1)
            pe.wait_ge(s_shacc, 8)

            def gate_up(k, n, turned=0):
                for r in range(2):
                    pe.wait_ge(s_w[3 * k + r], 16 * (n + 1))
                if k == 0:
                    pe.wait_ge(s_turnout, turned)
                if not (isinstance(n, int) and n == 0):
                    pe.wait_ge(s_eh, 2 * n + k - 1)
                for r in range(2):
                    w = exp_w[3 * k + r][:, :].rearrange("p (t f) -> p t f", t=KT)
                    for f in range(FT):
                        o = (r * FT + f) * SLOTS
                        for t in range(KT):
                            ins = pe.matmul(ps_proj[k][:, o:o + SLOTS], w[:, t, f * P:(f + 1) * P],
                                            xg_t[:, t, k * SLOTS:(k + 1) * SLOTS], start=(t == 0), stop=(t == KT - 1))
                ins.then_inc(s_gu, 1)

            def down(k, n):
                pe.wait_ge(s_w[3 * k + 2], 16 * (n + 1))
                pe.wait_ge(s_eh, 2 * n + k + 1)
                if not (isinstance(n, int) and n == 0):
                    pe.wait_ge(s_yt, 2 * n + k - 1)
                w = exp_w[3 * k + 2][:, :].rearrange("p (t c) -> p t c", t=FT)
                for c in range(KT):
                    for f in range(FT):
                        ins = pe.matmul(down_out[k][:, c * SLOTS:(c + 1) * SLOTS], w[:, f, c * P:(c + 1) * P],
                                        expert_h[k][:, f, :], start=(f == 0), stop=(f == FT - 1))
                ins.then_inc(s_dn, 1)

            def turn(src, t0, g):
                if not (isinstance(t0, int) and t0 + g < 2):
                    pe.wait_ge(s_turnout, t0 + g - 1)
                for k in range(4):
                    c = 4 * g + k
                    ins = pe.transpose(turn_ring[g % 2][:, k * P:(k + 1) * P], src(c), ident[:, :])
                ins.then_inc(s_turn, 1)

            def turn_out(t0, n):
                pe.wait_ge(s_yt, 2 * n + 2)
                for g in range(4):
                    turn(lambda c: y_t[:, c, :], t0, g)

            def turn_in(t0, n):
                pe.wait_ge(s_hg, 16 * (n + 1))
                for g in range(4):
                    turn(lambda c: hg[:, c * P:(c + 1) * P], t0, g)

            def whole_pass(n):
                turn_in(8 * n, n)
                gate_up(0, n, 8 * n + 4)
                gate_up(1, n)
                turn_in(8 * n + 4, n + 1)
                down(0, n)
                with pe.Fori(1, PAIRS - 1) as i:
                    m = n + i
                    gate_up(0, m, 8 * m)
                    down(1, m - 1)
                    gate_up(1, m)
                    turn_out(8 * m, m - 1)
                    turn_in(8 * m + 4, m + 1)
                    down(0, m)
                m = n + PAIRS - 1
                gate_up(0, m, 8 * m)
                down(1, m - 1)
                gate_up(1, m)
                turn_out(8 * m, m - 1)
                down(0, m)
                down(1, m)
                turn_out(8 * m + 4, m)

            whole_pass(0)
            pe.wait_ge(s_jobs, 1)
            n_jobs = pe.value_load(jobs[0:1, 0:1], min_val=0, max_val=MAX_JOBS)
            with pe.Fori(0, MAX_JOBS // 2) as i:
                with pe.If(n_jobs > 2 * i):
                    n = PAIRS + i
                    pe.wait_ge(s_jobhit, 2 * TT * (i + 1))
                    for tt in range(TT):
                        ins = pe.matmul(ps_s[0][:, 0:2], job_hits[:, tt, :, :].rearrange("p a s -> p (a s)"),
                                        tok_val[:, tt, :], start=(tt == 0), stop=(tt == TT - 1))
                    ins.then_inc(s_jobsum, 1)
                    turn_in(8 * n, n)
                    gate_up(0, n, 8 * n + 4)
                    gate_up(1, n)
                    down(0, n)
                    down(1, n)
                    turn_out(8 * n + 4, n)


_INS = ['x', 'w_in', 'conv_a_w', 'conv_a_b', 'ln_a_g', 'ln_a_b', 'conv_c_w', 'w_branch', 'w_out', 'ln1_g', 'ln1_b',
        'router_w', 'router_bias', 'w_gate', 'w_up', 'w_down', 'ws_gate', 'ws_up', 'ws_down', 'ln2_g', 'ln2_b']
_OUTS = [((1, 256, 2048), 'float32')]


def kernel(**inputs):
    import numpy as _np
    import concourse.bacc as _bacc
    from concourse import mybir as _mybir
    from concourse.bass_utils import run_bass_kernel_spmd as _run

    nc = _bacc.Bacc("TRN2", target_bir_lowering=False, num_devices=1)
    arrays, args = {}, []
    for name in _INS:
        a = _np.ascontiguousarray(inputs[name])
        arrays[f"in_{name}_dram"] = a
        args.append(nc.dram_tensor(f"in_{name}_dram", a.shape, _mybir.dt.from_np(a.dtype), kind="ExternalInput").ap())
    for i, (shape, dtype) in enumerate(_OUTS):
        dt = _mybir.dt.from_np(_np.dtype(dtype))
        args.append(nc.dram_tensor(f"out_{i}_dram", shape, dt, kind="ExternalOutput").ap())
    build(nc, *args)
    r = _run(nc, [arrays], core_ids=[0])
    got = tuple(r.results[0][f"out_{i}_dram"] for i in range(len(_OUTS)))
    return got[0]
```

```python
from contextlib import ExitStack

import concourse.bass as bass
from concourse import mybir

P = 128
F32 = mybir.dt.float32
F32R = mybir.dt.float32r
I32 = mybir.dt.int32
U32 = mybir.dt.uint32
ACT = mybir.ActivationFunctionType
ALU = mybir.AluOpType
AX_X = mybir.AxisListType.X
KB = 1024

N_GROUPS_ATT = 3
DILATIONS = (1, 4, 16)
SPAN = 128
N_ROUTE_GROUPS = 8
TOPK_GROUPS = 4
TOPK = 8
ROUTED_SCALE = 2.5
LN_EPS = 1e-5
NEG = -1e30
FILL = -2e38
CHOSEN = -3e38
NO_SLOT = 1000.0
SLOTS = 64


class Unit:

    def __init__(self, base, length, i, j):
        self.n = base + length * i + j
        self.ring = j % 4
        self.bank = j % 2
        self.half = j % 2
        self.raw = (j // 2) % 2
        self.raw_count = base // 4 + (length // 4) * i + j // 4 + 1
        self.bank_count = base // 2 + (length // 2) * i + j // 2
        self.first = isinstance(i, int) and base + length * i + j < 4
        self.first_bank = isinstance(i, int) and base + length * i + j < 2


class ExpertUnit:

    def __init__(self, first, q, c, j):
        self.n = 24 * q + c
        self.ring = c % 4
        self.loads = 6 * q + (c - first) // 4 + 1
        self.j = j


def build(nc, x, w_in, conv_a_w, conv_a_b, ln_a_g, ln_a_b, conv_c_w, w_branch, w_out, ln1_g, ln1_b,
          router_w, router_bias, w_gate, w_up, w_down, ws_gate, ws_up, ws_down, ln2_g, ln2_b, out):
    DEPTH, D, N_IN = w_in.shape
    assert DEPTH == 1
    TOK = x.shape[1]
    TT = TOK // P
    KT = D // P
    C = conv_a_w.shape[2]
    CT = C // P
    TAPS_A = conv_a_w.shape[1]
    TAPS_C = conv_c_w.shape[1]
    HEADS = CT
    ATT_W = N_GROUPS_ATT * C
    OFF_Q = 2 * C
    OFF_C = OFF_Q + 3 * ATT_W
    OFF_G = OFF_C + 3 * C
    E = w_gate.shape[1]
    F = w_gate.shape[3]
    FT = F // P
    QUADS = E // 4
    ALPHA = float((2.0 * DEPTH) ** 0.25)
    SCALE = float(P) ** -0.5
    MASKED = NEG / SCALE
    BLOCKS = TOK // SLOTS
    MAX_JOBS = TOK * TOPK // SLOTS
    N_PAR = TAPS_A + 3 + TAPS_C
    HALF = HEADS // 2
    N_GATHER = 4
    assert TT == 2 and KT == 16 and CT == 8 and FT == 2

    ctx = ExitStack()
    with ctx:
        base0 = -(-nc.sbuf_base // 32) * 32

        def at(name, shape, dt, kb):
            return nc.alloc_sbuf_tensor_at(name, shape, dt, offset=base0 + int(kb * KB))

        def sem(name):
            return ctx.enter_context(nc.semaphore(name))

        raw = [at(f"raw{r}", [P, 4096], F32, 16 * r) for r in range(2)]
        w_hi = at("w_hi", [P, 4, 2048], F32R, 32)
        w_lo = at("w_lo", [P, 4, 2048], F32R, 64)
        x_hi = at("x_hi", [P, KT, TOK], F32R, 96)
        x_lo = at("x_lo", [P, KT, TOK], F32R, 112)
        x_rows = at("x_rows", [P, TT, D], F32, 128)
        par_rows = at("par_rows", [N_PAR, C], F32, 144)
        dist = at("dist", [P, 2 * P], I32, 148)
        dist_mod = at("dist_mod", [P, 2, 2 * P], I32, 149)
        q_k = at("q_k", [P, 2 * N_GROUPS_ATT, HALF, TOK], F32, 128)
        q_t, k_t = q_k[:, 0:N_GROUPS_ATT, :, :], q_k[:, N_GROUPS_ATT:, :, :]
        v_rows = at("v_rows", [P, N_GROUPS_ATT, HALF, TT, P], F32, 152)
        merged = at("merged", [P, KT, TOK], F32, 128)
        branch_hi = at("branch_hi", [P, CT, TOK], F32R, 144)
        branch_lo = at("branch_lo", [P, CT, TOK], F32R, 152)
        a_mean = at("a_mean", [P, TOK], F32, 160)
        a_rstd = at("a_rstd", [P, TOK], F32, 161)
        branch = at("branch", [P, 3, CT, TOK], F32, 164)
        att_p = [at(f"att_p{r}", [P, N_GROUPS_ATT * 2 * P], F32, 180 + 3 * r) for r in range(2)]
        a_pad = at("a_pad", [P, CT, TAPS_A - 1 + TOK], F32, 188)
        c_pad = at("c_pad", [P, CT, TAPS_C - 1 + TOK], F32, 188)
        gated = [at(f"gated{r}", [P, 2, TOK], F32, 188 + 2 * r) for r in range(2)]
        p_t = [at("p_t0", [P, N_GROUPS_ATT, P], F32, 203), at("p_t1", [P, 2 * N_GROUPS_ATT, P], F32, 197)]
        mask = at("mask", [P, N_GROUPS_ATT, 2, P], F32, 200)
        a_sig = [at(f"a_sig{r}", [P, TOK], F32, 203 + r) for r in range(2)]
        a_sq = at("a_sq", [P, CT, TOK], F32, 197)
        gates = at("gates", [P, CT, TOK], F32, 197)
        zeros = at("zeros", [P, 512], F32, 186)
        par = at("par", [P, CT, N_PAR], F32, 205)
        ident = at("ident", [P, P], F32, 206.25)
        ones = at("ones", [P, P], F32, 206.75)
        tiny = at("tiny", [P, 64], F32, 207.25)
        jobs = at("jobs", [P, 1], I32, 207.59375)
        neg_max = [tiny[:, r:r + 1] for r in range(2)]
        row_max = [tiny[:, 2 + r:3 + r] for r in range(2)]
        row_sum = [tiny[:, 4 + r:5 + r] for r in range(2)]
        row_rcp = [tiny[:, 6 + r:7 + r] for r in range(2)]
        mean_var = tiny[:, 8:12].rearrange("p (a b) -> p a b", a=2)
        var_eps = tiny[:, 12:14]
        std = tiny[:, 14:16]
        rstd = tiny[:, 16:18]
        w_sum = tiny[:, 18:20]
        w_rcp = tiny[:, 20:22]
        tok_no = tiny[:, 22:24]
        merged_hi = at("merged_hi", [P, KT, TOK], F32R, 96)
        merged_lo = at("merged_lo", [P, KT, TOK], F32R, 112)
        acc = at("acc", [P, TT, D], F32, 144)
        ln_g = at("ln_g", [P, D], F32, 128)
        ln_b = at("ln_b", [P, D], F32, 136)
        exp_raw = [at(f"exp_raw{r}", [P, 2048], F32, 8 * r) for r in range(4)]
        h_hi = at("h_hi", [P, TT, D], F32R, 96)
        h_lo = at("h_lo", [P, TT, D], F32R, 112)
        sh_ht_hi = at("sh_ht_hi", [P, FT, TOK], F32R, 128)
        sh_ht_lo = at("sh_ht_lo", [P, FT, TOK], F32R, 130)
        y_rows = at("y_rows", [SLOTS, D], F32, 128)
        rw = at("rw", [P, KT, E], F32, 136)
        job_table = at("job_table", [P, MAX_JOBS, E], F32, 136)
        match = at("match", [P, TOPK, E], F32, 136)
        xt_hi = at("xt_hi", [P, KT, TOK], F32R, 160)
        xt_lo = at("xt_lo", [P, KT, TOK], F32R, 176)
        gather = [at(f"gather{r}", [P, D], F32, 8 * r) for r in range(N_GATHER)]
        ln2_gt = at("ln2_gt", [P, D], F32, 96)
        ln2_bt = at("ln2_bt", [P, D], F32, 104)
        choice = at("choice", [P, TT, E], F32, 192)
        scores = at("scores", [P, TT, E], F32, 192.5)
        chosen = at("chosen", [P, TT, E], F32, 193)
        slot_of = at("slot_of", [P, TT, E], F32, 193.5)
        weight = at("weight", [P, TT, E], F32, 194)
        row_of = at("row_of", [P, TT, E], F32, 194.5)
        iota_slot = at("iota_slot", [P, TOK], F32, 195)
        row_base = at("row_base", [P, E], F32, 196)
        bias_b = at("bias_b", [P, E], F32, 196.25)
        top_in_group = at("top_in_group", [P, TT, N_ROUTE_GROUPS, 8], F32, 196.5)
        groups = at("groups", [P, TT, 16], F32, 197)
        groups_left = at("groups_left", [P, TT, 16], F32, 197.125)
        best_groups = at("best_groups", [P, TT, 8], F32, 197.25)
        group_in = at("group_in", [P, TT, 8], F32, 197.3125)
        group_out = at("group_out", [P, TT, 8], F32, 197.375)
        best = at("best", [P, TT, 8], F32, 197.4375)
        masked = at("masked", [P, TT, E], F32, 197.5)
        left = at("left", [P, TT, E], F32, 194.5)
        job_n = at("job_n", [P, 2, MAX_JOBS], F32, 198)
        extra = at("extra", [P, E], F32, 196.25)
        job_ends = at("job_ends", [P, E], F32, 205.5)
        over_row = at("over_row", [P, E], F32, 205.75)
        gate_sig = at("gate_sig", [P, F], F32, 198.5)
        hidden = [at(f"hidden{r}", [P, F], F32, kb) for r, kb in enumerate((199.5, 202.5))]
        select = at("select", [P, TT, 4 * SLOTS], F32R, 200.5)
        ht_hi = [at(f"ht_hi{r}", [P, FT, SLOTS], F32R, kb) for r, kb in enumerate((203.5, 204.5))]
        ht_lo = [at(f"ht_lo{r}", [P, FT, SLOTS], F32R, kb) for r, kb in enumerate((204, 205))]
        job_expert = at("job_expert", [P, MAX_JOBS], I32, 198.25)
        job_first = at("job_first", [P, MAX_JOBS], I32, 198.375)
        count_of = at("count_of", [P, E], F32, 196.5)
        stats = at("stats", [P, TT, 4, 6], F32, 204.625)
        before = at("before", [P, P], F32, 205)
        my_row = at("my_row", [P, TT, TOPK], F32, 206)
        my_idx = at("my_idx", [P, TT, TOPK], U32, 206.0625)
        my_w = at("my_w", [P, TT, TOPK], F32, 206.125)

        ps_proj = [nc.alloc_psum_tensor(f"ps_proj{r}", [P, 512], F32) for r in range(2)]
        ps_s = [nc.alloc_psum_tensor(f"ps_s{r}", [P, 1024], F32) for r in range(2)]
        ps_t = nc.alloc_psum_tensor("ps_t", [P, 1024], F32)
        turn_ring = [ps_s[0][:, 0:512], ps_s[0][:, 512:1024]]
        down_out = [ps_s[1], ps_t]
        turned_p = [ps_s[0][:, 512:1024], ps_t[:, 0:768]]
        attended = [ps_t[:, 768:768 + P], ps_t[:, 768 + P:768 + 2 * P]]
        gathered = [ps_s[0][:, 0:512], ps_s[0][:, 512:1024], ps_proj[0][:, :]]

        y_dram = nc.dram_tensor("y_dram", ((E + MAX_JOBS) * SLOTS, D), F32, kind="Internal").ap()
        x2 = x[0]
        out2 = out[0]
        w_in_v = w_in[0].rearrange("(t p) c -> p t c", p=P)
        w_branch_v = w_branch[0].rearrange("n (t p) c -> p (n t) c", p=P)
        w_out_v = w_out[0].rearrange("(t p) c -> p t c", p=P)
        gate_v = w_gate[0].rearrange("e (p t) f -> e p (t f)", p=P)
        up_v = w_up[0].rearrange("e (p t) f -> e p (t f)", p=P)
        down_v = w_down[0].rearrange("e (t p) c -> e p t c", p=P)
        sh_gate_v = ws_gate.rearrange("e (p t) f -> e p (t f)", p=P)
        sh_up_v = ws_up.rearrange("e (p t) f -> e p (t f)", p=P)
        sh_down_v = ws_down.rearrange("e (t p) c -> e p t c", p=P)

        s_x, s_par, s_const, s_residue, s_turned, s_xhi, s_xlo = map(sem, (
            "s_x", "s_par", "s_const", "s_residue", "s_turned", "s_xhi", "s_xlo"))
        s_raw = [sem(f"s_raw{r}") for r in range(2)]
        s_hi, s_lo, s_mm = map(sem, ("s_hi", "s_lo", "s_mm"))
        s_ev = [sem(f"s_ev{r}") for r in range(2)]
        s_scored, s_masked, s_exp, s_norm, s_pturn, s_pt, s_av, s_att = map(sem, (
            "s_scored", "s_masked", "s_exp", "s_norm", "s_pturn", "s_pt", "s_av", "s_att"))
        s_asig, s_glu, s_conv, s_asum, s_acent, s_asq, s_avar, s_astd, s_anorm, s_aout = map(sem, (
            "s_asig", "s_glu", "s_conv", "s_asum", "s_acent", "s_asq", "s_avar", "s_astd", "s_anorm", "s_aout"))
        s_ctap, s_gated, s_added, s_brhi, s_brlo, s_mhi, s_mlo = map(sem, (
            "s_ctap", "s_gated", "s_added", "s_brhi", "s_brlo", "s_mhi", "s_mlo"))
        s_xr, s_lnp, s_var, s_std, s_scaled = map(sem, (
            "s_xr", "s_lnp", "s_var", "s_std", "s_scaled"))
        s_hhi, s_hlo, s_rw, s_logit, s_score, s_chosen, s_count, s_counted, s_tab, s_bias = map(sem, (
            "s_hhi", "s_hlo", "s_rw", "s_logit", "s_score", "s_chosen", "s_count", "s_counted", "s_tab", "s_bias"))
        s_shd, s_shacc, s_shthi, s_shtlo = map(sem, ("s_shd", "s_shacc", "s_shthi", "s_shtlo"))
        s_w = [sem(f"s_w{r}") for r in range(4)]
        s_select, s_gathered, s_xthi, s_xtlo, s_sig, s_hidden, s_hturned, s_hthi, s_htlo, s_y, s_yw = map(sem, (
            "s_select", "s_gathered", "s_xthi", "s_xtlo", "s_sig", "s_hidden", "s_hturned", "s_hthi", "s_htlo",
            "s_y", "s_yw"))
        s_mine, s_ln2p, s_done, s_used, s_turned_par, s_par_t, s_jobs = map(sem, (
            "s_mine", "s_ln2p", "s_done", "s_used", "s_turned_par", "s_par_t", "s_jobs"))
        s_jobsel, s_turning = map(sem, ("s_jobsel", "s_turning"))
        s_stats, s_out = map(sem, ("s_stats", "s_out"))
        s_shifted = [sem(f"s_shifted{tt}") for tt in range(TT)]
        s_got = [sem(f"s_got{r}") for r in range(N_GATHER)]
        s_pool, s_dve, s_zeros, s_cleared = map(sem, ("s_pool", "s_dve", "s_zeros", "s_cleared"))

        def seg(name, n, length, base):
            return {"name": name, "n": n, "len": length, "base": base, "unroll": name in ("aval", "cc")}

        segs, units = [], 0
        for name, n, length in (("qk0", 6, 4), ("v0", 3, 4), ("aval", CT // 4, 4), ("agate", CT // 4, 4),
                                ("qk1", 6, 4), ("v1", 3, 4), ("cc", CT // 4, 4), ("ch", CT // 4, 4),
                                ("cb", CT // 4, 4), ("gb", 6, 12), ("out", KT // 4, 4)):
            segs.append(seg(name, n, length, units))
            units += n * length
        at_seg = {s["name"]: s for s in segs}
        BASE_OUT = at_seg["out"]["base"]

        def chunk(name, i, c):
            if name in ("qk0", "v0", "qk1", "v1"):
                first = {"qk": 0, "v0": 6, "v1": 6}[name if name in ("v0", "v1") else "qk"]
                col = OFF_Q + first * C + i * C + int(name[-1]) * (C // 2) + c * 256
            elif name == "aval":
                col = i * 512 + c * 256
            elif name == "agate":
                col = C + i * 512 + c * 256
            elif name in ("cb", "cc", "ch"):
                col = OFF_C + ("cb", "cc", "ch").index(name) * C + i * 512 + c * 256
            elif name == "gb" and c < 4:
                col = OFF_G + i * (D // 2) + c * 256
            elif name == "gb":
                return w_branch_v[:, bass.ds((i // 2) * CT, CT), bass.ds((i % 2) * (D // 2) + (c - 4) * 512, 512)]
            else:
                return w_out_v[:, :, bass.ds(i * 512 + c * 256, 256)]
            return w_in_v[:, :, bass.ds(col, 256)]

        def wide(name, j):
            return name == "gb" and j >= 8

        def raw_half(u, w):
            if w:
                return raw[u.raw][:, :].rearrange("p (t c) -> p t c", t=CT)[:, :, u.half * 256:u.half * 256 + 256]
            return raw[u.raw][:, :].rearrange("p (t c) -> p t c", t=KT)[:, :, u.half * P:u.half * P + P]

        def tiles(ring, u, w):
            return ring[:, u.ring, :].rearrange("p (t c) -> p t c", t=CT if w else KT)

        def by_pair(name):
            return name in ("v0", "v1", "out")

        def pair_out(j):
            if j // 2 == 0:
                return ps_s[0][:, 512 * (j % 2):512 * (j % 2) + 2 * P]
            return ps_proj[j % 2][:, 0:2 * P]

        def stream(eng, per_unit, evacuate, after, before_last):
            prev = None
            for s in segs:
                def body(i, s=s, prev=prev):
                    for j in range(s["len"]):
                        u = Unit(s["base"], s["len"], i, j)
                        per_unit(s["name"], i, j, u)
                        if j >= 3:
                            evacuate(s["name"], i, j - 3, Unit(s["base"], s["len"], i, j - 3))
                        elif not (isinstance(i, int) and i == 0):
                            jj = s["len"] + j - 3
                            evacuate(s["name"], i - 1, jj, Unit(s["base"], s["len"], i - 1, jj))
                        elif prev is not None:
                            jj = prev["len"] + j - 3
                            evacuate(prev["name"], prev["n"] - 1, jj, Unit(prev["base"], prev["len"], prev["n"] - 1, jj))
                        after(s["name"], i, j)
                body(0)
                if s["unroll"]:
                    for i in range(1, s["n"]):
                        body(i)
                else:
                    with eng.Fori(1, s["n"]) as i:
                        body(i)
                prev = s
            for j in range(prev["len"] - 3, prev["len"]):
                if j == prev["len"] - 2:
                    before_last()
                evacuate(prev["name"], prev["n"] - 1, j, Unit(prev["base"], prev["len"], prev["n"] - 1, j))

        SHARED = units
        FIRST = SHARED + 6
        LAST_DOWN = FIRST + 4 + 6 * (E - 1)
        JOB = LAST_DOWN + 2
        assert units % 4 == 0

        def expert_unit(q, k, j):
            if isinstance(q, int) and q == 0 and k == 0:
                return ExpertUnit(units, 0, FIRST + j, j)
            return ExpertUnit(units, q, FIRST - 2 + 6 * k + j, j)

        def experts_stream(eng, per_unit, event):
            def steps(q):
                return [(k, j) for k in range(4) for j in range(6)
                        if not (isinstance(q, int) and q == 0 and k == 0 and j >= 4)]

            def body(q, before):
                todo = before + [(q, k, j) for k, j in steps(q)]
                for at_unit in range(len(before), len(todo)):
                    qq, k, j = todo[at_unit]
                    per_unit(qq, k, expert_unit(qq, k, j))
                    if at_unit >= 3:
                        qq, k, j = todo[at_unit - 3]
                        event(qq, k, expert_unit(qq, k, j))

            tail = steps(1)[-3:]
            body(0, [])
            with eng.Fori(1, QUADS - 1) as q:
                body(q, [(q - 1, k, j) for k, j in tail])
            body(QUADS - 1, [(QUADS - 2, k, j) for k, j in tail])
            for f in range(2):
                per_unit(QUADS, 0, ExpertUnit(units, 0, LAST_DOWN + f, 4 + f))
            event(QUADS - 1, 3, expert_unit(QUADS - 1, 3, 3))

        def evacuated(eng, name):
            for r in range(2):
                eng.wait_ge(s_ev[r], at_seg[name]["base"] // 2)

        def for_jobs(eng, four, job):
            eng.wait_ge(s_jobs, 1)
            n_jobs = eng.value_load(jobs[0:1, 0:1], min_val=0, max_val=MAX_JOBS)

            def body(i):
                four(i)
                job(i, 0)
                for k in range(1, 4):
                    with eng.If(n_jobs > 4 * i + k):
                        job(i, k)

            with eng.If(n_jobs > 0):
                body(0)
                with eng.If(n_jobs > 4):
                    with eng.Fori(1, MAX_JOBS // 4) as i:
                        with eng.If(n_jobs > 4 * i):
                            body(i)

        counted = {"dve": 0, "pool": 0}

        def dve_done(k):
            counted["dve"] += k
            return counted["dve"]

        def pool_done(k):
            counted["pool"] += k
            return counted["pool"]

        block = ctx.enter_context(nc.Block())

        @block.sync
        def _(sp):
            for s in segs:
                def body(i, s=s):
                    for c in range(s["len"] // 2):
                        u = Unit(s["base"], s["len"], i, 2 * c)
                        if not u.first:
                            sp.wait_ge(s_lo, u.n - 2)
                        if s["name"] == "gb" and c >= 4:
                            dst = raw[u.raw][:, :].rearrange("p (t c) -> p t c", t=CT)
                        else:
                            dst = raw[u.raw][:, :].rearrange("p (t c) -> p t c", t=KT)
                        sp.dma_start(dst, chunk(s["name"], i, c)).then_inc(s_raw[u.raw], 16)
                body(0)
                with sp.Fori(1, s["n"]) as i:
                    body(i)

            def load(u, e, v_gate, v_up, v_down):
                if u.j < 4:
                    v = (v_gate, v_up)[u.j // 2]
                    src = v[bass.ds(e, 1), :, bass.ds(u.j % 2 * 2048, 2048)].rearrange("e p m -> (e p) m")
                else:
                    src = v_down[bass.ds(e, 1), :, bass.ds(u.j - 4, 1), :].rearrange("e p t c -> (e p) (t c)")
                sp.dma_start(exp_raw[u.ring][:, :], src).then_inc(s_w[u.ring], 16)

            for j in range(6):
                sp.wait_ge(s_lo, units - 2 + j // 2 * 2 if j < 4 else units + j - 3)
                load(ExpertUnit(units, 0, SHARED + j, j), 0, sh_gate_v, sh_up_v, sh_down_v)

            def load_step(q, k, u):
                sp.wait_ge(s_lo, u.n - 3)
                load(u, 4 * q + k - (1 if u.j >= 4 else 0), gate_v, up_v, down_v)

            experts_stream(sp, load_step, lambda q, k, u: None)

            def load_job(i, k):
                e = sp.value_load(job_expert[0:1, bass.ds(4 * i + k, 1)], min_val=0, max_val=E - 1)
                for j in range(6):
                    u = ExpertUnit(units, i, JOB + 6 * k + j, j)
                    sp.wait_ge(s_lo, u.n - 3)
                    load(u, e, gate_v, up_v, down_v)

            for_jobs(sp, lambda i: None, load_job)
            for tt in range(TT):
                for half in range(2):
                    cols = slice(half * (D // 2), (half + 1) * (D // 2))
                    sp.wait_ge(s_out, 2 * tt + half + 1)
                    sp.dma_start(out2[tt * P:(tt + 1) * P, cols], acc[:, tt, cols]).then_inc(s_done, 16)
            sp.wait_ge(s_done, 16 * 4)

        @block.gpsimd
        def _(pool):
            pool.memset(ident[:, :], 0.0).then_inc(s_pool, 1)
            pool.memset(ones[:, :], 1.0).then_inc(s_const, 1)
            pool.wait_ge(s_pool, pool_done(1))
            pool.affine_select(out=ident[:, :], in_=ident[:, :], compare_op=ALU.not_equal, fill=1.0, base=0,
                               pattern=[[-1, P]], channel_multiplier=1).then_inc(s_const, 1)
            pool.iota(dist[:, :], pattern=[[-1, 2 * P]], base=P, channel_multiplier=1).then_inc(s_const, 1)
            pool.memset(a_pad[:, :, 0:TAPS_A - 1], 0.0).then_inc(s_const, 1)
            pool.wait_ge(s_residue, 3)
            for g in range(N_GROUPS_ATT):
                m = mask[:, g, :, :].rearrange("p a b -> p (a b)")
                pool.affine_select(out=m, in_=m, compare_op=ALU.is_ge, fill=MASKED, base=P,
                                   pattern=[[-1, 2 * P]], channel_multiplier=1).then_inc(s_pool, 1)
            pool.wait_ge(s_pool, pool_done(3))
            m = mask[:, 0, :, :].rearrange("p a b -> p (a b)")
            pool.affine_select(out=m, in_=m, compare_op=ALU.is_ge, fill=MASKED, base=0,
                               pattern=[[1, 2 * P]], channel_multiplier=-1).then_inc(s_const, 1)

            pool.memset(zeros[:, :], 0.0).then_inc(s_zeros, 1)
            pool.wait_ge(s_zeros, 1)
            for n in range(MAX_JOBS // 2):
                pool.wait_ge(s_mm, 2 * n + 1)
                row = E * SLOTS + n * P
                pool.dma_start(y_dram[row:row + P, :].rearrange("p (b c) -> p b c", c=512),
                               zeros[:, :].unsqueeze(1).to_broadcast([P, D // 512, 512])).then_inc(s_cleared, 16)

            for j in range(CT):
                pool.wait_ge(s_asig, j + 1)
                row = a_pad[:, j, TAPS_A - 1:]
                pool.tensor_tensor(row, row, a_sig[j % 2][:, :], ALU.mult).then_inc(s_glu, 1)

            pool.wait_ge(s_conv, CT * TAPS_A)
            pool.memset(c_pad[:, :, 0:TAPS_C - 1], 0.0).then_inc(s_const, 1)
            pool.wait_ge(s_att, 4 * HALF)
            pool.memset(merged[:, :, :], 0.0).then_inc(s_pool, 1)
            pool.wait_ge(s_pool, pool_done(1))

            def add_branch(i, k):
                w = 4 * i + k
                pool.wait_ge(s_gated, w + 1)
                if not (isinstance(w, int) and w == 0):
                    pool.wait_ge(s_added, w)
                m = merged[:, bass.ds((i % 2) * CT + 2 * k, 2), :]
                pool.tensor_tensor(m, m, gated[k % 2][:, :, :], ALU.add).then_inc(s_added, 1)

            for k in range(4):
                add_branch(0, k)
            with pool.Fori(1, 6) as i:
                for k in range(4):
                    add_branch(i, k)

            pool.wait_ge(s_mm, BASE_OUT)
            pool.dma_start(acc[:, :, :], x2.rearrange("(a p) c -> p a c", p=P)).then_inc(s_xr, 16)
            pool.wait_ge(s_mlo, 4)
            pool.dma_start(ln_g[:, :], ln1_g.to_broadcast([P, D])).then_inc(s_lnp, 16)
            pool.dma_start(ln_b[:, :], ln1_b.to_broadcast([P, D])).then_inc(s_lnp, 16)
            pool.dma_start(bias_b[:, :], router_bias.to_broadcast([P, E])).then_inc(s_bias, 16)
            pool.iota(iota_slot[:, :], pattern=[[1, TOK]], base=0, channel_multiplier=0,
                      allow_small_or_imprecise_dtypes=True).then_inc(s_tab, 1)
            pool.iota(row_base[:, :], pattern=[[SLOTS, E]], base=1, channel_multiplier=0,
                      allow_small_or_imprecise_dtypes=True).then_inc(s_tab, 1)
            pool.iota(tok_no, pattern=[[P, TT]], base=0, channel_multiplier=1,
                      allow_small_or_imprecise_dtypes=True).then_inc(s_tab, 1)
            pool.memset(before[:, :], 1.0).then_inc(s_pool, 1)
            pool.wait_ge(s_pool, pool_done(1))
            pool.affine_select(out=before[:, :], in_=before[:, :], compare_op=ALU.is_ge, fill=0.0, base=-1,
                               pattern=[[1, P]], channel_multiplier=-1).then_inc(s_tab, 1)

            pool.wait_ge(s_scaled, 1)
            pool.tensor_tensor(acc[:, 0, :], acc[:, 0, :], ln_b[:, :], ALU.add).then_inc(s_shifted[0], 1)

            def keep(e):
                pool.wait_ge(s_y, 2 * e + 2)
                pool.dma_start(y_dram[bass.ds(e * SLOTS, SLOTS), :], y_rows[:, :]).then_inc(s_yw, 16)

            with pool.Fori(0, E) as e:
                keep(e)

            def keep_job(i, k):
                keep(E + 4 * i + k)
                pool.wait_ge(s_yw, 16 * (E + 4 * i + k + 1))

            pool.wait_ge(s_cleared, 16 * (MAX_JOBS // 2))
            pool.wait_ge(s_yw, 16 * E)
            for_jobs(pool, lambda i: None, keep_job)
            pool.dma_start(ln2_gt[:, :], ln2_g.to_broadcast([P, D])).then_inc(s_ln2p, 16)
            pool.dma_start(ln2_bt[:, :], ln2_b.to_broadcast([P, D])).then_inc(s_ln2p, 16)
            pool.wait_ge(s_mine, 1)
            for tt in range(TT):
                for k in range(TOPK):
                    n = TOPK * tt + k
                    if n >= N_GATHER:
                        pool.wait_ge(s_used, n - N_GATHER + 1)
                    pool.indirect_dma_start(out=gather[n % N_GATHER][:, :], out_offset=None, in_=y_dram[:, :],
                                            in_offset=bass.IndirectOffsetOnAxis(ap=my_idx[:, tt, k:k + 1], axis=0),
                                            bounds_check=(E + MAX_JOBS) * SLOTS - 1,
                                            oob_is_err=False).then_inc(s_got[n % N_GATHER], 16)

        @block.scalar
        def _(act):
            act.dma_start(x_rows[:, :, :], x2.rearrange("(a p) c -> p a c", p=P)).then_inc(s_x, 16)
            row = 0
            for v, k in ((conv_a_w[0], TAPS_A), (conv_a_b, 1), (ln_a_g, 1), (ln_a_b, 1), (conv_c_w[0], TAPS_C)):
                act.dma_start(par_rows[row:row + k, :], v).then_inc(s_par, 16)
                row += k
            for n in range(8):
                act.wait_ge(s_turned, n + 1)
                tt, t = n // 4, n % 4 * 4
                nc.scalar.activation(x_hi[:, t:t + 4, tt * P:(tt + 1) * P],
                                     turn_ring[n % 2].rearrange("p (t c) -> p t c", t=4), ACT.Copy).then_inc(s_xhi, 1)

            def split(name, i, j, u):
                if u.half == 0:
                    act.wait_ge(s_raw[u.raw], 16 * u.raw_count)
                if not u.first:
                    act.wait_ge(s_mm, u.n - 3)
                w = wide(name, j)
                nc.scalar.activation(tiles(w_hi, u, w), raw_half(u, w), ACT.Copy).then_inc(s_hi, 1)

            def evacuate(name, i, j, u):
                if name in ("ch", "cb", "out") or wide(name, j):
                    return
                act.wait_ge(s_mm, u.n + 1)
                ps = ps_proj[u.bank][:, 0:TOK]
                if name in ("qk0", "qk1"):
                    both = q_k[:, bass.ds(i, 1), j, :]
                    ins = nc.scalar.activation(both.rearrange("p a c -> p (a c)"), ps, ACT.Copy)
                elif name in ("v0", "v1"):
                    m = j // 2 * 2
                    dst = v_rows[:, bass.ds(i, 1), m:m + 2, j % 2, :].rearrange("p a h c -> p (a h) c")
                    ins = nc.scalar.activation(dst, pair_out(j).rearrange("p (h c) -> p h c", h=2), ACT.Copy)
                elif name == "aval":
                    dst = a_pad[:, bass.ds(4 * i + j, 1), TAPS_A - 1:].rearrange("p a c -> p (a c)")
                    if j == 0 and isinstance(i, int):
                        act.wait_ge(s_const, 4)
                    ins = nc.scalar.activation(dst, ps, ACT.Copy)
                elif name == "agate":
                    n = 4 * i + j
                    if not (isinstance(n, int) and n < 2):
                        act.wait_ge(s_glu, n - 1)
                    ins = nc.scalar.activation(a_sig[j % 2][:, :], ps, ACT.Sigmoid)
                    ins.then_inc(s_asig, 1)
                    act.wait_ge(s_asig, n + 1)
                    act.sem_inc(s_ev[u.bank], 1)
                    return
                elif name == "cc":
                    if j == 0 and isinstance(i, int):
                        act.wait_ge(s_const, 6)
                    dst = c_pad[:, bass.ds(4 * i + j, 1), TAPS_C - 1:].rearrange("p a c -> p (a c)")
                    ins = nc.scalar.activation(dst, ps, ACT.Copy)
                else:
                    if j == 0 and not (isinstance(i, int) and i == 0):
                        act.wait_ge(s_gated, 4 * i)
                    elif j == 0:
                        act.wait_ge(s_aout, CT)
                    ins = nc.scalar.activation(gates[:, j, :], ps, ACT.Sigmoid)
                ins.then_inc(s_ev[u.bank], 1)

            def exps(half, head):
                for r in range(2):
                    n = 2 * (HALF * half + head) + r
                    w = N_GROUPS_ATT * P * (r + 1)
                    act.wait_ge(s_masked, n + 1)
                    nc.scalar.activation(att_p[r][:, 0:w], att_p[r][:, 0:w], ACT.Exp, bias=neg_max[r],
                                         accum_out=row_sum[r]).then_inc(s_exp, 1)

            def take_probs(half, head):
                for r in range(2):
                    n = 2 * (HALF * half + head) + r
                    act.wait_ge(s_pturn, n + 1)
                    if HALF * half + head:
                        act.wait_ge(s_av, HALF * half + head)
                    nc.scalar.activation(p_t[r][:, :, :],
                                         turned_p[r][:, 0:3 * (r + 1) * P].rearrange("p (a b) -> p a b", b=P),
                                         ACT.Copy).then_inc(s_pt, 1)

            def take_values(half, head):
                act.wait_ge(s_av, HALF * half + head + 1)
                for r in range(2):
                    nc.scalar.activation(branch[:, 1, HALF * half + head, r * P:(r + 1) * P], attended[r],
                                         ACT.Copy).then_inc(s_att, 1)

            def attend(half, w):
                if 7 <= w < 7 + HALF:
                    take_values(half, w - 7)
                if 6 <= w < 6 + HALF:
                    take_probs(half, w - 6)
                if 5 <= w < 5 + HALF:
                    exps(half, w - 5)

            def after(name, i, j):
                first = isinstance(i, int) and i == 0
                last = j == 3
                if name in ("aval", "cc"):
                    attend(int(name == "cc"), 4 * i + j)
                if name in ("agate", "ch") and first:
                    attend(int(name == "ch"), 8 + j)
                if first and last and name == "ch":
                    act.wait_ge(s_acent, 1)
                    nc.scalar.activation(a_sq[:, :, :], branch[:, 0, :, :], ACT.Square).then_inc(s_asq, 1)
                if first and last and name == "cb":
                    act.wait_ge(s_avar, 1)
                    nc.scalar.activation(a_rstd[:, :], a_mean[:, :], ACT.Sqrt).then_inc(s_astd, 1)
                    act.wait_ge(s_anorm, 1)
                    for c in range(CT):
                        nc.scalar.activation(branch[:, 0, c, :], branch[:, 0, c, :], ACT.Silu,
                                             scale=par[:, c, TAPS_A + 1:TAPS_A + 2],
                                             bias=par[:, c, TAPS_A + 2:TAPS_A + 3]).then_inc(s_aout, 1)
                if name == "gb" and j == 6:
                    if first:
                        act.wait_ge(s_aout, CT)
                        evacuated(act, "gb")
                    nc.scalar.activation(branch_hi[:, :, :],
                                         branch[:, bass.ds(i // 2, 1), :, :].rearrange("p n t c -> p (n t) c"),
                                         ACT.Copy).then_inc(s_brhi, 1)
                if name == "out" and first and j == 2:
                    act.wait_ge(s_added, 24)
                    for c in range(4):
                        nc.scalar.activation(merged_hi[:, 4 * c:4 * c + 4, :], merged[:, 4 * c:4 * c + 4, :],
                                             ACT.Copy).then_inc(s_mhi, 1)

            stream(act, split, evacuate, after, lambda: None)

            def expert_split(u):
                act.wait_ge(s_w[u.ring], 16 * u.loads)
                act.wait_ge(s_mm, u.n - 3)
                nc.scalar.activation(w_hi[:, u.ring, :], exp_raw[u.ring][:, :], ACT.Copy).then_inc(s_hi, 1)

            def take_gathered(g):
                for t in range(KT // 2):
                    act.wait_ge(s_gathered, KT * g + 2 * t + 1)
                    nc.scalar.activation(xt_hi[:, 2 * t:2 * t + 2, :].rearrange("p a c -> p (a c)"),
                                         gathered[2 * t % 3], ACT.Copy).then_inc(s_xthi, 1)

            def silu(m, r, rows, n):
                act.wait_ge(s_mm, n + 1)
                if not (isinstance(m, int) and m == 0):
                    act.wait_ge(s_hidden, m)
                nc.scalar.activation(gate_sig[0:rows, :], ps_proj[r][0:rows, 0:F], ACT.Silu).then_inc(s_sig, 1)

            for j in range(2):
                expert_split(ExpertUnit(units, 0, SHARED + j, j))
            act.wait_ge(s_var, 1)
            nc.scalar.activation(std, var_eps, ACT.Sqrt).then_inc(s_std, 1)
            for j in range(2, 4):
                expert_split(ExpertUnit(units, 0, SHARED + j, j))
            for tt in range(TT):
                act.wait_ge(s_shifted[tt], 1)
                nc.scalar.activation(h_hi[:, tt, :].rearrange("p (t q) -> p t q", t=KT),
                                     acc[:, tt, :].rearrange("p (q t) -> p t q", t=KT), ACT.Copy).then_inc(s_hhi, 1)
            act.dma_start(rw[:, :, :], router_w[0].rearrange("(p t) e -> p t e", p=P)).then_inc(s_rw, 16)
            take_gathered(0)
            act.wait_ge(s_logit, 1)
            nc.scalar.activation(scores[:, :, :], ps_s[1][:, 0:TT * E].rearrange("p (a e) -> p a e", a=TT),
                                 ACT.Sigmoid).then_inc(s_score, 1)
            for j in range(4, 6):
                expert_split(ExpertUnit(units, 0, SHARED + j, j))
            for tt in range(TT):
                silu(tt, tt, P, SHARED + 3)
            act.wait_ge(s_hturned, 1)
            nc.scalar.activation(sh_ht_hi[:, :, :], turn_ring[0].rearrange("p (f c) -> p f c", f=FT),
                                 ACT.Copy).then_inc(s_shthi, 1)

            def take_hidden(e, r):
                act.wait_ge(s_hturned, e + 2)
                nc.scalar.activation(ht_hi[r][:, :, :], turn_ring[0][:, 0:FT * SLOTS].rearrange("p (f c) -> p f c", f=FT),
                                     ACT.Copy).then_inc(s_hthi, 1)

            def take_rows(e, n):
                act.wait_ge(s_mm, n + 1)
                if not (isinstance(e, int) and e == 0):
                    act.wait_ge(s_yw, 16 * e)
                for half in range(2):
                    nc.scalar.activation(y_rows[:, half * 1024:(half + 1) * 1024], down_out[half][0:SLOTS, :],
                                         ACT.Copy).then_inc(s_y, 1)

            def event(q, k, u):
                e = 4 * q + k
                if u.j == 0 and isinstance(e, int) and e == 0:
                    take_gathered(1)
                if u.j == 0 and not (isinstance(e, int) and e < 2):
                    take_rows(e - 2, u.n - 1)
                if u.j == 1 and not (isinstance(e, int) and e < 1):
                    take_hidden(e - 1, (k - 1) % 2)
                if u.j == 3:
                    silu(e + 2, k % 2, SLOTS, u.n)
                if u.j == 3 and k == 3 and not (isinstance(q, int) and q == QUADS - 1):
                    take_gathered(q + 2)

            experts_stream(act, lambda q, k, u: expert_split(u), event)
            take_hidden(E - 1, 1)
            take_rows(E - 2, LAST_DOWN - 1)
            take_rows(E - 1, LAST_DOWN + 1)

            def one_job(i, k):
                e = E + 4 * i + k
                job_units = [ExpertUnit(units, i, JOB + 6 * k + j, j) for j in range(6)]
                for u in job_units:
                    expert_split(u)
                silu(e + 2, k % 2, SLOTS, job_units[3].n)
                take_hidden(e, k % 2)
                take_rows(e, job_units[5].n)

            for_jobs(act, lambda i: take_gathered(QUADS + 1 + i), one_job)
            for tt in range(TT):
                act.wait_ge(s_var, tt + 2)
                nc.scalar.activation(std[:, tt:tt + 1], var_eps[:, tt:tt + 1], ACT.Sqrt).then_inc(s_std, 1)

        @block.vector
        def _(dve):
            dve.wait_ge(s_const, 4)
            nc.vector.memset(mask[:, 0, :, :], 0.0).then_inc(s_residue, 1)
            for g in (1, 2):
                nc.vector.tensor_scalar(dist_mod[:, g - 1, :], dist[:, :], DILATIONS[g] - 1, None,
                                        ALU.bitwise_and).then_inc(s_dve, 1)
            dve.wait_ge(s_dve, dve_done(2))
            for g in (1, 2):
                nc.vector.tensor_scalar(mask[:, g, :, :].rearrange("p a b -> p (a b)"), dist_mod[:, g - 1, :], 1.0,
                                        MASKED, ALU.min, ALU.mult).then_inc(s_residue, 1)
            for r in range(2):
                dve.wait_ge(s_turned_par, r + 1)
                nc.vector.tensor_copy(par[:, 4 * r:4 * r + 4, :],
                                      ps_s[1][:, r * 512:r * 512 + 4 * N_PAR].rearrange("p (a b) -> p a b", b=N_PAR)
                                      ).then_inc(s_par_t, 1)
            for n in range(8):
                dve.wait_ge(s_xhi, n + 1)
                tt, t = n // 4, n % 4 * 4
                nc.vector.tensor_tensor(x_lo[:, t:t + 4, tt * P:(tt + 1) * P],
                                        turn_ring[n % 2].rearrange("p (t c) -> p t c", t=4),
                                        x_hi[:, t:t + 4, tt * P:(tt + 1) * P].bitcast(F32),
                                        ALU.subtract).then_inc(s_xlo, 1)

            def split(name, i, j, u):
                dve.wait_ge(s_hi, u.n + 1)
                w = wide(name, j)
                nc.vector.tensor_tensor(tiles(w_lo, u, w), raw_half(u, w), tiles(w_hi, u, w).bitcast(F32),
                                        ALU.subtract).then_inc(s_lo, 1)

            def evacuate(name, i, j, u):
                if not (name in ("ch", "cb", "out") or wide(name, j)):
                    return
                dve.wait_ge(s_mm, u.n + 1)
                if name == "ch":
                    n = 4 * i + j
                    if j == 0 and isinstance(i, int):
                        evacuated(dve, "ch")
                        dve.wait_ge(s_const, 6)
                        dve.wait_ge(s_pturn, 4 * HALF)
                        dve.wait_ge(s_cleared, 16 * (MAX_JOBS // 2))
                    dst = c_pad[:, bass.ds(n, 1), TAPS_C - 1:].rearrange("p a c -> p (a c)")
                    nc.vector.tensor_tensor(dst, ps_proj[u.bank][:, 0:TOK], dst, ALU.mult).then_inc(s_ev[u.bank], 1)
                    dve.wait_ge(s_ev[u.bank], u.bank_count + 1)
                    y = branch[:, 2, bass.ds(n, 1), :].rearrange("p a c -> p (a c)")
                    for k in range(TAPS_C):
                        v = c_pad[:, bass.ds(n, 1), k:k + TOK].rearrange("p a c -> p (a c)")
                        w = par[:, bass.ds(n, 1), TAPS_A + 3 + k:TAPS_A + 4 + k].rearrange("p a c -> p (a c)")
                        if k == 0:
                            ins = nc.vector.tensor_scalar(y, v, w, None, ALU.mult)
                        else:
                            ins = nc.vector.scalar_tensor_tensor(out=y, in0=v, scalar=w, in1=y, op0=ALU.mult, op1=ALU.add)
                        ins.then_inc(s_ctap, 1)
                        dve.wait_ge(s_ctap, n * TAPS_C + k + 1)
                elif name == "cb":
                    y = branch[:, 2, bass.ds(4 * i + j, 1), :].rearrange("p a c -> p (a c)")
                    nc.vector.tensor_tensor(y, ps_proj[u.bank][:, 0:TOK], y, ALU.mult).then_inc(s_ev[u.bank], 1)
                elif name == "out":
                    if j == 0 and isinstance(i, int):
                        dve.wait_ge(s_xr, 16)
                    cols = acc[:, j % 2, bass.ds(512 * i + 2 * P * (j // 2), 2 * P)]
                    nc.vector.scalar_tensor_tensor(out=cols, in0=cols, scalar=ALPHA, in1=pair_out(j),
                                                   op0=ALU.mult, op1=ALU.add).then_inc(s_ev[u.bank], 1)
                    if j == 3:
                        for r in range(2):
                            dve.wait_ge(s_ev[r], u.bank_count + 1)
                        for tt in range(TT):
                            nc.vector.bn_stats(stats[:, tt, bass.ds(i, 1), :].rearrange("p a b -> p (a b)"),
                                               acc[:, tt, bass.ds(512 * i, 512)]).then_inc(s_stats, 1)
                else:
                    k = j - 8
                    w = 4 * i + k
                    if not (isinstance(w, int) and w < 2):
                        dve.wait_ge(s_added, w - 1)
                    if k == 0:
                        dve.wait_ge(s_ev[0], u.bank_count)
                        dve.wait_ge(s_ev[1], u.bank_count)
                    nc.vector.tensor_tensor(gated[k % 2][:, :, :].rearrange("p a c -> p (a c)"), ps_proj[u.bank][:, :],
                                            gates[:, 2 * k:2 * k + 2, :].rearrange("p a c -> p (a c)"),
                                            ALU.mult).then_inc(s_gated, 1)
                    dve.wait_ge(s_gated, w + 1)
                    dve.sem_inc(s_ev[u.bank], 1)

            def softmax(half, head):
                for r in range(2):
                    n, kt = 2 * (HALF * half + head) + r, r + 1
                    if n == 0:
                        dve.wait_ge(s_const, 5)
                    dve.wait_ge(s_scored, n + 1)
                    if n >= 2:
                        dve.wait_ge(s_pturn, n - 1)
                    p = att_p[r][:, 0:3 * kt * P].rearrange("p (g k) -> p g k", g=N_GROUPS_ATT)
                    m = mask[:, :, 2 - kt:2, :].rearrange("p g a b -> p g (a b)")
                    nc.vector.tensor_tensor_reduce(p, ps_s[r][:, 0:3 * kt * P].rearrange("p (g k) -> p g k", g=N_GROUPS_ATT),
                                                   m, SCALE, NEG, ALU.add, ALU.max, row_max[r]).then_inc(s_dve, 1)
                    dve.wait_ge(s_dve, dve_done(1))
                    nc.vector.tensor_scalar(neg_max[r], row_max[r], -1.0, None, ALU.mult).then_inc(s_masked, 1)
                for r in range(2):
                    n, kt = 2 * (HALF * half + head) + r, r + 1
                    dve.wait_ge(s_exp, n + 1)
                    nc.vector.reciprocal(row_rcp[r], row_sum[r]).then_inc(s_dve, 1)
                    dve.wait_ge(s_dve, dve_done(1))
                    nc.vector.tensor_scalar(att_p[r][:, 0:3 * kt * P], att_p[r][:, 0:3 * kt * P], row_rcp[r], None,
                                            ALU.mult).then_inc(s_norm, 1)

            def conv_tap(tap, const):
                if const and tap == 0:
                    dve.wait_ge(s_glu, CT)
                    dve.wait_ge(s_par_t, 2)
                else:
                    dve.wait_ge(s_conv, CT * tap)
                for c in range(CT):
                    v = a_pad[:, c, bass.ds(tap, TOK)]
                    w = par[:, c, bass.ds(tap, 1)]
                    y = branch[:, 0, c, :]
                    if const and tap == 0:
                        ins = nc.vector.tensor_scalar(y, v, w, par[:, c, TAPS_A:TAPS_A + 1], ALU.mult, ALU.add)
                    else:
                        ins = nc.vector.scalar_tensor_tensor(out=y, in0=v, scalar=w, in1=y, op0=ALU.mult, op1=ALU.add)
                    ins.then_inc(s_conv, 1)

            def after(name, i, j):
                first = isinstance(i, int) and i == 0
                if name in ("aval", "cc") and 5 <= 4 * i + j:
                    softmax(int(name == "cc"), 4 * i + j - 5)
                if name in ("agate", "ch") and first and j == 0:
                    softmax(int(name == "ch"), HALF - 1)
                if name == "qk1" and (j == 3 or not first):
                    conv_tap(4 * i + j - 3, first)
                if name == "v1" and first:
                    conv_tap(21 + j, False)
                if name == "v1" and not first and j < 3:
                    conv_tap(25 + 3 * (i - 1) + j, False)
                if first and j == 3 and name == "ch":
                    dve.wait_ge(s_asum, 1)
                    nc.vector.tensor_scalar(a_mean[:, :], ps_s[0][:, 0:TOK], 1.0 / C, None, ALU.mult).then_inc(s_dve, 1)
                    dve.wait_ge(s_dve, dve_done(1))
                    nc.vector.tensor_tensor(branch[:, 0, :, :], branch[:, 0, :, :],
                                            a_mean[:, :].unsqueeze(1).to_broadcast([P, CT, TOK]),
                                            ALU.subtract).then_inc(s_acent, 1)
                if first and j == 3 and name == "cb":
                    dve.wait_ge(s_asum, 2)
                    nc.vector.tensor_scalar(a_mean[:, :], ps_s[0][:, 512:512 + TOK], 1.0 / C, LN_EPS, ALU.mult,
                                            ALU.add).then_inc(s_avar, 1)
                    dve.wait_ge(s_astd, 1)
                    nc.vector.reciprocal(a_mean[:, :], a_rstd[:, :]).then_inc(s_dve, 1)
                    dve.wait_ge(s_dve, dve_done(1))
                    nc.vector.tensor_tensor(branch[:, 0, :, :], branch[:, 0, :, :],
                                            a_mean[:, :].unsqueeze(1).to_broadcast([P, CT, TOK]),
                                            ALU.mult).then_inc(s_anorm, 1)
                if name == "gb" and j == 6:
                    dve.wait_ge(s_brhi, i + 1)
                    nc.vector.tensor_tensor(branch_lo[:, :, :],
                                            branch[:, bass.ds(i // 2, 1), :, :].rearrange("p n t c -> p (n t) c"),
                                            branch_hi[:, :, :].bitcast(F32), ALU.subtract).then_inc(s_brlo, 1)
                if name == "out" and first and j == 2:
                    for c in range(4):
                        dve.wait_ge(s_mhi, c + 1)
                        nc.vector.tensor_tensor(merged_lo[:, 4 * c:4 * c + 4, :], merged[:, 4 * c:4 * c + 4, :],
                                                merged_hi[:, 4 * c:4 * c + 4, :].bitcast(F32),
                                                ALU.subtract).then_inc(s_mlo, 1)

            def expert_split(u):
                dve.wait_ge(s_hi, u.n + 1)
                nc.vector.tensor_tensor(w_lo[:, u.ring, :], exp_raw[u.ring][:, :], w_hi[:, u.ring, :].bitcast(F32),
                                        ALU.subtract).then_inc(s_lo, 1)

            def first_splits():
                for j in range(2):
                    expert_split(ExpertUnit(units, 0, SHARED + j, j))

            stream(dve, split, evacuate, after, first_splits)

            dve.wait_ge(s_stats, 8)
            for tt in range(TT):
                nc.vector.bn_aggr(mean_var[:, tt, :], stats[:, tt, :, :]).then_inc(s_dve, 1)
            dve.wait_ge(s_dve, dve_done(2))
            nc.vector.tensor_scalar(var_eps, mean_var[:, :, 1], LN_EPS, None, ALU.add).then_inc(s_var, 1)
            dve.wait_ge(s_std, 1)
            nc.vector.reciprocal(rstd, std).then_inc(s_dve, 1)
            dve.wait_ge(s_dve, dve_done(1))
            for tt in range(TT):
                nc.vector.tensor_scalar(acc[:, tt, :], acc[:, tt, :], mean_var[:, tt, 0:1], rstd[:, tt:tt + 1],
                                        ALU.subtract, ALU.mult).then_inc(s_dve, 1)
                dve.wait_ge(s_dve, dve_done(1))
                if tt == 0:
                    dve.wait_ge(s_lnp, 32)
                nc.vector.tensor_tensor(acc[:, tt, :], acc[:, tt, :], ln_g[:, :], ALU.mult).then_inc(s_scaled, 1)
            dve.wait_ge(s_scaled, 2)
            nc.vector.tensor_tensor(acc[:, 1, :], acc[:, 1, :], ln_b[:, :], ALU.add).then_inc(s_shifted[1], 1)

            def take_gathered(g):
                for t in range(KT // 2):
                    dve.wait_ge(s_gathered, KT * g + 2 * t + 2)
                    nc.vector.tensor_copy(xt_lo[:, 2 * t:2 * t + 2, :].rearrange("p a c -> p (a c)"),
                                          gathered[(2 * t + 1) % 3]).then_inc(s_xtlo, 1)

            def product(m, r, rows):
                dve.wait_ge(s_sig, m + 1)
                if not (isinstance(m, int) and m < 2):
                    dve.wait_ge(s_hturned, m - 2 if not isinstance(m, int) or m > 2 else 1)
                nc.vector.tensor_tensor(hidden[r][0:rows, :], ps_proj[r][0:rows, F:2 * F], gate_sig[0:rows, :],
                                        ALU.mult).then_inc(s_hidden, 1)

            expert_split(ExpertUnit(units, 0, SHARED + 2, 2))
            dve.wait_ge(s_tab, 4)
            for tt in range(TT):
                nc.vector.tensor_scalar(select[:, tt, :], iota_slot[:, :], tok_no[:, tt:tt + 1], None,
                                        ALU.is_equal).then_inc(s_select, 1)
            for tt in range(TT):
                dve.wait_ge(s_hhi, tt + 1)
                nc.vector.tensor_tensor(h_lo[:, tt, :].rearrange("p (t q) -> p t q", t=KT),
                                        acc[:, tt, :].rearrange("p (q t) -> p t q", t=KT),
                                        h_hi[:, tt, :].rearrange("p (t q) -> p t q", t=KT).bitcast(F32),
                                        ALU.subtract).then_inc(s_hlo, 1)
            expert_split(ExpertUnit(units, 0, SHARED + 3, 3))
            take_gathered(0)

            def step(ins, k=1):
                ins.then_inc(s_dve, 1)
                dve.wait_ge(s_dve, dve_done(1))

            def batch(instructions):
                k = 0
                for ins in instructions:
                    ins.then_inc(s_dve, 1)
                    k += 1
                dve.wait_ge(s_dve, dve_done(k))

            nc.vector.memset(groups[:, :, 8:16], FILL).then_inc(s_dve, 1)
            dve.wait_ge(s_dve, dve_done(1))
            dve.wait_ge(s_score, 1)
            dve.wait_ge(s_bias, 16)
            step(nc.vector.tensor_tensor(choice[:, :, :], scores[:, :, :],
                                         bias_b[:, :].unsqueeze(1).to_broadcast([P, TT, E]), ALU.add))
            G8 = E // N_ROUTE_GROUPS
            batch(nc.vector.max(top_in_group[:, tt, g, :], choice[:, tt, g * G8:(g + 1) * G8])
                  for tt in range(TT) for g in range(N_ROUTE_GROUPS))
            step(nc.vector.tensor_tensor(groups[:, :, 0:8], top_in_group[:, :, :, 0], top_in_group[:, :, :, 1], ALU.add))
            batch(nc.vector.max(best_groups[:, tt, :], groups[:, tt, :]) for tt in range(TT))
            step(nc.vector.memset(best_groups[:, :, TOPK_GROUPS:8], FILL))
            batch(nc.vector.match_replace(groups_left[:, tt, :], best_groups[:, tt, :], groups[:, tt, :], CHOSEN)
                  for tt in range(TT))
            step(nc.vector.tensor_scalar(group_in[:, :, :], groups_left[:, :, 0:8], CHOSEN, None, ALU.is_equal))
            step(nc.vector.tensor_scalar(group_out[:, :, :], group_in[:, :, :], -NEG, NEG, ALU.mult, ALU.add))
            by_group = lambda a: a[:, :, :].rearrange("p a (g e) -> p (a g) e", e=G8)
            spread = lambda a: a[:, :, :].rearrange("p a g -> p (a g)").unsqueeze(2).to_broadcast(
                [P, TT * N_ROUTE_GROUPS, G8])
            step(nc.vector.tensor_tensor(by_group(masked), by_group(choice), spread(group_in), ALU.mult))
            step(nc.vector.tensor_tensor(by_group(masked), by_group(masked), spread(group_out), ALU.add))
            batch(nc.vector.max(best[:, tt, :], masked[:, tt, :]) for tt in range(TT))
            batch(nc.vector.match_replace(left[:, tt, :], best[:, tt, :], masked[:, tt, :], CHOSEN) for tt in range(TT))
            nc.vector.tensor_scalar(chosen[:, :, :], left[:, :, :], CHOSEN, None, ALU.is_equal).then_inc(s_chosen, 1)
            dve.wait_ge(s_chosen, 1)
            step(nc.vector.tensor_scalar(slot_of[:, :, :], chosen[:, :, :], -NO_SLOT, NO_SLOT, ALU.mult, ALU.add))
            dve.wait_ge(s_count, 1)
            step(nc.vector.tensor_tensor(slot_of[:, :, :], slot_of[:, :, :],
                                         ps_s[1][:, 512:512 + TT * E].rearrange("p (a e) -> p a e", a=TT), ALU.add))
            nc.vector.tensor_copy(count_of[:, :], ps_s[1][:, 512 + TT * E:512 + (TT + 1) * E]).then_inc(s_counted, 1)

            def select_quad(q):
                for tt in range(TT):
                    nc.vector.tensor_tensor(select[:, tt, :].rearrange("p (a s) -> p a s", a=4),
                                            slot_of[:, tt, bass.ds(4 * q, 4)].unsqueeze(2).to_broadcast([P, 4, SLOTS]),
                                            iota_slot[:, 0:SLOTS].unsqueeze(1).to_broadcast([P, 4, SLOTS]),
                                            ALU.is_equal).then_inc(s_select, 1)

            dve.wait_ge(s_dve, dve_done(0))
            dve.wait_ge(s_gathered, KT)
            select_quad(0)
            for tt in range(TT):
                product(tt, tt, P)
            for j in range(4, 6):
                expert_split(ExpertUnit(units, 0, SHARED + j, j))
            dve.wait_ge(s_shthi, 1)
            nc.vector.tensor_tensor(sh_ht_lo[:, :, :], turn_ring[0].rearrange("p (f c) -> p f c", f=FT),
                                    sh_ht_hi[:, :, :].bitcast(F32), ALU.subtract).then_inc(s_shtlo, 1)
            dve.wait_ge(s_hhi, 2)
            for tt in range(TT):
                dve.wait_ge(s_shd, tt + 1)
                for half in range(2):
                    cols = acc[:, tt, half * 1024:(half + 1) * 1024]
                    nc.vector.scalar_tensor_tensor(out=cols, in0=cols, scalar=ALPHA, in1=down_out[half][:, :],
                                                   op0=ALU.mult, op1=ALU.add).then_inc(s_shacc, 1)

            def weights_of_tokens():
                step(nc.vector.tensor_tensor(weight[:, :, :], scores[:, :, :], chosen[:, :, :], ALU.mult))
                step(nc.vector.tensor_reduce(w_sum, weight[:, :, :], AX_X, ALU.add))
                step(nc.vector.reciprocal(w_rcp, w_sum))
                batch(nc.vector.tensor_scalar(weight[:, tt, :], weight[:, tt, :], w_rcp[:, tt:tt + 1], ROUTED_SCALE,
                                              ALU.mult, ALU.mult) for tt in range(TT))

            def count_jobs():
                dve.wait_ge(s_counted, 1)
                step(nc.vector.tensor_scalar(extra[:, :], count_of[:, :], float(SLOTS), None, ALU.is_gt))
                for b in range(2, BLOCKS):
                    step(nc.vector.tensor_scalar(over_row[:, :], count_of[:, :], float(b * SLOTS), None, ALU.is_gt))
                    step(nc.vector.tensor_tensor(extra[:, :], extra[:, :], over_row[:, :], ALU.add))
                step(nc.vector.tensor_tensor_scan(job_ends[:, :], ones[:, 0:E], extra[:, :], 0.0, ALU.mult, ALU.add))

            def job_tables():
                numbers = iota_slot[:, 0:MAX_JOBS]
                step(nc.vector.tensor_tensor(job_table[:, :, :], job_ends[:, :].unsqueeze(1).to_broadcast([P, MAX_JOBS, E]),
                                             numbers.unsqueeze(2).to_broadcast([P, MAX_JOBS, E]), ALU.is_le))
                step(nc.vector.tensor_reduce(job_n[:, 0, :], job_table[:, :, :], AX_X, ALU.add))
                step(nc.vector.tensor_tensor(job_table[:, :, :], job_table[:, :, :],
                                             extra[:, :].unsqueeze(1).to_broadcast([P, MAX_JOBS, E]), ALU.mult))
                step(nc.vector.tensor_reduce(job_n[:, 1, :], job_table[:, :, :], AX_X, ALU.add))
                step(nc.vector.tensor_scalar(job_expert[:, :], job_n[:, 0, :], float(E - 1), None, ALU.min))
                step(nc.vector.tensor_tensor(job_n[:, 1, :], numbers, job_n[:, 1, :], ALU.subtract))
                step(nc.vector.tensor_scalar(job_n[:, 1, :], job_n[:, 1, :], 1.0, float(SLOTS), ALU.add, ALU.mult))
                step(nc.vector.tensor_scalar(job_first[:, :], job_n[:, 1, :], float((BLOCKS - 1) * SLOTS), None, ALU.min))
                nc.vector.tensor_copy(jobs[:, :], job_ends[:, E - 1:E]).then_inc(s_jobs, 1)

            def rows_of_tokens():
                step(nc.vector.tensor_tensor(over_row[:, :], job_ends[:, :], extra[:, :], ALU.subtract))
                step(nc.vector.tensor_scalar(over_row[:, :], over_row[:, :], float(SLOTS), float(E * SLOTS - SLOTS + 1),
                                             ALU.mult, ALU.add))
                step(nc.vector.tensor_tensor(over_row[:, :], over_row[:, :], row_base[:, :], ALU.subtract))
                step(nc.vector.tensor_scalar(masked[:, :, :], slot_of[:, :, :], float(SLOTS), None, ALU.is_ge))
                step(nc.vector.tensor_tensor(masked[:, :, :], masked[:, :, :],
                                             over_row[:, :].unsqueeze(1).to_broadcast([P, TT, E]), ALU.mult))
                step(nc.vector.tensor_tensor(row_of[:, :, :], slot_of[:, :, :],
                                             row_base[:, :].unsqueeze(1).to_broadcast([P, TT, E]), ALU.add))
                step(nc.vector.tensor_tensor(row_of[:, :, :], row_of[:, :, :], masked[:, :, :], ALU.add))
                step(nc.vector.tensor_tensor(row_of[:, :, :], row_of[:, :, :], chosen[:, :, :], ALU.mult))
                batch(nc.vector.max(my_row[:, tt, :], row_of[:, tt, :]) for tt in range(TT))
                nc.vector.tensor_scalar(my_idx[:, :, :], my_row[:, :, :], -1.0, None, ALU.add).then_inc(s_mine, 1)

            def weights_by_row(tt):
                batch(nc.vector.scalar_tensor_tensor(out=match[:, k, :], in0=row_of[:, tt, :],
                                                     scalar=my_row[:, tt, k:k + 1], in1=weight[:, tt, :],
                                                     op0=ALU.is_equal, op1=ALU.mult) for k in range(TOPK))
                step(nc.vector.tensor_reduce(my_w[:, tt, :], match[:, :, :], AX_X, ALU.add))

            def take_hidden(e, r):
                dve.wait_ge(s_hthi, e + 1)
                nc.vector.tensor_tensor(ht_lo[r][:, :, :], turn_ring[0][:, 0:FT * SLOTS].rearrange("p (f c) -> p f c", f=FT),
                                        ht_hi[r][:, :, :].bitcast(F32), ALU.subtract).then_inc(s_htlo, 1)

            def event(q, k, u):
                e = 4 * q + k
                first = isinstance(q, int) and q == 0
                if u.j == 0 and isinstance(e, int) and e == 0:
                    take_gathered(1)
                if u.j == 1 and not (isinstance(e, int) and e < 1):
                    take_hidden(e - 1, (k - 1) % 2)
                if u.j == 2 and k == 1 and not (isinstance(q, int) and q == QUADS - 1):
                    select_quad(q + 1)
                if u.j == 3:
                    product(e + 2, k % 2, SLOTS)
                if u.j == 3 and k == 3 and not (isinstance(q, int) and q == QUADS - 1):
                    take_gathered(q + 2)
                if first and (k, u.j) == (1, 4):
                    weights_of_tokens()
                if first and (k, u.j) == (1, 5):
                    count_jobs()
                if first and (k, u.j) == (2, 1):
                    job_tables()
                if first and (k, u.j) == (2, 4):
                    rows_of_tokens()
                if first and k == 3 and u.j in (1, 2):
                    weights_by_row(u.j - 1)

            experts_stream(dve, lambda q, k, u: expert_split(u), event)
            take_hidden(E - 1, 1)

            def select_jobs(i):
                for k in range(4):
                    e = dve.value_load(job_expert[0:1, bass.ds(4 * i + k, 1)], min_val=0, max_val=E - 1)
                    first = dve.value_load(job_first[0:1, bass.ds(4 * i + k, 1)], min_val=0,
                                           max_val=(BLOCKS - 1) * SLOTS)
                    for tt in range(TT):
                        nc.vector.tensor_scalar(select[:, tt, k * SLOTS:(k + 1) * SLOTS],
                                                iota_slot[:, bass.ds(first, SLOTS)],
                                                slot_of[:, tt, bass.ds(e, 1)], None, ALU.is_equal).then_inc(s_jobsel, 1)
                take_gathered(QUADS + 1 + i)

            def one_job(i, k):
                e = E + 4 * i + k
                for j in range(6):
                    expert_split(ExpertUnit(units, i, JOB + 6 * k + j, j))
                product(e + 2, k % 2, SLOTS)
                take_hidden(e, k % 2)

            for_jobs(dve, select_jobs, one_job)
            for tt in range(TT):
                for k in range(TOPK):
                    n = TOPK * tt + k
                    dve.wait_ge(s_got[n % N_GATHER], 16 * (n // N_GATHER + 1))
                    if n:
                        dve.wait_ge(s_used, n)
                    nc.vector.scalar_tensor_tensor(out=acc[:, tt, :], in0=gather[n % N_GATHER][:, :],
                                                   scalar=my_w[:, tt, k:k + 1], in1=acc[:, tt, :],
                                                   op0=ALU.mult, op1=ALU.add).then_inc(s_used, 1)
                dve.wait_ge(s_used, TOPK * (tt + 1))
                for c in range(4):
                    nc.vector.bn_stats(stats[:, tt, c, :], acc[:, tt, c * 512:(c + 1) * 512]).then_inc(s_dve, 1)
                dve.wait_ge(s_dve, dve_done(4))
                nc.vector.bn_aggr(mean_var[:, tt, :], stats[:, tt, :, :]).then_inc(s_dve, 1)
                dve.wait_ge(s_dve, dve_done(1))
                nc.vector.tensor_scalar(var_eps[:, tt:tt + 1], mean_var[:, tt, 1:2], LN_EPS, None,
                                        ALU.add).then_inc(s_var, 1)
                dve.wait_ge(s_std, tt + 2)
                step(nc.vector.reciprocal(rstd[:, tt:tt + 1], std[:, tt:tt + 1]))
                step(nc.vector.tensor_scalar(acc[:, tt, :], acc[:, tt, :], mean_var[:, tt, 0:1], rstd[:, tt:tt + 1],
                                             ALU.subtract, ALU.mult))
                if tt == 0:
                    dve.wait_ge(s_ln2p, 32)
                for half in range(2):
                    cols = slice(half * (D // 2), (half + 1) * (D // 2))
                    step(nc.vector.tensor_tensor(acc[:, tt, cols], acc[:, tt, cols], ln2_gt[:, cols], ALU.mult))
                    nc.vector.tensor_tensor(acc[:, tt, cols], acc[:, tt, cols], ln2_bt[:, cols],
                                            ALU.add).then_inc(s_out, 1)

        @block.tensor
        def _(pe):
            pe.wait_ge(s_const, 2)
            pe.wait_ge(s_par, 16 * 5)
            for r in range(2):
                for c in range(4):
                    ins = pe.transpose(ps_s[1][:, r * 512 + c * N_PAR:r * 512 + (c + 1) * N_PAR],
                                       par_rows[:, (4 * r + c) * P:(4 * r + c + 1) * P], ident[0:N_PAR, 0:N_PAR])
                ins.then_inc(s_turned_par, 1)

            def turn_tokens(rows, first, seen, seen_base):
                for n in range(8):
                    if n >= 2:
                        pe.wait_ge(seen, seen_base + n - 1)
                    tt, t = n // 4, n % 4 * 4
                    for k in range(4):
                        ins = pe.transpose(turn_ring[n % 2][:, k * P:(k + 1) * P],
                                           rows[:, tt, (t + k) * P:(t + k + 1) * P], ident[:, :])
                    ins.then_inc(s_turned, 1)

            pe.wait_ge(s_x, 16)
            turn_tokens(x_rows, 0, s_xlo, 0)
            pe.wait_ge(s_xlo, 8)

            def multiply(name, i, j, u):
                if by_pair(name) and j % 2 == 0:
                    return
                pe.wait_ge(s_lo, u.n + 1)
                if by_pair(name):
                    for r in range(2):
                        pe.wait_ge(s_ev[r], u.bank_count - 1)
                elif not u.first_bank:
                    pe.wait_ge(s_ev[u.bank], u.bank_count)
                w = wide(name, j)
                hi, lo = tiles(w_hi, u, w), tiles(w_lo, u, w)
                ps = ps_proj[u.bank]
                if w:
                    if j == 8:
                        pe.wait_ge(s_brlo, i + 1)
                    for half in range(2):
                        n = 0
                        for t in range(CT):
                            for a, b in ((hi, branch_hi), (hi, branch_lo), (lo, branch_hi)):
                                ins = pe.matmul(ps[:, half * TOK:(half + 1) * TOK], a[:, t, half * P:(half + 1) * P],
                                                b[:, t, :], start=(n == 0), stop=(n == 3 * CT - 1))
                                n += 1
                elif by_pair(name):
                    hi, lo = (a[:, u.ring - 1:u.ring + 1, :].rearrange("p r (t c) -> p r t c", t=KT) for a in (w_hi, w_lo))
                    m_hi, m_lo = (merged_hi, merged_lo) if name == "out" else (x_hi, x_lo)
                    if name == "out" and j == 1 and isinstance(i, int):
                        pe.wait_ge(s_mlo, 4)
                    for tt in range(TT):
                        n = 0
                        for t in range(KT):
                            for a, b in ((m_hi, hi), (m_hi, lo), (m_lo, hi)):
                                ins = pe.matmul(pair_out(j - 1 + tt), a[:, t, tt * P:(tt + 1) * P], b[:, :, t, :],
                                                start=(n == 0), stop=(n == 3 * KT - 1))
                                n += 1
                    ins.then_inc(s_mm, 2)
                    return
                else:
                    n = 0
                    for t in range(KT):
                        for a, b in ((hi, x_hi), (hi, x_lo), (lo, x_hi)):
                            ins = pe.matmul(ps[:, 0:TOK], a[:, t, :], b[:, t, :], start=(n == 0), stop=(n == 3 * KT - 1))
                            n += 1
                ins.then_inc(s_mm, 1)

            def scores_of(half, head):
                for kt in (1, 2):
                    n = 2 * (HALF * half + head) + kt - 1
                    if n >= 2:
                        pe.wait_ge(s_masked, n - 1)
                    for g in range(N_GROUPS_ATT):
                        ins = pe.matmul(ps_s[kt - 1][:, g * kt * P:(g + 1) * kt * P],
                                        q_t[:, g, head, (kt - 1) * P:kt * P], k_t[:, g, head, 0:kt * P],
                                        start=True, stop=True)
                    ins.then_inc(s_scored, 1)

            def turn_probs(half, head):
                for kt in (1, 2):
                    n = 2 * (HALF * half + head) + kt - 1
                    pe.wait_ge(s_norm, n + 1)
                    if n >= 2:
                        pe.wait_ge(s_pt, n - 1)
                        pe.wait_ge(s_att, 2 * (HALF * half + head))
                    for m in range(3 * kt):
                        ins = pe.transpose(turned_p[kt - 1][:, m * P:(m + 1) * P], att_p[kt - 1][:, m * P:(m + 1) * P],
                                           ident[:, :])
                    ins.then_inc(s_pturn, 1)

            def values(half, head):
                pe.wait_ge(s_pt, 2 * (HALF * half + head) + 2)
                for kt in (1, 2):
                    for m in range(3 * kt):
                        ins = pe.matmul(attended[kt - 1], v_rows[:, m // kt, head, m % kt, :], p_t[kt - 1][:, m, :],
                                        start=(m == 0), stop=(m == 3 * kt - 1))
                ins.then_inc(s_av, 1)

            def channel_sum(src, col):
                for c in range(CT):
                    ins = pe.matmul(ps_s[0][:, col:col + TOK], ones[:, :], src[:, c, :], start=(c == 0), stop=(c == CT - 1))
                ins.then_inc(s_asum, 1)

            def before_unit(name, w):
                if name in ("aval", "cc"):
                    half = int(name == "cc")
                    if 3 <= w < 3 + HALF:
                        if w == 3:
                            evacuated(pe, name)
                        scores_of(half, w - 3)
                    if 4 <= w < 4 + HALF:
                        turn_probs(half, w - 4)
                if name == "ch" and w == 0:
                    pe.wait_ge(s_conv, CT * TAPS_A)
                    channel_sum(branch[:, 0, :, :], 0)
                if name == "cb" and w == 0:
                    pe.wait_ge(s_asq, 1)
                    channel_sum(a_sq, 512)

            def after_unit(name, w):
                if name in ("aval", "cc") and 4 <= w < 4 + HALF:
                    values(int(name == "cc"), w - 4)

            for s in segs:
                name = s["name"]
                for i in range(s["n"] if s["unroll"] else 1):
                    for j in range(s["len"]):
                        before_unit(name, 4 * i + j)
                        multiply(name, i, j, Unit(s["base"], s["len"], i, j))
                        after_unit(name, 4 * i + j)
                if not s["unroll"]:
                    with pe.Fori(1, s["n"]) as i:
                        for j in range(s["len"]):
                            multiply(name, i, j, Unit(s["base"], s["len"], i, j))

            def gather_tokens(g, ready, count):
                pe.wait_ge(ready, count)
                for t in range(KT // 2):
                    for r, h in enumerate((h_hi, h_lo)):
                        m = 2 * t + r
                        if m >= 3:
                            pe.wait_ge(s_xtlo if (m - 3) % 2 else s_xthi, KT // 2 * g + (m - 3) // 2 + 1)
                        for a in range(2):
                            for tt in range(TT):
                                c = (2 * t + a) * P
                                ins = pe.matmul(gathered[m % 3][:, a * TOK:(a + 1) * TOK], h[:, tt, c:c + P],
                                                select[:, tt, :], start=(tt == 0), stop=(tt == TT - 1))
                        ins.then_inc(s_gathered, 1)

            THREE = lambda a_hi, a_lo, b_hi, b_lo: ((a_hi, b_hi), (a_hi, b_lo), (a_lo, b_hi))

            def gate_up(u, g, columns, banks):
                pe.wait_ge(s_lo, u.n + 1)
                if u.j == 0:
                    for s in (s_xthi, s_xtlo):
                        pe.wait_ge(s, KT // 2 * (g + 1))
                for cols, bank in zip(columns, banks):
                    rows = cols.stop - cols.start
                    n = 0
                    for t in range(KT // 2):
                        w = slice(t * F, (t + 1) * F)
                        for x, b in THREE(xt_hi, xt_lo, w_hi, w_lo):
                            ins = pe.matmul(ps_proj[bank][0:rows, u.j // 2 * F:(u.j // 2 + 1) * F],
                                            x[:, u.j % 2 * (KT // 2) + t, cols], b[:, u.ring, w],
                                            start=(u.j % 2 == 0 and n == 0), stop=(u.j % 2 == 1 and n == 3 * KT // 2 - 1))
                            n += 1
                ins.then_inc(s_mm, 1)

            pe.wait_ge(s_hlo, 2)
            gather_tokens(0, s_select, TT)
            pe.wait_ge(s_xthi, KT // 2)
            pe.wait_ge(s_xtlo, KT // 2)
            pe.wait_ge(s_rw, 16)
            for tt in range(TT):
                for t in range(KT):
                    for x in (xt_hi, xt_lo):
                        ins = pe.matmul(ps_s[1][:, tt * E:(tt + 1) * E], x[:, t, tt * P:(tt + 1) * P].bitcast(F32),
                                        rw[:, t, :], start=(t == 0 and x is xt_hi), stop=(t == KT - 1 and x is xt_lo))
            ins.then_inc(s_logit, 1)
            for j in range(4):
                gate_up(ExpertUnit(units, 0, SHARED + j, j), 0, [slice(0, P), slice(P, 2 * P)], [0, 1])
            pe.wait_ge(s_chosen, 1)
            pe.wait_ge(s_tab, 4)
            count = lambda k: ps_s[1][:, 512 + k * E:512 + (k + 1) * E]
            pe.matmul(count(0), before[:, :], chosen[:, 0, :], start=True, stop=True)
            pe.matmul(count(1), ones[:, :], chosen[:, 0, :], start=True, stop=False)
            pe.matmul(count(1), before[:, :], chosen[:, 1, :], start=False, stop=True)
            pe.matmul(count(2), ones[:, :], chosen[:, 0, :], start=True, stop=False)
            pe.matmul(count(2), ones[:, :], chosen[:, 1, :], start=False, stop=True).then_inc(s_count, 1)
            pe.wait_ge(s_hidden, 2)
            for f in range(FT):
                for tt in range(TT):
                    ins = pe.transpose(turn_ring[0][:, f * TOK + tt * P:f * TOK + (tt + 1) * P],
                                       hidden[tt][:, f * P:(f + 1) * P], ident[:, :])
            ins.then_inc(s_hturned, 1)
            pe.wait_ge(s_shtlo, 1)
            pe.wait_ge(s_lo, SHARED + 6)
            pe.wait_ge(s_counted, 1)

            def down_bank(c):
                return down_out[c // 2][:, c % 2 * 512:(c % 2 + 1) * 512]

            for tt in range(TT):
                if tt:
                    pe.wait_ge(s_shacc, 2)
                for c in range(4):
                    for f in range(FT):
                        ring = (SHARED + 4 + f) % 4
                        for k, (h, w) in enumerate(THREE(sh_ht_hi, sh_ht_lo, w_hi, w_lo)):
                            ins = pe.matmul(down_bank(c), h[:, f, tt * P:(tt + 1) * P], w[:, ring, c * 512:(c + 1) * 512],
                                            start=(f == 0 and k == 0), stop=(f == FT - 1 and k == 2))
                ins.then_inc(s_shd, 1)
            pe.wait_ge(s_shd, 2)
            pe.sem_inc(s_mm, 2)

            def turn_hidden(e, r):
                pe.wait_ge(s_hidden, e + 3)
                if not (isinstance(e, int) and e == 0):
                    pe.wait_ge(s_htlo, e)
                pe.sem_inc(s_turning, 1)
                for f in range(FT):
                    ins = pe.transpose(turn_ring[0][:, f * SLOTS:(f + 1) * SLOTS], hidden[r][0:SLOTS, f * P:(f + 1) * P],
                                       ident[0:SLOTS, 0:SLOTS])
                ins.then_inc(s_hturned, 1)

            def down(u, e, r):
                pe.wait_ge(s_lo, u.n + 1)
                if u.j == 4:
                    pe.wait_ge(s_htlo, e + 1)
                    if isinstance(e, int) and e == 0:
                        pe.wait_ge(s_shacc, 4)
                    else:
                        pe.wait_ge(s_y, 2 * e)
                f = u.j - 4
                for c in range(4):
                    for k, (h, w) in enumerate(THREE(ht_hi[r], ht_lo[r], w_hi, w_lo)):
                        ins = pe.matmul(down_bank(c)[0:SLOTS, :], h[:, f, :], w[:, u.ring, c * 512:(c + 1) * 512],
                                        start=(f == 0 and k == 0), stop=(f == FT - 1 and k == 2))
                ins.then_inc(s_mm, 1)

            def step(q, k, u):
                e = 4 * q + k
                if u.j == 0 and isinstance(e, int) and e == 0:
                    gather_tokens(1, s_select, TT * 2)
                if u.j == 4 and k == 3 and not (isinstance(q, int) and q == QUADS - 1):
                    pe.wait_ge(s_htlo, e)
                    gather_tokens(q + 2, s_select, TT * (q + 3))
                if u.j == 0:
                    pe.wait_ge(s_hidden, e + 1)
                if u.j == 2 and not (isinstance(e, int) and e < 1):
                    turn_hidden(e - 1, (k - 1) % 2)
                if u.j < 4:
                    gate_up(u, q + 1, [slice(k * SLOTS, (k + 1) * SLOTS)], [k % 2])
                elif isinstance(u.n, int) and u.n >= LAST_DOWN:
                    if u.j == 4:
                        turn_hidden(E - 1, 1)
                    down(u, E - 1, 1)
                else:
                    down(u, e - 1, (k - 1) % 2)

            experts_stream(pe, step, lambda q, k, u: None)

            def gather_jobs(i):
                pe.wait_ge(s_htlo, E + 4 * i)
                pe.wait_ge(s_hidden, E + 4 * i + 2)
                gather_tokens(QUADS + 1 + i, s_jobsel, 4 * TT * (i + 1))

            def one_job(i, k):
                e = E + 4 * i + k
                for j in range(6):
                    u = ExpertUnit(units, i, JOB + 6 * k + j, j)
                    if j == 0:
                        pe.wait_ge(s_hidden, e + 1)
                    if j == 4:
                        turn_hidden(e, k % 2)
                    if j < 4:
                        gate_up(u, QUADS + 1 + i, [slice(k * SLOTS, (k + 1) * SLOTS)], [k % 2])
                    else:
                        down(u, e, k % 2)

            for_jobs(pe, gather_jobs, one_job)


_INS = ['x', 'w_in', 'conv_a_w', 'conv_a_b', 'ln_a_g', 'ln_a_b', 'conv_c_w', 'w_branch', 'w_out', 'ln1_g', 'ln1_b',
        'router_w', 'router_bias', 'w_gate', 'w_up', 'w_down', 'ws_gate', 'ws_up', 'ws_down', 'ln2_g', 'ln2_b']
_OUTS = [((1, 256, 2048), 'float32')]


def kernel(**inputs):
    import numpy as _np
    import concourse.bacc as _bacc
    from concourse import mybir as _mybir
    from concourse.bass_utils import run_bass_kernel_spmd as _run

    nc = _bacc.Bacc("TRN2", target_bir_lowering=False, num_devices=1)
    arrays, args = {}, []
    for name in _INS:
        a = _np.ascontiguousarray(inputs[name])
        arrays[f"in_{name}_dram"] = a
        args.append(nc.dram_tensor(f"in_{name}_dram", a.shape, _mybir.dt.from_np(a.dtype), kind="ExternalInput").ap())
    for i, (shape, dtype) in enumerate(_OUTS):
        dt = _mybir.dt.from_np(_np.dtype(dtype))
        args.append(nc.dram_tensor(f"out_{i}_dram", shape, dt, kind="ExternalOutput").ap())
    build(nc, *args)
    r = _run(nc, [arrays], core_ids=[0])
    got = tuple(r.results[0][f"out_{i}_dram"] for i in range(len(_OUTS)))
    return got[0]
```
